# Optimizing a Trainium2 kernel written in Bass

```python
import math
import jax, jax.numpy as jnp
from jax import lax
import numpy as np

D_MODEL = 2048
BATCH = 1
SEQ = 512
DEPTH = 1
DEC_BATCH = 8
DEC_SEQ = 1
PAST_LEN = 2048
PAGE_SIZE = 128

ATTN_V_DIM = 128
ATTN_HEADS = (D_MODEL // 2) // ATTN_V_DIM
ATTN_QK_DIM = ATTN_V_DIM // 2
ATTN_WIDTH = ATTN_HEADS * ATTN_V_DIM
QK_WIDTH = ATTN_HEADS * 2 * ATTN_QK_DIM
SSM_WIDTH = D_MODEL - ATTN_WIDTH
SSM_CH = 16
SSM_GROUPS = SSM_WIDTH // SSM_CH
SSM_STATE = 64
MIX_WIDTH = ATTN_WIDTH + SSM_WIDTH
IN_WIDTH = 2 * QK_WIDTH + ATTN_WIDTH + SSM_WIDTH
DT_MIN = 1e-3
DT_MAX = 1e-1
PEER_HEADS = 8
PEER_TOPK = 16
PEER_NKEYS = 128
PEER_EXPERTS = PEER_NKEYS * PEER_NKEYS
PEER_QDIM = 256
PEER_HALF = PEER_QDIM // 2
PEER_BLOCK = 128
Q_BLOCK = 128
ROPE_THETA = 10000.0
EPS = 1e-6
NEG_INF = -1e30

kernel_name = 'hybrid_diffattn_s5_peer_decode_step'

def rmsnorm(x, g):
    xf = x.astype(jnp.float32)
    y = xf * lax.rsqrt(jnp.mean(xf * xf, axis=-1, keepdims=True) + EPS) * g.astype(jnp.float32)
    return y.astype(x.dtype)

def rope(x, pos):
    half = ATTN_QK_DIM // 2
    inv = 1.0 / (ROPE_THETA ** (jnp.arange(half, dtype=jnp.float32) * 2.0 / ATTN_QK_DIM))
    ang = pos.astype(jnp.float32)[:, None] * inv[None, :]
    c = jnp.cos(ang)[:, None, None, :]
    s = jnp.sin(ang)[:, None, None, :]
    xf = x.astype(jnp.float32)
    x1, x2 = xf[..., :half], xf[..., half:]
    return jnp.concatenate([x1 * c - x2 * s, x2 * c + x1 * s], axis=-1).astype(x.dtype)

def diff_attend(q, k, v, q_pos, k_pos, lam, g_sub, lam_init):
    b, tq = q.shape[0], q.shape[1]
    qb = min(Q_BLOCK, tq)
    nq = -(-tq // qb)
    pad = nq * qb - tq
    qp = jnp.pad(q, ((0, 0), (0, pad), (0, 0), (0, 0), (0, 0)))
    pp = jnp.pad(q_pos, (0, pad), mode='edge')
    q_blocks = qp.reshape(b, nq, qb, ATTN_HEADS, 2, ATTN_QK_DIM).swapaxes(0, 1)
    p_blocks = pp.reshape(nq, qb)
    kf = k.astype(jnp.float32)
    vf = v.astype(jnp.float32)
    scale = ATTN_QK_DIM ** -0.5

    def one_block(args):
        qi, pi = args
        s = jnp.einsum('bqhcd,bkhcd->bchqk', qi.astype(jnp.float32), kf) * scale
        mask = pi[:, None] >= k_pos[None, :]
        s = jnp.where(mask, s, NEG_INF)
        p = jax.nn.softmax(s, axis=-1)
        w = p[:, 0] - lam * p[:, 1]
        return jnp.einsum('bhqk,bkhd->bqhd', w, vf)

    o = lax.map(one_block, (q_blocks, p_blocks))
    o = o.swapaxes(0, 1).reshape(b, nq * qb, ATTN_HEADS, ATTN_V_DIM)[:, :tq]
    o = o * lax.rsqrt(jnp.mean(o * o, axis=-1, keepdims=True) + EPS)
    o = o * g_sub.astype(jnp.float32) * (1.0 - lam_init)
    return o.reshape(b, tq, ATTN_WIDTH)

def s5_scan(u, h0_re, h0_im, a_re, a_im, log_dt, b_re, b_im, c_re, c_im, d):
    uf = u.astype(jnp.float32)
    are = a_re.astype(jnp.float32)
    aim = a_im.astype(jnp.float32)
    dt = jnp.exp(log_dt.astype(jnp.float32))[:, None]
    mag = jnp.exp(are * dt)
    lr = mag * jnp.cos(aim * dt)
    li = mag * jnp.sin(aim * dt)
    den = are * are + aim * aim
    zr = lr - 1.0
    fr = (zr * are + li * aim) / den
    fi = (li * are - zr * aim) / den
    br = b_re.astype(jnp.float32)
    bi = b_im.astype(jnp.float32)
    bbar_re = fr[..., None] * br - fi[..., None] * bi
    bbar_im = fr[..., None] * bi + fi[..., None] * br
    bu_re = jnp.einsum('btgc,gpc->btgp', uf, bbar_re)
    bu_im = jnp.einsum('btgc,gpc->btgp', uf, bbar_im)
    al_re = jnp.broadcast_to(lr, bu_re.shape)
    al_im = jnp.broadcast_to(li, bu_im.shape)

    def combine(e1, e2):
        a1r, a1i, b1r, b1i = e1
        a2r, a2i, b2r, b2i = e2
        return (a1r * a2r - a1i * a2i,
                a1r * a2i + a1i * a2r,
                a2r * b1r - a2i * b1i + b2r,
                a2r * b1i + a2i * b1r + b2i)

    cum_r, cum_i, hr, hi = lax.associative_scan(combine, (al_re, al_im, bu_re, bu_im), axis=1)
    h0r = h0_re.astype(jnp.float32)[:, None]
    h0i = h0_im.astype(jnp.float32)[:, None]
    hr = hr + cum_r * h0r - cum_i * h0i
    hi = hi + cum_r * h0i + cum_i * h0r
    y = (jnp.einsum('btgp,gcp->btgc', hr, c_re.astype(jnp.float32))
         - jnp.einsum('btgp,gcp->btgc', hi, c_im.astype(jnp.float32))
         + d.astype(jnp.float32) * uf)
    b, t = u.shape[0], u.shape[1]
    return y.reshape(b, t, SSM_WIDTH), hr[:, -1], hi[:, -1]

def peer(h, w_q, sub_keys, u_tab, v_tab):
    n, dm = h.shape
    nb = -(-n // PEER_BLOCK)
    pad = nb * PEER_BLOCK - n
    hb_all = jnp.pad(h, ((0, pad), (0, 0))).reshape(nb, PEER_BLOCK, dm)
    keys = sub_keys.astype(jnp.float32)

    def block(hb):
        q = (hb @ w_q).astype(jnp.float32).reshape(PEER_BLOCK, PEER_HEADS, 2, PEER_HALF)
        s = jnp.einsum('thcd,hckd->thck', q, keys)
        s1, i1 = lax.top_k(s[:, :, 0], PEER_TOPK)
        s2, i2 = lax.top_k(s[:, :, 1], PEER_TOPK)
        ncand = PEER_TOPK * PEER_TOPK
        cand_s = (s1[..., :, None] + s2[..., None, :]).reshape(PEER_BLOCK, PEER_HEADS, ncand)
        cand_i = (i1[..., :, None] * PEER_NKEYS + i2[..., None, :]).reshape(PEER_BLOCK, PEER_HEADS, ncand)
        top_s, top_p = lax.top_k(cand_s, PEER_TOPK)
        idx = jnp.take_along_axis(cand_i, top_p, axis=-1)
        gate = jax.nn.softmax(top_s, axis=-1)
        u = u_tab[idx]
        act = jax.nn.gelu(jnp.einsum('thkd,td->thk', u, hb).astype(jnp.float32))
        v = v_tab[idx].astype(jnp.float32)
        return jnp.einsum('thk,thkd->td', gate * act, v).astype(h.dtype)

    return lax.map(block, hb_all).reshape(nb * PEER_BLOCK, dm)[:n]

def decoder_layer(x, pos, past_k, past_v, k_pos, h0_re, h0_im, lp, lam_init):
    b, t, _ = x.shape
    h = rmsnorm(x, lp['g_mix'])
    z = h @ lp['w_in']
    q, k, v, u = jnp.split(z, [QK_WIDTH, 2 * QK_WIDTH, 2 * QK_WIDTH + ATTN_WIDTH], axis=-1)
    q = rope(q.reshape(b, t, ATTN_HEADS, 2, ATTN_QK_DIM), pos)
    k = rope(k.reshape(b, t, ATTN_HEADS, 2, ATTN_QK_DIM), pos)
    v = v.reshape(b, t, ATTN_HEADS, ATTN_V_DIM)
    if past_k is None:
        k_all, v_all = k, v
    else:
        k_all = jnp.concatenate([past_k.astype(k.dtype), k], axis=1)
        v_all = jnp.concatenate([past_v.astype(v.dtype), v], axis=1)
    lam = (jnp.exp(jnp.sum(lp['lq1'].astype(jnp.float32) * lp['lk1'].astype(jnp.float32)))
           - jnp.exp(jnp.sum(lp['lq2'].astype(jnp.float32) * lp['lk2'].astype(jnp.float32)))
           + lam_init)
    attn = diff_attend(q, k_all, v_all, pos, k_pos, lam, lp['g_sub'], lam_init)
    y, hr, hi = s5_scan(u.reshape(b, t, SSM_GROUPS, SSM_CH), h0_re, h0_im,
                        lp['a_re'], lp['a_im'], lp['log_dt'], lp['b_re'], lp['b_im'],
                        lp['c_re'], lp['c_im'], lp['d'])
    y = jax.nn.gelu(y)
    y = y * jax.nn.sigmoid(y @ lp['w_glu'].astype(jnp.float32) + lp['b_glu'].astype(jnp.float32))
    mix = jnp.concatenate([attn.astype(x.dtype), y.astype(x.dtype)], axis=-1)
    x = x + mix @ lp['w_out']
    h2 = rmsnorm(x, lp['g_ffn'])
    x = x + peer(h2.reshape(b * t, D_MODEL), lp['pq'], lp['pk'], lp['pu'], lp['pv']).reshape(b, t, D_MODEL)
    k_rows = k.reshape(b, t, ATTN_HEADS, 2 * ATTN_QK_DIM)
    return x, k_rows, v, hr, hi

def setup_inputs(seed: int = 0) -> dict:
    key = jax.random.key(seed)
    ks = jax.random.split(key, 32)
    f32 = jnp.float32
    n_pages = PAST_LEN // PAGE_SIZE
    n_used = DEC_BATCH * n_pages
    n_pool = n_used + (n_used + 3) // 4
    nrm = lambda k, shape, s: jax.random.normal(k, shape, f32) * s
    page_table = jax.random.permutation(ks[0], n_pool)[:n_used].reshape(DEC_BATCH, n_pages).astype(jnp.int32)
    a_im_base = math.pi * jnp.arange(SSM_STATE, dtype=f32)
    return {
        'x_prompt': nrm(ks[1], (BATCH, SEQ, D_MODEL), 1.0),
        'x_sample': nrm(ks[2], (DEC_BATCH, DEC_SEQ, D_MODEL), 1.0),
        'cache_k': nrm(ks[3], (DEPTH, n_pool, PAGE_SIZE, ATTN_HEADS, 2 * ATTN_QK_DIM), 1.0),
        'cache_v': nrm(ks[4], (DEPTH, n_pool, PAGE_SIZE, ATTN_HEADS, ATTN_V_DIM), 1.0),
        'state_ssm_re': nrm(ks[5], (DEPTH, DEC_BATCH, SSM_GROUPS, SSM_STATE), 0.5),
        'state_ssm_im': nrm(ks[6], (DEPTH, DEC_BATCH, SSM_GROUPS, SSM_STATE), 0.5),
        'page_table': page_table,
        'g_mix': 1.0 + nrm(ks[7], (DEPTH, D_MODEL), 0.02),
        'w_in': nrm(ks[8], (DEPTH, D_MODEL, IN_WIDTH), D_MODEL ** -0.5),
        'lambda_q1': nrm(ks[9], (DEPTH, ATTN_QK_DIM), 0.1),
        'lambda_k1': nrm(ks[10], (DEPTH, ATTN_QK_DIM), 0.1),
        'lambda_q2': nrm(ks[11], (DEPTH, ATTN_QK_DIM), 0.1),
        'lambda_k2': nrm(ks[12], (DEPTH, ATTN_QK_DIM), 0.1),
        'g_sub': 1.0 + nrm(ks[13], (DEPTH, ATTN_V_DIM), 0.02),
        'ssm_a_re': -0.5 + nrm(ks[14], (DEPTH, SSM_GROUPS, SSM_STATE), 0.01),
        'ssm_a_im': a_im_base + nrm(ks[15], (DEPTH, SSM_GROUPS, SSM_STATE), 0.01),
        'ssm_log_dt': jax.random.uniform(ks[16], (DEPTH, SSM_GROUPS), f32, math.log(DT_MIN), math.log(DT_MAX)),
        'ssm_b_re': nrm(ks[17], (DEPTH, SSM_GROUPS, SSM_STATE, SSM_CH), (2 * SSM_CH) ** -0.5),
        'ssm_b_im': nrm(ks[18], (DEPTH, SSM_GROUPS, SSM_STATE, SSM_CH), (2 * SSM_CH) ** -0.5),
        'ssm_c_re': nrm(ks[19], (DEPTH, SSM_GROUPS, SSM_CH, SSM_STATE), (2 * SSM_STATE) ** -0.5),
        'ssm_c_im': nrm(ks[20], (DEPTH, SSM_GROUPS, SSM_CH, SSM_STATE), (2 * SSM_STATE) ** -0.5),
        'ssm_d': nrm(ks[21], (DEPTH, SSM_GROUPS, SSM_CH), 1.0),
        'w_glu': nrm(ks[22], (DEPTH, SSM_WIDTH, SSM_WIDTH), SSM_WIDTH ** -0.5),
        'b_glu': nrm(ks[23], (DEPTH, SSM_WIDTH), 0.01),
        'w_out': nrm(ks[24], (DEPTH, MIX_WIDTH, D_MODEL), MIX_WIDTH ** -0.5),
        'g_ffn': 1.0 + nrm(ks[25], (DEPTH, D_MODEL), 0.02),
        'peer_w_q': nrm(ks[26], (DEPTH, D_MODEL, PEER_HEADS * PEER_QDIM), D_MODEL ** -0.5),
        'peer_sub_keys': nrm(ks[27], (DEPTH, PEER_HEADS, 2, PEER_NKEYS, PEER_HALF), PEER_HALF ** -0.5),
        'peer_u': nrm(ks[28], (DEPTH, PEER_EXPERTS, D_MODEL), D_MODEL ** -0.5),
        'peer_v': nrm(ks[29], (DEPTH, PEER_EXPERTS, D_MODEL), PEER_HEADS ** -0.5),
        'g_final': 1.0 + nrm(ks[30], (D_MODEL,), 0.02),
    }

def reference(x_prompt, x_sample, cache_k, cache_v, state_ssm_re, state_ssm_im, page_table,
              g_mix, w_in, lambda_q1, lambda_k1, lambda_q2, lambda_k2, g_sub,
              ssm_a_re, ssm_a_im, ssm_log_dt, ssm_b_re, ssm_b_im, ssm_c_re, ssm_c_im, ssm_d,
              w_glu, b_glu, w_out, g_ffn, peer_w_q, peer_sub_keys, peer_u, peer_v, g_final):
    bp, tp = x_prompt.shape[0], x_prompt.shape[1]
    bs, ts = x_sample.shape[0], x_sample.shape[1]
    n_pages = page_table.shape[1]
    past_len = n_pages * PAGE_SIZE
    pos_p = jnp.arange(tp)
    pos_s = past_len + jnp.arange(ts)
    kpos_s = jnp.concatenate([jnp.arange(past_len), pos_s])
    h0_zero = jnp.zeros((bp, SSM_GROUPS, SSM_STATE), jnp.float32)
    xp, xs = x_prompt, x_sample
    kp_l, vp_l, rp_l, ip_l, ks_l, vs_l, rs_l, is_l = [], [], [], [], [], [], [], []
    for l in range(DEPTH):
        lam_init = 0.8 - 0.6 * math.exp(-0.3 * l)
        lp = {'g_mix': g_mix[l], 'w_in': w_in[l], 'lq1': lambda_q1[l], 'lk1': lambda_k1[l],
              'lq2': lambda_q2[l], 'lk2': lambda_k2[l], 'g_sub': g_sub[l],
              'a_re': ssm_a_re[l], 'a_im': ssm_a_im[l], 'log_dt': ssm_log_dt[l],
              'b_re': ssm_b_re[l], 'b_im': ssm_b_im[l], 'c_re': ssm_c_re[l], 'c_im': ssm_c_im[l],
              'd': ssm_d[l], 'w_glu': w_glu[l], 'b_glu': b_glu[l], 'w_out': w_out[l],
              'g_ffn': g_ffn[l], 'pq': peer_w_q[l], 'pk': peer_sub_keys[l],
              'pu': peer_u[l], 'pv': peer_v[l]}
        xp, kp, vp, rp, ip = decoder_layer(xp, pos_p, None, None, pos_p, h0_zero, h0_zero, lp, lam_init)
        pk = cache_k[l][page_table].reshape(bs, past_len, ATTN_HEADS, 2, ATTN_QK_DIM)
        pv = cache_v[l][page_table].reshape(bs, past_len, ATTN_HEADS, ATTN_V_DIM)
        xs, kn, vn, rn, inn = decoder_layer(xs, pos_s, pk, pv, kpos_s,
                                            state_ssm_re[l], state_ssm_im[l], lp, lam_init)
        kp_l.append(kp); vp_l.append(vp); rp_l.append(rp); ip_l.append(ip)
        ks_l.append(kn); vs_l.append(vn); rs_l.append(rn); is_l.append(inn)
    y_prompt = rmsnorm(xp, g_final)
    y_sample = rmsnorm(xs, g_final)
    return (y_prompt, y_sample,
            jnp.stack(kp_l), jnp.stack(vp_l), jnp.stack(rp_l), jnp.stack(ip_l),
            jnp.stack(ks_l), jnp.stack(vs_l), jnp.stack(rs_l), jnp.stack(is_l))


_drawn_inputs = setup_inputs


def setup_inputs(seed=0):
    import zlib

    import numpy as np

    out = dict(_drawn_inputs(seed))
    spreads = {}
    factors = {'lambda_q1': 3.535,
     'lambda_k1': 7.322,
     'g_sub': 3.034,
     'ssm_a_re': 15.479,
     'b_glu': 58.352,
     'g_final': 7.629,
     'lambda_k2': 4.169,
     'g_ffn': 4.123}
    for name, (base, spread) in spreads.items():
        noise = np.random.default_rng([zlib.crc32(name.encode()), seed]).standard_normal(out[name].shape)
        drawn = base * np.exp(spread * noise) if base else spread * noise
        out[name] = __import__('jax').numpy.asarray(drawn.astype(out[name].dtype))
    for name, factor in factors.items():
        out[name] = (out[name] * factor).astype(out[name].dtype)
    return out
```

```python
from contextlib import ExitStack

import math

import numpy as np

import concourse.bass as bass
from concourse import mybir

F32 = mybir.dt.float32
F32R = mybir.dt.float32r
I32 = mybir.dt.int32
U32 = mybir.dt.uint32
ALU = mybir.AluOpType
ACT = mybir.ActivationFunctionType
AX = mybir.AxisListType
ds = bass.ds

P = 128
D = 2048
KT = D // P
NS, NT = 8, 512
T = NS + NT
HALVES = ((0, 264), (264, 256))
H = 8
PAST, PAGE = 2048, 128
NPG = PAST // PAGE
N_IN, N_GLU, N_OUT, N_PQ, N_EXP = 32, 4, 16, 16, 128
U_GLU = N_IN
U_OUT = U_GLU + N_GLU
U_PQ = U_OUT + N_OUT
U_EXP_U = U_PQ + N_PQ
U_EXP_V = U_EXP_U + N_EXP
N_UNITS = U_EXP_V + N_EXP
EPS = 1e-6
G = 64
GP = G // 2
CH, NST = 16, 64
CL = 8
NCH = NT // CL
LAM0 = 0.2


class Chain:

    def __init__(self, eng, sem):
        self.eng, self.sem, self.base, self.n = eng, sem, 0, 0

    def __call__(self, ins):
        self.n += 1
        ins.then_inc(self.sem, 1)
        self.eng.wait_ge(self.sem, self.base + self.n)

    def enter(self, i, per):
        self.outer, self.per = self.base + self.n, per
        self.base, self.n = self.outer + i * per, 0

    def leave(self, turns):
        assert self.n == self.per, (self.n, self.per)
        self.base, self.n = self.outer + turns * self.per, 0


def common(nc, ctx, ins, outs):
    class K: pass
    m = K()
    base = (nc.sbuf_base + 63) // 64 * 64
    m.top = base
    def at(name, shape, dt=F32, off=None):
        size = int(np.prod(shape[1:])) * 4
        size = (size + 31) // 32 * 32
        if off is None:
            off = m.top = (m.top + 31) // 32 * 32
            m.top += size
        assert off + size <= nc.sbuf_usable_end, (name, off, size, nc.sbuf_usable_end)
        t = nc.alloc_sbuf_tensor_at(name, shape, dt, offset=off)
        m.end = off + size
        return t
    m.at = at
    m.sem = lambda n: ctx.enter_context(nc.semaphore(n))
    m.ident = at("ident", [P, P]); m.ones = at("ones", [P, P]); m.rot = at("rot", [P, P])
    m.gains = at("gains", [P, 3, KT]); m.eps = at("eps", [P, 1]); m.pages = at("pages", [1, P], I32); m.lam = at("lam", [P, 8])
    m.qs = at("qs", [P, H, NS])
    m.x0 = m.top
    m.xt = at("xt", [P, KT, T]); m.hh = at("hh", [P, KT, T], F32R); m.hl = at("hl", [P, KT, T], F32R)
    m.raw = [at(f"raw{s}", [P, KT, P]) for s in range(2)]
    m.wh = [at(f"wh{s}", [P, KT, P], F32R) for s in range(2)]
    m.wl = [at(f"wl{s}", [P, KT, P], F32R) for s in range(2)]
    m.scd = at("scd", [P, NPG, P])
    m.free = m.top
    m.acc = ctx.enter_context(nc.psum_tensor("acc", [P, 2, 2, 512], F32))
    m.aux = ctx.enter_context(nc.psum_tensor("aux", [P, 4, 512], F32))
    m.raw_in = [m.sem(f"raw_in{s}") for s in range(2)]
    m.hi_done = m.sem("hi_done"); m.lo_done = m.sem("lo_done"); m.mm_done = m.sem("mm_done"); m.acc_free = m.sem("acc_free")
    m.units = ins["units"]
    return m

def load_unit(m, sp, u, s):
    sp.wait_ge(m.lo_done, u + 1)
    sp.dma_start(m.raw[s][:, :, :].rearrange("p k n -> p (k n)"), m.units[ds(u, 1), :, :].rearrange("a p n -> (a p) n")).then_inc(m.raw_in[s], 16)

def split_hi(m, act, u, s, pair):
    act.wait_ge(m.raw_in[s], pair * 16 + 16)
    act.wait_ge(m.mm_done, u + 1)
    act.activation(m.wh[s][:, :, :], m.raw[s][:, :, :], ACT.Copy).then_inc(m.hi_done, 1)

def split_lo(m, pool, u, s):
    pool.wait_ge(m.hi_done, u + 1)
    pool.tensor_tensor(m.wl[s][:, :, :], m.raw[s][:, :, :], m.wh[s][:, :, :].bitcast(F32), ALU.subtract).then_inc(m.lo_done, 1)

def unit_matmuls(m, pe, u, s, rhs_hi, rhs_lo, acc_slot, k_range=range(KT), first=True, wait_k=None, out=None):
    pe.wait_ge(m.lo_done, u + 3)
    pe.wait_ge(m.acc_free, u + 1)
    if wait_k is None:
        order = [(h, k) for h in range(2) for k in k_range]
    else:
        order = [(h, k) for k in k_range for h in range(2)]
    k_range = list(k_range)
    for h, k in order:
        if wait_k is not None and h == 0:
            pe.wait_ge(wait_k, k + 1)
        c0, n = HALVES[h]
        o = m.acc[:, acc_slot, h, 0:n]
        pe.matmul(o, m.wh[s][:, k, :], rhs_hi[:, k, c0:c0 + n], start=(k == k_range[0]), stop=False)
        pe.matmul(o, m.wh[s][:, k, :], rhs_lo[:, k, c0:c0 + n], start=False, stop=False)
        mm = pe.matmul(o, m.wl[s][:, k, :], rhs_hi[:, k, c0:c0 + n], start=False, stop=(k == k_range[-1]))
    mm.then_inc(m.mm_done, 1)

def halves_copy(eng_op, out, m, slot):
    for h, (c0, n) in enumerate(HALVES):
        ins = eng_op(out[:, c0:c0 + n], m.acc[:, slot, h, 0:n])
    return ins

def stage_a(nc, m, ins, outs):
    at, sem = m.at, m.sem
    m.top = m.free
    cosT = at("cosT", [P, T]); sinT = at("sinT", [P, T])
    zst = [at(f"zst{j}", [P, T]) for j in range(3)]
    zo = [at(f"zo{j}", [P, T]) for j in range(2)]
    t1 = at("t1", [P, T]); t2 = at("t2", [P, T])
    kring = at("kring", [P, 6, 1024]); sq = at("sq", [P, 4, T], F32, off=m.top - 6 * 4096)
    prod = at("prod", [P, 1024]); rs = at("rs", [P, T])
    qb = at("qb", [P, NS, 1024], F32, off=m.x0)
    c_in, x_in = sem("c_in"), [sem(f"x_in{j}") for j in range(4)]
    sq_ready, sq_used = sem("sq_ready"), sem("sq_used")
    rt_ready, h_ready, hh_ready, hl_ready = sem("rt_ready"), sem("h_ready"), sem("hh_ready"), sem("hl_ready")
    z_ready = sem("z_ready")
    rope_done, rot_ready, rot_free = sem("rope_done"), sem("rot_ready"), sem("rot_free")
    st_zo = [sem(f"st_zo{j}") for j in range(2)]; st_v, st_u, st_k = sem("st_v"), sem("st_u"), sem("st_k")
    qs_done, qb_mm, qb_ready = sem("qs_done"), sem("qb_mm"), sem("qb_ready")
    kp_in, kp_free = [sem(f"kp_in{j}") for j in range(6)], sem("kp_free")
    s_v = sem("s_v")
    qT, kT, vT, uT = m.qT, m.kT, m.vT, m.uT
    keys = ins["cache_k"]
    PQ = 4
    PM = 4
    with nc.Block() as block:
        @block.sync
        def _(sp):
            for j in range(4):
                sp.dma_start(m.xt[:, 4 * j:4 * j + 4, :], ins["x_t"][:, 4 * j:4 * j + 4, :]).then_inc(x_in[j], 16)
            for a, b in ((m.ident, "ident"), (m.ones, "ones"), (m.rot, "rot"), (cosT, "cos_t"), (sinT, "sin_t"), (m.gains, "gains"), (m.pages, "page_table"), (m.eps, "eps")):
                sp.dma_start(a[:], ins[b][:]).then_inc(c_in, 16)
            for u in range(2):
                load_unit(m, sp, u, u)
            with sp.Fori(0, PQ) as i:
                for s in range(2):
                    load_unit(m, sp, i * 2 + (s + 2), s)
            with sp.Fori(0, PM) as i:
                for n in range(6):
                    load_unit(m, sp, i * 6 + (8 + n + 2), n % 2)
                    for j in range(32 * n // 6, 32 * (n + 1) // 6):
                        page = sp.value_load(m.pages[0:1, ds(i * 32 + j, 1)], min_val=0, max_val=keys.shape[0] - 1)
                        sp.wait_ge(kp_free, i * 32 + (j + 1))
                        sp.dma_start(kring[:, j % 4, :], keys[ds(page, 1), :, :].rearrange("a p n -> (a p) n")).then_inc(kp_in[j % 4], 16)

        @block.scalar
        def _(act):
            act.wait_ge(c_in, 16 * 8)
            for k in range(KT):
                if k % 4 == 0:
                    act.wait_ge(x_in[k // 4], 16)
                if k >= 4:
                    act.wait_ge(sq_used, k - 3)
                act.activation(sq[:, k % 4, :], m.xt[:, k, :], ACT.Square).then_inc(sq_ready, 1)
            act.wait_ge(sq_used, KT)
            for h, (c0, n) in enumerate(HALVES):
                r = act.activation(rs[:, c0:c0 + n], m.aux[:, h, 0:n], ACT.Sqrt, bias=m.eps[:, 0:1], scale=1.0 / D)
                r.then_inc(rt_ready, 1)
            for k in range(KT):
                act.wait_ge(h_ready, k + 1)
                act.activation(m.hh[:, k, :], m.xt[:, k, :], ACT.Copy).then_inc(hh_ready, 1)
            for u in range(2):
                split_hi(m, act, u, u, 0)

            def evac(u, slot, dst, permuted=False):
                act.wait_ge(m.mm_done, u + 3)
                if not permuted:
                    act.activation(dst[:, 0:264], m.acc[:, slot, 0, 0:264], ACT.Copy).then_inc(z_ready, 1)
                    act.activation(dst[:, 264:520], m.acc[:, slot, 1, 0:256], ACT.Copy).then_inc(m.acc_free, 1)
                else:
                    act.activation(dst[:, 0:8], m.acc[:, slot, 0, 0:8], ACT.Copy)
                    v = dst[:, 8:520].rearrange("p (s n) -> p n s", s=CL)
                    act.activation(v[:, 0:32, :], m.acc[:, slot, 0, 8:264].rearrange("p (n s) -> p n s", s=CL), ACT.Copy).then_inc(z_ready, 1)
                    act.activation(v[:, 32:64, :], m.acc[:, slot, 1, 0:256].rearrange("p (n s) -> p n s", s=CL), ACT.Copy).then_inc(m.acc_free, 1)

            with act.Fori(0, PQ) as i:
                for s in range(2):
                    u = i * 2 + s
                    act.wait_ge(rope_done, u + 1)
                    evac(u, s, zst[s])
                    split_hi(m, act, u + 2, s, i + 1)
                for s in range(2):
                    act.wait_ge(rope_done, i * 2 + (s + 3))
                    act.dma_start(qT[ds(i * 2 + s, 1), :, :].rearrange("a p n -> (a p) n"), zo[s][:, :]).then_inc(st_zo[s], 16)
            for b in range(NS):
                for g in range(2):
                    act.wait_ge(qb_mm, 2 * b + g + 1)
                    act.activation(qb[:, b, 512 * g:512 * g + 512], m.aux[:, 2 + g, :], ACT.Copy).then_inc(qb_ready, 1)
            with act.Fori(0, PM) as i:
                for n in range(6):
                    u = i * 6 + (8 + n)
                    kind, half = n % 3, n // 3
                    if kind == 0:
                        act.wait_ge(rope_done, i * 2 + (half + 8 + 2))
                    elif kind == 1:
                        act.wait_ge(st_v, i * 32 + (half + 1) * 16)
                    else:
                        act.wait_ge(st_u, i * 32 + (half + 1) * 16)
                    evac(u, n % 2, zst[kind], permuted=(kind == 2))
                    split_hi(m, act, u + 2, n % 2, i * 3 + (4 + n // 2 + 1))
                    tile = i * 2 + half
                    if kind == 1:
                        act.wait_ge(m.acc_free, u + 3)
                        act.dma_start(vT[ds(tile, 1), :, :].rearrange("a p n -> (a p) n"), zst[1][:, :]).then_inc(st_v, 16)
                        act.wait_ge(rope_done, i * 2 + (half + 8 + 3))
                        act.dma_start(kT[ds(tile, 1), :, :].rearrange("a p n -> (a p) n"), zo[half][:, :]).then_inc(st_zo[half], 16)
                    if kind == 2:
                        act.wait_ge(m.acc_free, u + 3)
                        act.dma_start(uT[ds(tile, 1), :, :].rearrange("a p n -> (a p) n"), zst[2][:, :]).then_inc(st_u, 16)
            act.wait_ge(st_v, 16 * 9)
            act.wait_ge(st_u, 16 * 9)
            for s in range(2):
                act.wait_ge(st_zo[s], 16 * 9)

        @block.gpsimd
        def _(pool):
            pool.sem_inc(m.lo_done, 2); pool.sem_inc(m.mm_done, 2); pool.sem_inc(m.acc_free, 2)
            pool.sem_inc(rope_done, 2); pool.sem_inc(rot_free, 1); pool.sem_inc(kp_free, 4)
            for s in (st_v, st_u, st_zo[0], st_zo[1]):
                pool.sem_inc(s, 16)
            for k in range(KT):
                pool.wait_ge(hh_ready, k + 1)
                pool.tensor_tensor(m.hl[:, k, :], m.xt[:, k, :], m.hh[:, k, :].bitcast(F32), ALU.subtract).then_inc(hl_ready, 1)
            for u in range(2):
                split_lo(m, pool, u, u)
            with pool.Fori(0, PQ) as i:
                for s in range(2):
                    split_lo(m, pool, i * 2 + (s + 2), s)
            with pool.Fori(0, PM) as i:
                for n in range(6):
                    split_lo(m, pool, i * 6 + (8 + n + 2), n % 2)

        @block.tensor
        def _(pe):
            pe.wait_ge(c_in, 16 * 8)
            for k in range(KT):
                pe.wait_ge(sq_ready, k + 1)
                for h, (c0, n) in enumerate(HALVES):
                    mm = pe.matmul(m.aux[:, h, 0:n], m.ones[:, :], sq[:, k % 4, c0:c0 + n], start=(k == 0), stop=(k == KT - 1))
                mm.then_inc(sq_used, 1)

            pe.wait_ge(hl_ready, KT)

            def rotate(src, r, z_count):
                pe.wait_ge(z_ready, z_count)
                pe.wait_ge(m.acc_free, z_count + 2)
                pe.wait_ge(rot_free, r + 1)
                for h, (c0, n) in enumerate(HALVES):
                    mm = pe.matmul(m.aux[:, h, 0:n], m.rot[:, :], src[:, c0:c0 + n], start=True, stop=True)
                mm.then_inc(rot_ready, 1)

            with pe.Fori(0, PQ) as i:
                for s in range(2):
                    unit_matmuls(m, pe, i * 2 + s, s, m.hh, m.hl, s)
                for s in range(2):
                    rotate(zst[s], i * 2 + s, i * 2 + (s + 1))
            pe.wait_ge(qs_done, 8)
            for b in range(NS):
                for g in range(2):
                    if b > 0:
                        pe.wait_ge(qb_ready, 2 * b + g - 1)
                    for q in range(4):
                        mm = pe.matmul(m.aux[:, 2 + g, 128 * q:128 * q + 128], m.qs[:, 4 * g + q, b:b + 1].broadcast_to([P, P]),
                                       m.ident[:, :], start=True, stop=True)
                    mm.then_inc(qb_mm, 1)
            with pe.Fori(0, PM) as i:
                for n in range(6):
                    unit_matmuls(m, pe, i * 6 + (8 + n), n % 2, m.hh, m.hl, n % 2)
                    if n % 3 == 1:
                        rotate(zst[0], i * 2 + (8 + n // 3), i * 6 + (8 + n))

        @block.vector
        def _(dve):
            ch = Chain(dve, s_v)
            dve.wait_ge(c_in, 16 * 8)
            dve.wait_ge(rt_ready, 2)
            ch(dve.reciprocal(rs[:, :], rs[:, :]))
            for k in range(KT):
                dve.scalar_tensor_tensor(m.xt[:, k, :], m.xt[:, k, :], m.gains[:, 0, k:k + 1], rs[:, :], ALU.mult, ALU.mult).then_inc(h_ready, 1)

            def rope(src, dst, r, z_count, dst_free, dst_count):
                dve.wait_ge(m.acc_free, z_count + 2)
                dve.tensor_tensor(t1[:, :], src[:, :], cosT[:, :], ALU.mult)
                dve.wait_ge(rot_ready, r + 1)
                for h, (c0, n) in enumerate(HALVES):
                    x = dve.tensor_tensor(t2[:, c0:c0 + n], m.aux[:, h, 0:n], sinT[:, c0:c0 + n], ALU.mult)
                    if h == 0:
                        ch(x)
                x.then_inc(rot_free, 1)
                dve.wait_ge(rot_free, r + 2)
                dve.wait_ge(dst_free, dst_count)
                dve.tensor_tensor(dst[:, :], t1[:, :], t2[:, :], ALU.add).then_inc(rope_done, 1)

            with dve.Fori(0, PQ) as i:
                ch.enter(i, 2)
                for s in range(2):
                    rope(zst[s], zo[s], i * 2 + s, i * 2 + (s + 1), st_zo[s], i * 16 + 16)
                    dve.wait_ge(rope_done, i * 2 + (s + 3))
                    dve.tensor_copy(m.qs[:, ds(i * 2 + s, 1), :].rearrange("p a b -> p (a b)"), zo[s][:, 0:NS]).then_inc(qs_done, 1)
                ch.leave(PQ)
            with dve.Fori(0, PM) as i:
                ch.enter(i, 2 + 32)
                for n in range(2):
                    for j in range(16):
                        jj = 16 * n + j
                        dve.wait_ge(kp_in[jj % 4], i * 128 + (16 * (jj // 4) + 16))
                        dve.wait_ge(qb_ready, i * 4 + (2 * n + 2))
                        ch(dve.tensor_tensor(prod[:, :], kring[:, jj % 4, :], qb[:, ds(i * 2 + n, 1), :].rearrange("p a b -> p (a b)"), ALU.mult))
                        dst = m.scd[:, j, :].rearrange("p (c b h) -> p b h c", c=2, b=NS)
                        dve.tensor_reduce(dst[:, ds(i * 2 + n, 1), :, :].rearrange("p a h c -> p (a h) c"), prod[:, :].rearrange("p (h c d) -> p h c d", c=2, d=64), AX.X, ALU.add).then_inc(kp_free, 1)
                        if j == 8:
                            rope(zst[0], zo[n], i * 2 + (8 + n), i * 6 + (9 + 3 * n), st_zo[n], i * 16 + (16 * 5))
                        dve.wait_ge(kp_free, i * 32 + (jj + 5))
                ch.leave(PM)

LMASK = 64

def stage_b1(nc, m, ins, outs):
    at, sem = m.at, m.sem
    m.top = m.free
    ot = m.ot = at("ot", [P, H, T])
    stT = at("stT", [P, 2052]); wtk = at("wtk", [P, NPG, NS * H])
    lamv = at("lamv", [P, 4, 64]); lamp = at("lamp", [P, 2, 64]); lam = m.lam
    ksv = at("ksv", [P, 2, H, NS]); tmp = at("tmp", [P, H, NS]); qk2 = at("qk2", [P, 2, NS, H]); dm = at("dm", [P, NS * H]); mm_ = at("mm_", [P, NS * H]); cm = at("cm", [P, 2]); sm = at("sm", [P, 8])
    vring = at("vring", [P, 8, 1024], F32, off=m.x0)
    c2_in, ks_in = sem("c2_in"), sem("ks_in")
    vp_in, vp_free = [sem(f"vp_in{j}") for j in range(8)], sem("vp_free")
    b_tr, b_ev, lam_e, lam_s, qk_ready, ns_ready, nm_ready, ex_ready, m_ready, wt_mm, wt_ev, pv_done, wn_done, od_done = [sem("b_" + x) for x in "tr ev lame lams qk ns nm ex m wtmm wtev pv wn od".split()]
    s_v2 = sem("s_v2")
    vals = ins["cache_v"]
    with nc.Block() as block:
        @block.sync
        def _(sp):
            for a, b in ((dm, "dmask"), (cm, "cmask")):
                sp.dma_start(a[:], ins[b][:]).then_inc(c2_in, 16)
            for j in range(4):
                sp.dma_start(lamv[:, j, :], ins["lambdas"][j:j + 1, :].broadcast_to([P, 64])).then_inc(c2_in, 16)
            sp.dma_start(ksv[:, 0, :, :], m.kT[:, :, 0:NS].rearrange("h p b -> p h b")).then_inc(ks_in, 16)
            sp.dma_start(ksv[:, 1, :, :], m.vT[:, :, 0:NS].rearrange("h p b -> p h b")).then_inc(ks_in, 16)
            with sp.Fori(0, NS) as b:
                for j in range(NPG):
                    page = sp.value_load(m.pages[0:1, ds(b * NPG + j, 1)], min_val=0, max_val=vals.shape[0] - 1)
                    sp.wait_ge(vp_free, b * NPG + (j + 1))
                    sp.dma_start(vring[:, j % 8, :], vals[ds(page, 1), :, :].rearrange("a p n -> (a p) n")).then_inc(vp_in[j % 8], 16)

        @block.gpsimd
        def _(pool):
            pool.sem_inc(vp_free, 8)

        @block.scalar
        def _(act):
            act.wait_ge(lam_s, 1)
            act.activation(lam[:, 2:4], lam[:, 0:2], ACT.Exp).then_inc(lam_e, 1)
            act.wait_ge(nm_ready, 1)
            act.activation(stT[:, 0:2049], stT[:, 0:2049], ACT.Exp, bias=sm[:, 1:2], scale=0.125, accum_out=sm[:, 2:3]).then_inc(ex_ready, 1)

        @block.tensor
        def _(pe):
            for j in range(NPG):
                if j % 4 == 0 and j >= 8:
                    pe.wait_ge(b_ev, j // 4 - 1)
                mm = pe.transpose(m.aux[:, (j // 4) % 2, 128 * (j % 4):128 * (j % 4) + 128], m.scd[:, j, :], m.ident[:, :])
                if j % 4 == 3:
                    mm.then_inc(b_tr, 1)
            pe.wait_ge(qk_ready, 1)
            pe.matmul(m.aux[:, 2, 0:1], qk2[:, :, :, :].rearrange("p c b h -> p (c b h)"), m.ones[:, 0:1], start=True, stop=True).then_inc(ns_ready, 1)
            pe.wait_ge(m_ready, 1)
            pe.wait_ge(ex_ready, 1)
            for j in range(NPG):
                mm = pe.matmul(m.aux[:, j // 8, 64 * (j % 8):64 * (j % 8) + 64], stT[:, 128 * j:128 * j + 128], mm_[:, :], start=True, stop=True)
                if j % 8 == 7:
                    mm.then_inc(wt_mm, 1)
            pe.matmul(m.aux[:, 2, 64:128], stT[:, 2048:2049].broadcast_to([P, P]), mm_[:, :], start=True, stop=True).then_inc(wn_done, 1)
            pe.wait_ge(wt_ev, 2)
            with pe.Fori(0, NS) as b:
                for j in range(NPG):
                    pe.wait_ge(vp_in[j % 8], b * 32 + (16 * (j // 8) + 16))
                    for h in range(H):
                        mm = pe.matmul(m.aux[:, 3, ds(b * H + h, 1)], vring[:, j % 8, 128 * h:128 * h + 128], wtk[:, j, ds(b * H + h, 1)],
                                       start=(j == 0 and h == 0), stop=(j == NPG - 1 and h == H - 1), skip_group_check=True)
                    mm.then_inc(vp_free, 1)

        @block.vector
        def _(dve):
            ch = Chain(dve, s_v2)
            dve.wait_ge(c2_in, 16 * 6)
            ch(dve.tensor_tensor(lamp[:, :, :], lamv[:, 0:4:2, :], lamv[:, 1:4:2, :], ALU.mult))
            dve.tensor_reduce(lam[:, 0:2], lamp[:, :, :], AX.X, ALU.add).then_inc(lam_s, 1)
            dve.wait_ge(ks_in, 32)
            ch(dve.tensor_tensor(tmp[:, :, :], m.qs[:, :, :], ksv[:, 0, :, :], ALU.mult))
            for c in range(2):
                x = dve.tensor_scalar(qk2[:, c, :, :].rearrange("p b h -> p h b"), tmp[:, :, :], cm[:, c:c + 1], None, ALU.mult)
                if c == 0:
                    ch(x)
            x.then_inc(qk_ready, 1)
            for g in range(4):
                dve.wait_ge(b_tr, g + 1)
                dve.tensor_copy(stT[:, 512 * g:512 * g + 512], m.aux[:, g % 2, :]).then_inc(b_ev, 1)
            dve.wait_ge(ns_ready, 1)
            dve.wait_ge(b_ev, 4)
            ch(dve.tensor_copy(stT[:, 2048:2049], m.aux[:, 2, 0:1]))
            ch(dve.tensor_reduce(sm[:, 0:1], stT[:, 0:2049], AX.X, ALU.max))
            dve.tensor_scalar(sm[:, 1:2], sm[:, 0:1], -0.125, None, ALU.mult).then_inc(nm_ready, 1)
            dve.wait_ge(lam_e, 1)
            ch(dve.tensor_tensor(lam[:, 4:5], lam[:, 3:4], lam[:, 2:3], ALU.subtract))
            ch(dve.tensor_scalar(lam[:, 4:5], lam[:, 4:5], -LAM0, None, ALU.add))
            ch(dve.scalar_tensor_tensor(sm[:, 4:5], cm[:, 1:2], lam[:, 4:5], cm[:, 0:1], ALU.mult, ALU.add))
            dve.wait_ge(ex_ready, 1)
            ch(dve.reciprocal(sm[:, 5:6], sm[:, 2:3]))
            ch(dve.tensor_tensor(sm[:, 6:7], sm[:, 5:6], sm[:, 4:5], ALU.mult))
            dve.tensor_scalar(mm_[:, :], dm[:, :], sm[:, 6:7], None, ALU.mult).then_inc(m_ready, 1)
            for g in range(2):
                dve.wait_ge(wt_mm, g + 1)
                dve.tensor_copy(wtk[:, 8 * g:8 * g + 8, :].rearrange("p j n -> p (j n)"), m.aux[:, g, :]).then_inc(wt_ev, 1)
            dve.wait_ge(wn_done, 1)
            ch(dve.tensor_tensor(tmp[:, :, :], m.aux[:, 2, 64:128].rearrange("p (b h) -> p h b", h=H), ksv[:, 1, :, :], ALU.mult))
            dve.wait_ge(vp_free, 8 + NS * NPG)
            dve.tensor_tensor(ot[:, :, 0:NS], m.aux[:, 3, 0:64].rearrange("p (b h) -> p h b", h=H), tmp[:, :, :], ALU.add).then_inc(od_done, 1)

def stage_b2(nc, m, ins, outs):
    at, sem = m.at, m.sem
    m.top = m.free
    at("ot_keep", [P, H, T])
    lam = m.lam
    qkv = at("qkv", [P, 2, 3, NT]); cmk = at("causal", [P, P])
    m.top = m.x0
    vtok = at("vtok", [P, 2, 4, P]); ex = at("ex", [P, 2, 2, NT]); dg = at("dg", [P, 2, 2, P]); wT = at("wT", [P, 2, 4, P])
    st = at("stt", [P, 2, 2, 8])
    q_in = [sem(f"q_in{j}") for j in range(2)]; h_free = sem("h_free"); cm_in = sem("cm_in")
    v_tr, v_ev, s_mm, s_free, nm_r, e_r, d_r, w_mm, w_ev, o_mm, o_ev, e_free, s_v3 = [sem("p_" + x) for x in "vtr vev smm sfree nm e d wmm wev omm oev efree v3".split()]
    R = H * 4
    with nc.Block() as block:
        @block.sync
        def _(sp):
            sp.dma_start(cmk[:, :], ins["causal"][:, :]).then_inc(cm_in, 16)
            with sp.Fori(0, H // 2) as hh:
                for s in range(2):
                    sp.wait_ge(h_free, hh * 2 + (s + 1))
                    for n, t in enumerate((m.qT, m.kT, m.vT)):
                        sp.dma_start(qkv[:, s, n, :], t[ds(hh * 2 + s, 1), :, NS:T].rearrange("a p n -> (a p) n")).then_inc(q_in[s], 16)

        @block.gpsimd
        def _(pool):
            for s, n in ((h_free, 2), (s_free, 2), (e_free, 2), (v_ev, 1), (w_ev, 2), (o_ev, 2), (o_mm, 2)):
                pool.sem_inc(s, n)

        @block.tensor
        def _(pe):
            with pe.Fori(0, H // 2) as hh:
                for s in range(2):
                    pe.wait_ge(q_in[s], hh * 48 + 48)
                    it = lambda q: hh * 8 + (4 * s + q)
                    for step in range(4 + 2):
                        if step < 4:
                            q = step
                            pe.wait_ge(s_free, it(q) + 1)
                            for c in range(2):
                                mm = pe.matmul(m.acc[:, q % 2, c, 0:128 * (q + 1)], qkv[64 * c:64 * c + 64, s, 0, 128 * q:128 * q + 128],
                                               qkv[64 * c:64 * c + 64, s, 1, 0:128 * (q + 1)], start=True, stop=True)
                            mm.then_inc(s_mm, 1)
                            if step == 0:
                                pe.wait_ge(o_ev, it(q))
                                pe.wait_ge(v_ev, hh * 2 + (s + 1))
                                for kb in range(4):
                                    mm = pe.transpose(m.aux[:, 3, 128 * kb:128 * kb + 128], qkv[:, s, 2, 128 * kb:128 * kb + 128], m.ident[:, :])
                                mm.then_inc(v_tr, 1)
                        if 1 <= step <= 4:
                            q = step - 1
                            pe.wait_ge(d_r, it(q) + 1)
                            pe.wait_ge(e_r, hh * 16 + (8 * s + 2 * q + 2))
                            pe.wait_ge(w_ev, it(q) + 1)
                            for kb in range(q + 1):
                                for c in range(2):
                                    mm = pe.matmul(m.aux[:, q % 2, 128 * kb:128 * kb + 128], ex[:, q % 2, c, 128 * kb:128 * kb + 128], dg[:, q % 2, c, :],
                                                   start=(c == 0), stop=(c == 1))
                            mm.then_inc(w_mm, 1)
                        if step >= 2:
                            q = step - 2
                            pe.wait_ge(w_ev, it(q) + 3)
                            pe.wait_ge(v_ev, hh * 2 + (s + 2))
                            pe.wait_ge(o_ev, it(q) + 2)
                            for kb in range(q + 1):
                                mm = pe.matmul(m.aux[:, 2, 0:128], vtok[:, s, kb, :], wT[:, q % 2, kb, :], start=(kb == 0), stop=(kb == q))
                            mm.then_inc(o_mm, 1)

        @block.scalar
        def _(act):
            with act.Fori(0, H // 2) as hh:
                for s in range(2):
                    it = lambda q: hh * 8 + (4 * s + q)
                    for step in range(4 + 2):
                        if step < 4:
                            q = step
                            act.wait_ge(nm_r, it(q) + 1)
                            act.wait_ge(e_free, it(q) + 1)
                            for c in range(2):
                                x = act.activation(ex[:, q % 2, c, 0:128 * (q + 1)], m.acc[:, q % 2, c, 0:128 * (q + 1)], ACT.Exp, bias=st[:, q % 2, c, 1:2], scale=0.125,
                                               accum_out=st[:, q % 2, c, 2:3])
                                x.then_inc(e_r, 1)
                            act.wait_ge(e_r, hh * 16 + (8 * s + 2 * q + 2))
                            act.sem_inc(s_free, 1)
                        if step == 1:
                            act.wait_ge(v_tr, hh * 2 + (s + 1))
                            act.wait_ge(o_mm, hh * 8 + (4 * s + 1))
                            act.activation(vtok[:, s, :, :].rearrange("p a b -> p (a b)"), m.aux[:, 3, :], ACT.Copy).then_inc(v_ev, 1)
                        if 1 <= step <= 4:
                            q = step - 1
                            act.wait_ge(w_mm, it(q) + 1)
                            act.sem_inc(e_free, 1)
                            act.wait_ge(o_mm, it(q) + 1)
                            act.activation(wT[:, q % 2, 0:q + 1, :].rearrange("p a b -> p (a b)"), m.aux[:, q % 2, 0:128 * (q + 1)], ACT.Copy).then_inc(w_ev, 1)
                        if step >= 2:
                            q = step - 2
                            act.wait_ge(o_mm, it(q) + 3)
                            act.activation(m.ot[:, ds(hh * 2 + s, 1), NS + 128 * q:NS + 128 * q + 128].rearrange("p a b -> p (a b)"), m.aux[:, 2, 0:128], ACT.Copy).then_inc(o_ev, 1)
                    act.wait_ge(o_ev, hh * 8 + (4 * s + 6))
                    act.sem_inc(h_free, 1)

        @block.vector
        def _(dve):
            ch = Chain(dve, s_v3)
            dve.wait_ge(cm_in, 16)
            with dve.Fori(0, H // 2) as hh:
                ch.enter(hh, 2 * (4 * 3 * 2 + 4 * 3))
                for s in range(2):
                    it = lambda q: hh * 8 + (4 * s + q)
                    for step in range(5):
                        if step < 4:
                            q = step
                            dve.wait_ge(s_mm, it(q) + 1)
                            for c in range(2):
                                sc = m.acc[:, q % 2, c, :]
                                ch(dve.tensor_tensor(sc[:, 128 * q:128 * q + 128], sc[:, 128 * q:128 * q + 128], cmk[:, :], ALU.add))
                                ch(dve.tensor_reduce(st[:, q % 2, c, 0:1], sc[:, 0:128 * (q + 1)], AX.X, ALU.max))
                                ch(dve.tensor_scalar(st[:, q % 2, c, 1:2], st[:, q % 2, c, 0:1], -0.125, None, ALU.mult))
                            dve.sem_inc(nm_r, 1)
                        if step >= 1:
                            q = step - 1
                            dve.wait_ge(e_r, hh * 16 + (8 * s + 2 * q + 2))
                            dve.wait_ge(e_free, it(q) + 1)
                            for c in range(2):
                                x = dve.reciprocal(st[:, q % 2, c, 3:4], st[:, q % 2, c, 2:3])
                                if c == 1:
                                    ch(x)
                                    ch(dve.tensor_tensor(st[:, q % 2, c, 3:4], st[:, q % 2, c, 3:4], lam[:, 4:5], ALU.mult))
                                else:
                                    ch(x)
                            for c in range(2):
                                x = dve.tensor_scalar(dg[:, q % 2, c, :], m.ident[:, :], st[:, q % 2, c, 3:4], None, ALU.mult)
                            x.then_inc(d_r, 1)
                ch.leave(H // 2)

TAU_HI = 6.28125
TAU_MID = 0.0019350051879882812
TAU_LO = 2 * math.pi - TAU_HI - TAU_MID
MAGIC = 1.5 * 2.0 ** 23
QP = 4
PPQ = GP // QP
NC = NCH + NS

def stage_s5(nc, m, ins, outs):
    at, sem = m.at, m.sem
    m.top = m.free; at("ot_keep2", [P, H, T])
    et = at("et", [P, 2, PPQ, P]); tz = at("tz", [P, 2 * PPQ, P], F32, off=m.top - 2 * PPQ * P * 4)
    qm = at("qm", [P, 2, 2, PPQ, 9, CH])
    tr = at("tr", [P, PPQ, 9, CH]); tr_off = m.end - PPQ * 9 * CH * 4
    m.top = m.x0
    ug = at("ug", [P, G, NC + NS])
    vv = at("vv", [P, NC, 2, GP]); yall = at("yall", [P, G, NC], F32, off=m.top - NC * 2 * GP * 4)
    assert G == 2 * GP
    hs = at("hs", [P, NC + 1, 3, GP])
    e = at("e", [P, 2, PPQ, CL, CH]); km = at("km", [CH, 2 * PPQ, P], F32, off=m.top - 2 * PPQ * CL * CH * 4)
    qq = at("qq", [P, 2, PPQ, 9, CH])
    ti = at("ti", [P, PPQ, 9, CH])
    pw = at("pw", [P, 2, 9, GP]); bb = at("bb", [P, 2, GP, CH])
    tb = at("tb", [P, GP, CH], F32, off=tr_off); hn2 = at("hn2", [P, NS, 2, GP], F32, off=tr_off)
    de = at("de", [CH, 2 * PPQ, CH])
    hn = at("hn", [P, NS, 2, GP]); dk = at("dk", [CH, G])
    assert m.top <= m.x0 + 3 * KT * T * 4, m.top - m.x0
    bc = at("bc", [P, 4, GP, CH], F32, off=m.free - NPG * P * 4)
    m.top = m.free; at("ot_keep3", [P, H, T]); m.top += (2 * PPQ * P + 2 * 2 * PPQ * 9 * CH + PPQ * 9 * CH) * 4
    sm = at("s5sm", [P, 24, GP]); a1 = at("a1", [P, 2, 2, GP]); a2 = at("a2", [P, 2, 2, GP])
    u1 = at("u1", [P, 2, GP]); u2 = at("u2", [P, 2, GP])
    cm5 = at("cm5", [P, 4])
    small_in, bc_in, h_in, dk_in = sem("small_in"), sem("bc_in"), sem("h_in"), sem("dk_in")
    ug_zero, ug_in, y_out, sh_in = sem("ug_zero"), sem("ug_in"), sem("y_out"), sem("sh_in")
    a_exp, d_x, a_sin, d_r, p_done, bb_done = [sem("f_" + x) for x in "aexp dx asin dr pw bb".split()]
    e_re, e_im, e_tr, e_ev, v_mm, v_ev, scan_d, hn_d = [sem("f_" + x) for x in "ere eim etr eev vmm vev scan hn".split()]
    q_re, q_im, q_mask, k_mm, k_ev, k_d, y_mm, y_ev, s_v4, s_p4, tz_zero, de_d = [sem("f_" + x) for x in "qre qim qmask kmm kev kd ymm yev v4 p4 tz de".split()]
    f = lambda j: sm[:, j, :]
    with nc.Block() as block:
        @block.sync
        def _(sp):
            for j, n in enumerate(("a_re", "a_im", "log_dt")):
                sp.dma_start(sm[:, j, :], ins[n][:, :]).then_inc(small_in, 16)
            sp.dma_start(cm5[:, :], ins["cmask4"][:, :]).then_inc(small_in, 16)
            for j, n in enumerate(("b_re", "b_im", "c_re", "c_im")):
                sp.dma_start(bc[:, j, :, :], ins[n][:, :, :]).then_inc(bc_in, 16)
            for r, n in enumerate(("h0_re", "h0_im")):
                sp.dma_start(hs[:, NCH:NC, r, :], ins[n][:, :, :]).then_inc(h_in, 16)
            sp.dma_start(dk[:, :], ins["d_t"][:, :]).then_inc(dk_in, 16)
            uv = m.uT[:, :, :].rearrange("a (g c) n -> c (a g) n", c=CH)
            sp.wait_ge(ug_zero, 1)
            for j in range(CL):
                s0 = NS + (CL - 1 - j) * NCH
                sp.dma_start(ug[CH * j:CH * j + CH, :, NS:NC], uv[:, :, s0:s0 + NCH]).then_inc(ug_in, 16)
            sp.dma_start(ug[0:CH, :, 0:NS], uv[:, :, 0:NS]).then_inc(ug_in, 16)
            sp.dma_start(ug[P - CH:P, :, NC:NC + NS], uv[:, :, 0:NS]).then_inc(ug_in, 16)
            for q in range(QP):
                sp.wait_ge(k_d, q + 1)
                if q >= 1:
                    sp.wait_ge(y_mm, 4 * q)
                else:
                    sp.wait_ge(tz_zero, 1)
                for j in range(CL):
                    sp.dma_start(tz[CH * j:CH * j + CH, :, CH * (CL - 1 - j):P], km[:, :, 0:CH * (j + 1)]).then_inc(sh_in, 16)
                sp.wait_ge(sh_in, 16 * CL * (q + 1))
            yv = m.yT[:, :, :].rearrange("a (g c) n -> c (a g) n", c=CH)
            sp.wait_ge(y_ev, 4 * QP)
            for s in range(CL):
                sp.dma_start(yv[:, :, NS + s * NCH:NS + (s + 1) * NCH], yall[CH * s:CH * s + CH, :, 0:NCH]).then_inc(y_out, 16)
            sp.dma_start(yv[:, :, 0:NS], yall[0:CH, :, NCH:NC]).then_inc(y_out, 16)
            sp.wait_ge(scan_d, NCH)
            sp.dma_start(outs["ssm_prompt"][:, :, :], hs[:, NC, 0:2, :]).then_inc(y_out, 16)
            sp.wait_ge(hn_d, 1)
            sp.dma_start(outs["ssm_sample"][:, :, :, :], hn[:, :, :, :]).then_inc(y_out, 16)
            sp.wait_ge(y_out, 16 * (CL + 3))

        def cplx(eng, ch, dst, a, b, c, d, t, op):
            ch(eng.tensor_tensor(t, c, d, ALU.mult))
            ch(eng.tensor_tensor(dst, a, b, ALU.mult))
            return eng.tensor_tensor(dst, dst, t, op)

        def e_args(q, im):
            g = slice(PPQ * q, PPQ * q + PPQ)
            B = [bb[:, r, g, :].unsqueeze(2).broadcast_to([P, PPQ, CL, CH]) for r in range(2)]
            W = [pw[:, r, 0:CL, g].rearrange("p j g -> p g j").unsqueeze(3).broadcast_to([P, PPQ, CL, CH]) for r in range(2)]
            return (B[0], W[1], B[1], W[0]) if im else (B[0], W[0], B[1], W[1])

        def q_args(q, im):
            g = slice(PPQ * q, PPQ * q + PPQ)
            C = [bc[:, 2 + r, g, :].unsqueeze(2).broadcast_to([P, PPQ, 9, CH]) for r in range(2)]
            W = [pw[:, r, :, g].rearrange("p j g -> p g j").unsqueeze(3).broadcast_to([P, PPQ, 9, CH]) for r in range(2)]
            return (C[0], W[1], C[1], W[0]) if im else (C[0], W[0], C[1], W[1])

        @block.gpsimd
        def _(pool):
            ch = Chain(pool, s_p4)
            pool.memset(ug[:, :, :], 0.0).then_inc(ug_zero, 1)
            pool.wait_ge(bb_done, 1)
            pool.wait_ge(p_done, 1)
            for q in range(QP):
                if q >= 1:
                    pool.wait_ge(e_tr, 4 * q)
                cplx(pool, ch, e[:, 1, :, :, :], *e_args(q, True), ti[:, :, 0:CL, :], ALU.add).then_inc(e_im, 1)
                pool.wait_ge(e_im, q + 1)
            pool.wait_ge(v_mm, 4 * QP)
            pool.memset(tz[:, :, :], 0.0).then_inc(tz_zero, 1)
            for q in range(QP):
                if q >= 1:
                    pool.wait_ge(q_mask, 4 * q)
                cplx(pool, ch, qq[:, 1, :, :, :], *q_args(q, True), ti[:, :, :, :], ALU.add).then_inc(q_im, 1)
                pool.wait_ge(q_im, q + 1)

        @block.scalar
        def _(act):
            act.wait_ge(small_in, 64)
            act.activation(f(3), f(2), ACT.Exp).then_inc(a_exp, 1)
            act.wait_ge(d_x, 1)
            act.activation(f(6), f(4), ACT.Exp).then_inc(a_exp, 1)
            act.wait_ge(d_r, 1)
            act.activation(f(9), f(7), ACT.Sin).then_inc(a_sin, 1)
            act.activation(f(10), f(8), ACT.Sin).then_inc(a_sin, 1)
            for q in range(QP):
                for n in range(4):
                    act.wait_ge(e_tr, 4 * q + n + 1)
                    if q >= 1:
                        act.wait_ge(v_mm, 4 * q)
                    act.activation(et[:, n // 2, 4 * (n % 2):4 * (n % 2) + 4, :].rearrange("p a b -> p (a b)"), m.aux[:, n, :], ACT.Copy).then_inc(e_ev, 1)
                for n in range(4):
                    act.wait_ge(v_mm, 4 * q + n + 1)
                    g0 = PPQ * q + 4 * (n % 2)
                    act.activation(vv[:, :, n // 2, g0:g0 + 4].rearrange("p n g -> p g n"), m.acc[:, n // 2, n % 2, 0:4 * NC].rearrange("p (g n) -> p g n", g=4), ACT.Copy).then_inc(v_ev, 1)
            for q in range(QP):
                act.wait_ge(q_re, q + 1)
                act.wait_ge(q_im, q + 1)
                if q >= 1:
                    act.wait_ge(y_mm, 4 * q)
                for g2 in range(2):
                    for r in range(2):
                        act.activation(qm[:, g2, r, :, :, :], qq[:, r, :, :, :], ACT.Copy, scale=cm5[:, 2 * r + g2:2 * r + g2 + 1]).then_inc(q_mask, 1)
                for n in range(4):
                    act.wait_ge(k_mm, 4 * q + n + 1)
                    if q >= 1:
                        act.wait_ge(sh_in, 16 * CL * q)
                    act.activation(km[:, 4 * n:4 * n + 4, :].rearrange("p a b -> p (a b)"), m.aux[0:CH, n, :], ACT.Copy).then_inc(k_ev, 1)
                for n in range(4):
                    act.wait_ge(y_mm, 4 * q + n + 1)
                    act.wait_ge(scan_d, NCH)
                    act.wait_ge(hn_d, 1)
                    act.activation(yall[:, 16 * q + 4 * n:16 * q + 4 * n + 4, :], m.acc[:, n // 2, n % 2, 0:4 * NC].rearrange("p (g n) -> p g n", g=4), ACT.Copy).then_inc(y_ev, 1)

        @block.tensor
        def _(pe):
            for q in range(QP):
                pe.wait_ge(e_re, q + 1)
                pe.wait_ge(e_im, q + 1)
                for n in range(4):
                    if q >= 1:
                        pe.wait_ge(e_ev, 4 * (q - 1) + n + 1)
                    for a in range(4):
                        mm = pe.transpose(m.aux[:, n, P * a:P * a + P], e[:, n // 2, 4 * (n % 2) + a, :, :].rearrange("p j c -> p (j c)"), m.ident[:, :])
                    mm.then_inc(e_tr, 1)
                pe.wait_ge(ug_in, 16 * (CL + 2))
                for n in range(4):
                    pe.wait_ge(e_ev, 4 * q + n + 1)
                    if q >= 1:
                        pe.wait_ge(v_ev, 4 * (q - 1) + n + 1)
                    for a in range(4):
                        gp = PPQ * q + 4 * (n % 2) + a
                        for g2 in range(2):
                            mm = pe.matmul(m.acc[64 * g2:64 * g2 + 64, n // 2, n % 2, NC * a:NC * a + NC], et[:, n // 2, 4 * (n % 2) + a, 64 * g2:64 * g2 + 64],
                                           ug[:, 2 * gp + g2, 0:NC], start=True, stop=True)
                    mm.then_inc(v_mm, 1)
            for q in range(QP):
                pe.wait_ge(q_mask, 4 * q + 4)
                for n in range(4):
                    pe.wait_ge(k_ev, 4 * (q - 1) + n + 1) if q >= 1 else pe.wait_ge(e_ev, 4 * QP)
                    for a in range(4):
                        g = 4 * n + a
                        for r in range(2):
                            mm = pe.matmul(m.aux[0:CH, n, P * a:P * a + P], bb[:, r, PPQ * q + g // 2, :], qm[:, g % 2, r, g // 2, 0:CL, :].rearrange("p j c -> p (j c)"),
                                           start=(r == 0), stop=(r == 1))
                    mm.then_inc(k_mm, 1)
                pe.wait_ge(sh_in, 16 * CL * (q + 1))
                pe.wait_ge(scan_d, NCH)
                pe.wait_ge(h_in, 32)
                for n in range(4):
                    pe.wait_ge(y_ev, 4 * (q - 1) + n + 1) if q >= 1 else pe.wait_ge(v_ev, 4 * QP)
                    for a in range(4):
                        g = 4 * n + a
                        o = m.acc[:, n // 2, n % 2, NC * a:NC * a + NC]
                        pe.matmul(o, tz[:, g, :], ug[:, 16 * q + g, NS:NC + NS], start=True, stop=False)
                        for r in range(2):
                            mm = pe.matmul(o, qm[:, g % 2, r, g // 2, 1:9, :].rearrange("p j c -> p (j c)"), hs[:, 0:NC, r, PPQ * q + g // 2], start=False, stop=(r == 1))
                    mm.then_inc(y_mm, 1)

        @block.vector
        def _(dve):
            ch = Chain(dve, s_v4)
            tt = lambda o, a, b, op: ch(dve.tensor_tensor(o, a, b, op))
            ts = lambda o, a, s1, s2, o1, o2=None: ch(dve.tensor_scalar(o, a, s1, s2, o1, o2) if o2 is not None else dve.tensor_scalar(o, a, s1, None, o1))
            dve.wait_ge(small_in, 64)
            dve.wait_ge(a_exp, 1)
            tt(f(5), f(1), f(3), ALU.mult)
            dve.tensor_tensor(f(4), f(0), f(3), ALU.mult).then_inc(d_x, 1)
            for out, quarter in ((7, 0.0), (8, 0.25)):
                ts(f(11), f(5), 1 / (2 * math.pi), quarter, ALU.mult, ALU.add)
                ts(f(11), f(11), MAGIC, None, ALU.add)
                ts(f(11), f(11), -MAGIC, None, ALU.add)
                ch(dve.scalar_tensor_tensor(f(12), f(11), -TAU_HI, f(5), ALU.mult, ALU.add))
                ch(dve.scalar_tensor_tensor(f(12), f(11), -TAU_MID, f(12), ALU.mult, ALU.add))
                ch(dve.scalar_tensor_tensor(f(12), f(11), -TAU_LO, f(12), ALU.mult, ALU.add))
                if quarter:
                    ts(f(12), f(12), math.pi / 2, None, ALU.add)
                ts(f(out), f(12), 3.1415925, -3.1415925, ALU.min, ALU.max)
            ch(dve.memset(pw[:, 0, 0, :], 1.0))
            dve.memset(pw[:, 1, 0, :], 0.0).then_inc(d_r, 1)
            dve.wait_ge(d_r, 1)
            dve.wait_ge(a_sin, 2)
            dve.wait_ge(a_exp, 2)
            tt(pw[:, 0, 1, :], f(6), f(10), ALU.mult)
            tt(pw[:, 1, 1, :], f(6), f(9), ALU.mult)

            def powers(lo, n, by):
                a = [pw[:, r, lo:lo + n, :] for r in range(2)]
                b = [pw[:, r, by:by + 1, :].broadcast_to([P, n, GP]) for r in range(2)]
                t = sm[:, 13:13 + n, :]
                ch(cplx(dve, ch, pw[:, 0, by + lo:by + lo + n, :], a[0], b[0], a[1], b[1], t, ALU.subtract))
                return cplx(dve, ch, pw[:, 1, by + lo:by + lo + n, :], a[0], b[1], a[1], b[0], t, ALU.add)

            ch(powers(1, 1, 1))
            ch(powers(1, 2, 2))
            powers(1, 4, 4).then_inc(p_done, 1)
            dve.wait_ge(p_done, 1)
            tt(f(13), f(0), f(0), ALU.mult)
            tt(f(14), f(1), f(1), ALU.mult)
            tt(f(13), f(13), f(14), ALU.add)
            ch(dve.reciprocal(f(13), f(13)))
            ts(f(14), pw[:, 0, 1, :], -1.0, None, ALU.add)
            ch(cplx(dve, ch, f(15), f(14), f(0), pw[:, 1, 1, :], f(1), f(17), ALU.add))
            ch(cplx(dve, ch, f(16), pw[:, 1, 1, :], f(0), f(14), f(1), f(17), ALU.subtract))
            tt(f(15), f(15), f(13), ALU.mult)
            tt(f(16), f(16), f(13), ALU.mult)
            fr = [f(15 + r).unsqueeze(2).broadcast_to([P, GP, CH]) for r in range(2)]
            dve.wait_ge(bc_in, 64)
            ch(cplx(dve, ch, bb[:, 0, :, :], fr[0], bc[:, 0, :, :], fr[1], bc[:, 1, :, :], tb[:, :, :], ALU.subtract))
            cplx(dve, ch, bb[:, 1, :, :], fr[0], bc[:, 1, :, :], fr[1], bc[:, 0, :, :], tb[:, :, :], ALU.add).then_inc(bb_done, 1)
            dve.wait_ge(bb_done, 1)
            for k, j in ((0, CL), (1, 1)):
                for r in range(2):
                    ch(dve.tensor_copy(a1[:, k, r, :], pw[:, 0, j, :]))
                ts(a2[:, k, 0, :], pw[:, 1, j, :], -1.0, None, ALU.mult)
                ch(dve.tensor_copy(a2[:, k, 1, :], pw[:, 1, j, :]))
            for q in range(QP):
                if q >= 1:
                    dve.wait_ge(e_tr, 4 * q)
                cplx(dve, ch, e[:, 0, :, :, :], *e_args(q, False), tr[:, :, 0:CL, :], ALU.subtract).then_inc(e_re, 1)
                dve.wait_ge(e_re, q + 1)
            dve.wait_ge(dk_in, 16)
            ch(dve.memset(hs[:, 0, :, :], 0.0))
            dve.wait_ge(v_ev, 4 * QP)
            dve.wait_ge(h_in, 32)
            for n in range(NCH):
                src = hs[:, n, :, :]
                dst = hs[:, n + 1 if n < NCH - 1 else NC, :, :]
                dve.tensor_tensor(u1[:, :, :], src[:, 0:2, :], a1[:, 0, :, :], ALU.mult)
                ch(dve.tensor_tensor(u2[:, :, :], src[:, 1:3, :], a2[:, 0, :, :], ALU.mult))
                ch(dve.tensor_tensor(u1[:, :, :], u1[:, :, :], vv[:, NS + n, :, :], ALU.add))
                dve.tensor_tensor(dst[:, 0:2, :], u1[:, :, :], u2[:, :, :], ALU.add).then_inc(scan_d, 1)
                ch(dve.tensor_tensor(dst[:, 2, :], u1[:, 0, :], u2[:, 0, :], ALU.add))
                dve.wait_ge(scan_d, n + 1)
            bcs = lambda x: x.unsqueeze(1).broadcast_to([P, NS, GP])
            for r in range(2):
                o = 1 - r
                tt(hn[:, :, r, :], hs[:, NCH:NC, r, :], bcs(a1[:, 1, r, :]), ALU.mult)
                tt(hn2[:, :, r, :], hs[:, NCH:NC, o, :], bcs(a2[:, 1, r, :]), ALU.mult)
            tt(hn[:, :, :, :], hn[:, :, :, :], hn2[:, :, :, :], ALU.add)
            dve.tensor_tensor(hn[:, :, :, :], hn[:, :, :, :], vv[:, 0:NS, :, :], ALU.add).then_inc(hn_d, 1)
            for q in range(QP):
                if q >= 1:
                    dve.wait_ge(q_mask, 4 * q)
                cplx(dve, ch, qq[:, 0, :, :, :], *q_args(q, False), tr[:, :, :, :], ALU.subtract).then_inc(q_re, 1)
                ch(dve.tensor_tensor(de[:, :, :], dk[:, 16 * q:16 * q + 16].unsqueeze(2).broadcast_to([CH, 2 * PPQ, CH]),
                                     m.ident[0:CH, 0:CH].unsqueeze(1).broadcast_to([CH, 2 * PPQ, CH]), ALU.mult))
                dve.wait_ge(k_ev, 4 * q + 4)
                dve.tensor_tensor(km[:, :, 0:CH], km[:, :, 0:CH], de[:, :, :], ALU.add).then_inc(k_d, 1)

TT, TW = 5, T // 5

def unit(u, x):
    return x

def norm_sums_act(m, act, src, sq, rs, sq_ready, sq_used, rt_ready):
    for k in range(KT):
        if k >= 4:
            act.wait_ge(sq_used, k - 3)
        act.activation(sq[:, k % 4, :], src[:, k, :], ACT.Square).then_inc(sq_ready, 1)
    act.wait_ge(sq_used, KT)
    for h, (c0, n) in enumerate(HALVES):
        act.activation(rs[:, c0:c0 + n], m.aux[:, h, 0:n], ACT.Sqrt, bias=m.eps[:, 0:1], scale=1.0 / D).then_inc(rt_ready, 1)

def norm_sums_pe(m, pe, sq, sq_ready, sq_used):
    for k in range(KT):
        pe.wait_ge(sq_ready, k + 1)
        for h, (c0, n) in enumerate(HALVES):
            mm = pe.matmul(m.aux[:, h, 0:n], m.ones[:, :], sq[:, k % 4, c0:c0 + n], start=(k == 0), stop=(k == KT - 1))
        mm.then_inc(sq_used, 1)

def stage_d(nc, m, ins, outs):
    at, sem = m.at, m.sem
    m.top = m.free
    ot = m.ot
    f0 = m.free
    yg = at("yg", [P, 8, T], F32, off=f0 + H * T * 4)
    sq = at("sq2", [P, 4, T], F32, off=f0 + 2 * H * T * 4)
    stg = at("stg", [P, 2, T], F32, off=f0 + 2 * H * T * 4 + 4 * T * 4)
    rs = at("rs2", [P, T], F32, off=f0 + 2 * H * T * 4 + 6 * T * 4)
    bgl = at("bgl", [P, 12], F32, off=f0 + 2 * H * T * 4 + 7 * T * 4)
    sc = m.sc = at("sc", [TW, TT, 16, P], F32, off=f0)
    keysT = at("keysT", [P, 16, P], F32, off=m.free - NPG * P * 4)
    yr = at("yr", [P, 8, T], F32, off=m.x0 + (2 * KT + 8) * T * 4)
    gh = at("gh", [P, 8, T], F32R, off=m.x0); gl = at("gl", [P, 8, T], F32R, off=m.x0 + 8 * T * 4)
    sems = {n: sem("d_" + n) for n in "yin cin xin keys gel gh gl osq osum ort osc ohi olo sig mixf mixh mixl sqr squ rtr hr hhr hlr qev smm sev v stx xres".split()}
    S = lambda n: sems[n]
    with nc.Block() as block:
        @block.sync
        def _(sp):
            sp.dma_start(yr[:, :, :], m.yT[:, :, :].rearrange("a p n -> p a n")).then_inc(S("yin"), 16)
            sp.dma_start(bgl[:, 0:8], ins["b_glu"][:, :]).then_inc(S("cin"), 16)
            sp.dma_start(bgl[:, 8:9], ins["g_sub"][:, :]).then_inc(S("cin"), 16)
            sp.dma_start(keysT[:, :, :], ins["keys_t"][:, :, :]).then_inc(S("keys"), 16)
            for u in range(U_GLU, U_OUT):
                load_unit(m, sp, u + 2, u % 2)
            sp.wait_ge(m.mm_done, U_OUT + 2)
            sp.wait_ge(S("gl"), 8)
            sp.dma_start(m.xt[:, :, :], ins["x_t"][:, :, :]).then_inc(S("xin"), 16)
            with sp.Fori(0, (N_OUT + N_PQ) // 2) as i:
                for s in range(2):
                    load_unit(m, sp, i * 2 + (U_OUT + s + 2), s)
            sp.wait_ge(S("xres"), N_OUT)
            sp.dma_start(m.x2[:, :, :], m.xt[:, :, :]).then_inc(S("stx"), 16)
            sp.wait_ge(S("stx"), 16)

        @block.gpsimd
        def _(pool):
            for k in range(8):
                pool.wait_ge(S("gh"), k + 1)
                pool.tensor_tensor(gl[:, k, :], yg[:, k, :], gh[:, k, :].bitcast(F32), ALU.subtract).then_inc(S("gl"), 1)
            for u in range(U_GLU, U_OUT):
                split_lo(m, pool, u + 2, u % 2)
            with pool.Fori(0, N_OUT // 2) as i:
                for s in range(2):
                    split_lo(m, pool, i * 2 + (U_OUT + s + 2), s)
            for k in range(KT):
                pool.wait_ge(S("hhr"), k + 1)
                pool.tensor_tensor(m.hl[:, k, :], stg[:, k % 2, :], m.hh[:, k, :].bitcast(F32), ALU.subtract).then_inc(S("hlr"), 1)
            with pool.Fori(0, N_PQ // 2) as i:
                for s in range(2):
                    split_lo(m, pool, i * 2 + (U_PQ + s + 2), s)

        @block.scalar
        def _(act):
            act.wait_ge(S("yin"), 16)
            for k in range(8):
                act.activation(yg[:, k, 0:NS], yr[:, k, 0:NS], ACT.Gelu_apprx_tanh)
                act.activation(yg[:, k, NS:T].rearrange("p (n s) -> p n s", s=CL), yr[:, k, NS:T].rearrange("p (s n) -> p n s", s=CL), ACT.Gelu_apprx_tanh).then_inc(S("gel"), 1)
            for k in range(8):
                act.wait_ge(S("gel"), k + 1)
                act.activation(gh[:, k, :], yg[:, k, :], ACT.Copy).then_inc(S("gh"), 1)
            for h in range(H):
                act.activation(sq[:, h % 4, :], ot[:, h, :], ACT.Square).then_inc(S("osq"), 1) if h < 4 else None
            for h in range(H):
                act.wait_ge(S("osum"), h + 1)
                if h >= 1:
                    act.wait_ge(S("osc"), h)
                for hf, (c0, n) in enumerate(HALVES):
                    act.activation(rs[:, c0:c0 + n], m.aux[:, 2 * (h % 2) + hf, 0:n], ACT.Sqrt, bias=m.eps[:, 0:1], scale=1.0 / P).then_inc(S("ort"), 1)
                if h + 4 < H:
                    act.activation(sq[:, h % 4, :], ot[:, h + 4, :], ACT.Square).then_inc(S("osq"), 1)
                act.wait_ge(S("osc"), h + 1)
                act.activation(m.hh[:, h, :], ot[:, h, :], ACT.Copy).then_inc(S("ohi"), 1)
            for n in range(N_GLU):
                u = U_GLU + n
                act.wait_ge(m.mm_done, u + 3)
                act.wait_ge(S("cin"), 32)
                for t in range(2):
                    if n >= 1:
                        act.wait_ge(S("mixf"), 2 * n + t - 1)
                    for hf, (c0, w) in enumerate(HALVES):
                        x = act.activation(stg[:, t, c0:c0 + w], m.acc[:, t, hf, 0:w], ACT.Sigmoid, bias=bgl[:, 2 * n + t:2 * n + t + 1])
                    x.then_inc(S("sig"), 1)
                act.wait_ge(S("sig"), 2 * n + 2)
                act.sem_inc(m.acc_free, 1)
                split_hi(m, act, u + 2, u % 2, (u + 2) // 2)
                for t in range(2):
                    act.wait_ge(S("mixf"), 2 * n + t + 1)
                    act.activation(m.hh[:, 8 + 2 * n + t, :], yg[:, 2 * n + t, :], ACT.Copy).then_inc(S("mixh"), 1)
            with act.Fori(0, N_OUT // 2) as i:
                for s in range(2):
                    split_hi(m, act, i * 2 + (U_OUT + s + 2), s, i + (U_OUT // 2 + 1))
            act.wait_ge(S("xres"), N_OUT)
            norm_sums_act(m, act, m.xt, sq, rs, S("sqr"), S("squ"), S("rtr"))
            for k in range(KT):
                act.wait_ge(S("hr"), k + 1)
                act.activation(m.hh[:, k, :], stg[:, k % 2, :], ACT.Copy).then_inc(S("hhr"), 1)
            with act.Fori(0, N_PQ // 2) as i:
                for s in range(2):
                    u = i * 2 + (U_PQ + s)
                    act.wait_ge(m.mm_done, u + 3)
                    act.wait_ge(S("smm"), i * 2 + (s + 1))
                    for hf, (c0, w) in enumerate(HALVES):
                        x = act.activation(stg[:, s, c0:c0 + w], m.acc[:, s, hf, 0:w], ACT.Copy)
                    x.then_inc(S("qev"), 1)
                    act.wait_ge(S("qev"), i * 2 + (s + 1))
                    act.sem_inc(m.acc_free, 1)
                    split_hi(m, act, u + 2, s, i + (U_PQ // 2 + 1))
                    if s == 1:
                        for v in range(2):
                            act.wait_ge(S("smm"), i * 2 + (v + 3))
                            act.activation(sc[:, 0:4, ds(i * 2 + v, 1), :].rearrange("p t a n -> p (t a) n"), m.aux[0:TW, 2 * v, :].rearrange("p (t n) -> p t n", t=4), ACT.Copy)
                            act.activation(sc[:, 4, ds(i * 2 + v, 1), :].rearrange("p a n -> p (a n)"), m.aux[0:TW, 2 * v + 1, 0:P], ACT.Copy).then_inc(S("sev"), 1)

        @block.tensor
        def _(pe):
            for h in range(H):
                pe.wait_ge(S("osq"), h + 1)
                if h >= 2:
                    pe.wait_ge(S("ort"), 2 * (h - 1))
                for hf, (c0, n) in enumerate(HALVES):
                    mm = pe.matmul(m.aux[:, 2 * (h % 2) + hf, 0:n], m.ones[:, :], sq[:, h % 4, c0:c0 + n], start=True, stop=True)
                mm.then_inc(S("osum"), 1)
            pe.wait_ge(S("gl"), 8)
            for u in range(U_GLU, U_OUT):
                s = u % 2
                pe.wait_ge(m.lo_done, u + 3)
                pe.wait_ge(m.acc_free, u + 2)
                for t in range(2):
                    for hf, (c0, n) in enumerate(HALVES):
                        o = m.acc[:, t, hf, 0:n]
                        for k in range(8):
                            pe.matmul(o, m.wh[s][:, 2 * k + t, :], gh[:, k, c0:c0 + n], start=(k == 0), stop=False)
                            pe.matmul(o, m.wh[s][:, 2 * k + t, :], gl[:, k, c0:c0 + n], start=False, stop=False)
                            mm = pe.matmul(o, m.wl[s][:, 2 * k + t, :], gh[:, k, c0:c0 + n], start=False, stop=(k == 7))
                mm.then_inc(m.mm_done, 1)
            pe.wait_ge(S("olo"), H)
            pe.wait_ge(S("mixl"), 8)
            with pe.Fori(0, N_OUT // 2) as i:
                for s in range(2):
                    unit_matmuls(m, pe, i * 2 + (U_OUT + s), s, m.hh, m.hl, s)
            norm_sums_pe(m, pe, sq, S("sqr"), S("squ"))
            pe.wait_ge(S("hlr"), KT)
            pe.wait_ge(S("keys"), 16)
            with pe.Fori(0, N_PQ // 2) as i:
                for s in range(2):
                    unit_matmuls(m, pe, i * 2 + (U_PQ + s), s, m.hh, m.hl, s)
                for s in range(2):
                    pe.wait_ge(S("qev"), i * 2 + (s + 1))
                    pe.wait_ge(S("sev"), i * 2 + (s + 1))
                    for t in range(TT):
                        mm = pe.matmul(m.aux[0:TW, 2 * s + t // 4, P * (t % 4):P * (t % 4) + P], stg[:, s, TW * t:TW * t + TW],
                                       keysT[:, ds(i * 2 + s, 1), :].rearrange("p a n -> p (a n)"), start=True, stop=True)
                    mm.then_inc(S("smm"), 1)

        @block.vector
        def _(dve):
            ch = Chain(dve, S("v"))
            dve.wait_ge(S("cin"), 32)
            dve.sem_inc(S("smm"), 2)
            dve.sem_inc(S("sev"), 2)
            ch(dve.tensor_scalar(bgl[:, 9:10], bgl[:, 8:9], 1.0 - LAM0, None, ALU.mult))
            for h in range(H):
                dve.wait_ge(S("ort"), 2 * h + 2)
                ch(dve.reciprocal(rs[:, :], rs[:, :]))
                dve.wait_ge(S("osq"), h + 1)
                dve.scalar_tensor_tensor(ot[:, h, :], ot[:, h, :], bgl[:, 9:10], rs[:, :], ALU.mult, ALU.mult).then_inc(S("osc"), 1)
                dve.wait_ge(S("ohi"), h + 1)
                dve.tensor_tensor(m.hl[:, h, :], ot[:, h, :], m.hh[:, h, :].bitcast(F32), ALU.subtract).then_inc(S("olo"), 1)
            for t in range(8):
                dve.wait_ge(S("sig"), t + 1)
                dve.wait_ge(S("gl"), 8)
                dve.tensor_tensor(yg[:, t, :], yg[:, t, :], stg[:, t % 2, :], ALU.mult).then_inc(S("mixf"), 1)
                dve.wait_ge(S("mixh"), t + 1)
                dve.tensor_tensor(m.hl[:, 8 + t, :], yg[:, t, :], m.hh[:, 8 + t, :].bitcast(F32), ALU.subtract).then_inc(S("mixl"), 1)
            dve.wait_ge(S("xin"), 16)
            with dve.Fori(0, N_OUT // 2) as i:
                for s in range(2):
                    dve.wait_ge(m.mm_done, i * 2 + (U_OUT + s + 3))
                    for hf, (c0, n) in enumerate(HALVES):
                        x = m.xt[:, ds(i * 2 + s, 1), c0:c0 + n].rearrange("p a n -> p (a n)")
                        x = dve.tensor_tensor(x, x, m.acc[:, s, hf, 0:n], ALU.add)
                        if hf == 0:
                            ch_half = x
                    x.then_inc(S("xres"), 1)
                    dve.wait_ge(S("xres"), i * 2 + (s + 1))
                    dve.sem_inc(m.acc_free, 1)
            dve.wait_ge(S("rtr"), 2)
            ch(dve.reciprocal(rs[:, :], rs[:, :]))
            for k in range(KT):
                if k >= 2:
                    dve.wait_ge(S("hlr"), k - 1)
                dve.scalar_tensor_tensor(stg[:, k % 2, :], m.xt[:, k, :], m.gains[:, 1, k:k + 1], rs[:, :], ALU.mult, ALU.mult).then_inc(S("hr"), 1)

TK = 16
HK = H * TK
NB, BW = 13, T // 13
NEG = -3.0e38
GRP, NG = 4, 32

def stage_e(nc, m, ins, outs):
    at, sem = m.at, m.sem
    f0 = m.free
    at_ = lambda n, s, d=F32: at(n, s, d)
    m.top = m.x0
    sct = at("sct", [TW, 16, P]); cand = at("cand", [TW, H, TK, TK]); eq = at("eq", [TW, HK, TK])
    assert m.end <= m.x0 + KT * T * 4
    m.top = f0 - NPG * P * 4
    wk = at("wk", [TW, 2, 256]); vals = at("vals", [TW, 16, TK]); idx = at("idx", [TW, 16, TK], U32); idf = at("idf", [TW, 16, TK])
    tv = at("tv", [TW, H, TK])
    assert m.end <= f0, (m.end, f0)
    sc = m.sc
    gs = [at(f"gs{j}", [P, P, BW], F32, off=f0 + j * P * BW * 4) for j in range(2)]
    m.top = f0 + 2 * P * BW * 4
    tp = at("tp", [TW, H, TK], U32); tpa = at("tpa", [TW, H, TK], U32); pf = at("pf", [TW, HK])
    gx = at("gx", [TW, 3, HK]); sm = at("esm", [TW, 2, H]); iota = at("iota", [P, P]); gt = at("gt", [P, 3, T])
    m.top = m.x0
    at("skip", [P, 3, 2048]) if False else None
    o2 = at("o2", [P, 8, P], F32, off=m.x0); og = at("og", [P, 8, P], F32, off=m.x0 + 4096); gts = at("gts", [P, 2, 3, BW], F32, off=m.x0 + 8192)
    m.top = m.x0 + 3 * 8192
    ast = at("ast", [P, 2, T])
    assert m.end <= m.x0 + KT * T * 4
    S = {n: sem("e_" + n) for n in "cin scv gel st0 st1 exp tvd gx gtr gev v gts o2r ogr omm oev gst0 gst1 ofree".split()}
    st, gst = [S["st0"], S["st1"]], [S["gst0"], S["gst1"]]
    PA, UA = TT, 8
    PB, UB = NB, 4
    UC = N_EXP - PA * UA - PB * UB
    B0 = U_EXP_U + PA * UA
    C0 = B0 + PB * UB
    PC = UC // 2
    TPU = BW // UB
    gD, aD = m.gD, m.aD
    with nc.Block() as block:
        @block.sync
        def _(sp):
            sp.dma_start(iota[:, :], ins["iota"][:, :]).then_inc(S["cin"], 16)
            sp.sem_inc(st[0], 16); sp.sem_inc(st[1], 16); sp.sem_inc(gst[0], 16); sp.sem_inc(gst[1], 16)
            with sp.Fori(0, N_EXP // 2) as i:
                for s in range(2):
                    load_unit(m, sp, i * 2 + (U_EXP_U + s + 2), s)

        @block.gpsimd
        def _(pool):
            def los(n, first, turns):
                with pool.Fori(0, turns) as i:
                    for k in range(n):
                        split_lo(m, pool, i * n + (first + k + 2), k % 2)
            los(UA, U_EXP_U, PA)
            los(UB, B0, PB)
            los(2, C0, PC)

        @block.scalar
        def _(act):
            def take(u, s, e, row, done):
                act.wait_ge(m.mm_done, u + 3)
                act.wait_ge(st[s], row * 16 + 16)
                for hf, (c0, w) in enumerate(HALVES):
                    x = act.activation(ast[:, s, c0:c0 + w], m.acc[:, s, hf, 0:w], ACT.Gelu_apprx_tanh)
                x.then_inc(S["gel"], 1)
                act.wait_ge(S["gel"], done)
                act.sem_inc(m.acc_free, 1)
                act.dma_start(aD[ds(e, 1), :, :].rearrange("a p n -> (a p) n"), ast[:, s, :]).then_inc(st[s], 16)

            with act.Fori(0, PA) as i:
                act.wait_ge(S["gx"], i)
                act.activation(sct[:, :, :], sc[:, ds(i, 1), :, :].rearrange("p a b c -> p (a b) c"), ACT.Copy).then_inc(S["scv"], 1)
                for n in range(UA):
                    u = i * UA + (U_EXP_U + n)
                    if n == UA - 1:
                        act.wait_ge(S["tvd"], i + 1)
                        act.activation(tv[:, :, :], tv[:, :, :], ACT.Exp).then_inc(S["exp"], 1)
                    take(u, n % 2, i * UA + n, i * (UA // 2) + n // 2, i * UA + (n + 1))
                    split_hi(m, act, u + 2, n % 2, i * (UA // 2) + (U_EXP_U // 2 + n // 2 + 1))
                act.wait_ge(S["gtr"], i + 1)
                act.activation(gt[:, :, :].rearrange("p x (t n) -> p t x n", t=TT)[:, ds(i, 1), :, :].rearrange("p a x n -> p (a x) n"),
                               m.aux[:, 0, 0:3 * TW].rearrange("p (x n) -> p x n", x=3), ACT.Copy).then_inc(S["gev"], 1)
            with act.Fori(0, PB) as i:
                act.wait_ge(S["gev"], TT)
                act.wait_ge(S["ofree"], i)
                act.activation(gts[:, 0, :, :], gt[:, :, :].rearrange("p x (t n) -> p t x n", t=NB)[:, ds(i, 1), :, :].rearrange("p a x n -> p (a x) n"), ACT.Copy).then_inc(S["gts"], 1)
                for n in range(UB):
                    u = i * UB + (B0 + n)
                    take(u, n % 2, i * UB + (PA * UA + n), i * (UB // 2) + (PA * UA // 2 + n // 2), i * UB + (PA * UA + n + 1))
                    split_hi(m, act, u + 2, n % 2, i * (UB // 2) + (B0 // 2 + n // 2 + 1))
                act.wait_ge(S["oev"], i * (BW // 4) + BW // 4)
                act.dma_start(gD[ds(i, 1), :, :, :].rearrange("a p e n -> (a p) (e n)"), gs[0][:, :, :].rearrange("p e n -> p (e n)")).then_inc(gst[0], 16)
            with act.Fori(0, PC) as i:
                for n in range(2):
                    u = i * 2 + (C0 + n)
                    take(u, n, i * 2 + (C0 - U_EXP_U + n), i + ((C0 - U_EXP_U) // 2), i * 2 + (C0 - U_EXP_U + n + 1))
                    split_hi(m, act, u + 2, n, i + (C0 // 2 + 1))
            for s in range(2):
                act.wait_ge(st[s], 16 + 16 * N_EXP // 2)
            act.wait_ge(gst[0], 16 + 16 * NB)

        @block.tensor
        def _(pe):
            with pe.Fori(0, PA) as i:
                for n in range(UA):
                    unit_matmuls(m, pe, i * UA + (U_EXP_U + n), n % 2, m.hh, m.hl, n % 2)
                pe.wait_ge(S["gx"], i + 1)
                pe.wait_ge(S["gev"], i)
                for x in range(3):
                    mm = pe.transpose(m.aux[:, 0, TW * x:TW * x + TW], gx[:, x, :], m.ident[0:TW, 0:TW])
                mm.then_inc(S["gtr"], 1)
            with pe.Fori(0, PB) as i:
                for n in range(UB):
                    unit_matmuls(m, pe, i * UB + (B0 + n), n % 2, m.hh, m.hl, n % 2)
                    for k in range(TPU):
                        t = n * TPU + k
                        pe.wait_ge(S["o2r"], i * BW + (t + 1))
                        pe.wait_ge(S["ogr"], i * BW + (t + 1))
                        if t % 4 == 0:
                            pe.wait_ge(S["oev"], i * (BW // 4) + (t // 4 - 1)) if t >= 4 else None
                            if t < 4:
                                pe.wait_ge(S["oev"], i * (BW // 4))
                        mm = pe.matmul(m.aux[:, 1 + (t // 4) % 2, P * (t % 4):P * (t % 4) + P], o2[:, t % 8, :], og[:, t % 8, :], start=True, stop=True)
                        mm.then_inc(S["omm"], 1)
            with pe.Fori(0, PC) as i:
                for n in range(2):
                    unit_matmuls(m, pe, i * 2 + (C0 + n), n, m.hh, m.hl, n)

        @block.vector
        def _(dve):
            ch = Chain(dve, S["v"])
            dve.wait_ge(S["cin"], 16)
            with dve.Fori(0, PA) as i:
                ch = Chain(dve, S["v"])
                dve.wait_ge(S["scv"], i + 1)
                ch(dve.memset(sm[:, :, :], 0.0))
                for c in range(16):
                    w = wk[:, c % 2, 0:P]
                    ch(dve.max(vals[:, c, 0:8], sct[:, c, :]))
                    ch(dve.max_index(idx[:, c, 0:8], vals[:, c, 0:8], sct[:, c, :]))
                    ch(dve.match_replace(w, vals[:, c, 0:8], sct[:, c, :], NEG))
                    ch(dve.max(vals[:, c, 8:16], w))
                    ch(dve.max_index(idx[:, c, 8:16], vals[:, c, 8:16], w))
                ch(dve.tensor_copy(idf[:, :, :], idx[:, :, :]))
                v = vals[:, :, :].rearrange("p (h c) k -> p h c k", c=2)
                ch(dve.tensor_tensor(cand[:, :, :, :], v[:, :, 0, :].unsqueeze(3).broadcast_to([TW, H, TK, TK]), v[:, :, 1, :].unsqueeze(2).broadcast_to([TW, H, TK, TK]), ALU.add))
                for h in range(H):
                    cd = cand[:, h, :, :].rearrange("p a b -> p (a b)")
                    w = wk[:, h % 2, :]
                    ch(dve.max(tv[:, h, 0:8], cd))
                    ch(dve.max_index(tp[:, h, 0:8], tv[:, h, 0:8], cd))
                    ch(dve.match_replace(w, tv[:, h, 0:8], cd, NEG))
                    ch(dve.max(tv[:, h, 8:16], w))
                    ch(dve.max_index(tp[:, h, 8:16], tv[:, h, 8:16], w))
                ch(dve.tensor_copy(sm[:, 0, :], tv[:, :, 0]))
                dve.tensor_tensor(tv[:, :, :], tv[:, :, :], sm[:, 0, :].unsqueeze(2).broadcast_to([TW, H, TK]), ALU.subtract).then_inc(S["tvd"], 1)
                il = idf[:, :, :].rearrange("p (h c) k -> p h c k", c=2)
                if True:
                    dve.wait_ge(S["gtr"], i)
                for c in range(2):
                    if c == 0:
                        ch(dve.tensor_scalar(tpa[:, :, :], tp[:, :, :], 4, None, ALU.logical_shift_right))
                    else:
                        ch(dve.tensor_scalar(tpa[:, :, :], tp[:, :, :], 15, None, ALU.bitwise_and))
                    ch(dve.tensor_copy(pf[:, :], tpa[:, :, :].rearrange("p h k -> p (h k)")))
                    ch(dve.tensor_tensor(eq[:, :, :], pf[:, :].unsqueeze(2).broadcast_to([TW, HK, TK]), iota[0:TW, 0:TK].unsqueeze(1).broadcast_to([TW, HK, TK]), ALU.is_equal))
                    e4 = eq[:, :, :].rearrange("p (h k) j -> p h k j", h=H)
                    ch(dve.tensor_tensor(e4, e4, il[:, :, c, :].unsqueeze(2).broadcast_to([TW, H, TK, TK]), ALU.mult))
                    ch(dve.tensor_reduce(gx[:, 1 + c, :], eq[:, :, :], AX.X, ALU.add))
                dve.wait_ge(S["exp"], i + 1)
                ch(dve.tensor_reduce(sm[:, 0, :], tv[:, :, :], AX.X, ALU.add))
                ch(dve.reciprocal(sm[:, 1, :], sm[:, 0, :]))
                ch(dve.tensor_tensor(gx[:, 0, :].rearrange("p (h k) -> p h k", h=H), tv[:, :, :], sm[:, 1, :].unsqueeze(2).broadcast_to([TW, H, TK]), ALU.mult))
                dve.sem_inc(S["gx"], 1)
                dve.sem_clear(S["v"])
            with dve.Fori(0, PB) as i:
                dve.wait_ge(S["gts"], i + 1)
                def spread(g):
                    dve.wait_ge(S["omm"], i * BW + (4 * g + 4))
                    if g == 0:
                        dve.wait_ge(gst[0], i * 16 + 16)
                    dve.tensor_copy(gs[0][:, :, 4 * g:4 * g + 4].rearrange("p e t -> p t e"), m.aux[:, 1 + g % 2, :].rearrange("p (t e) -> p t e", t=4)).then_inc(S["oev"], 1)
                for t in range(BW):
                    if t >= 8:
                        if t % 4 == 0:
                            dve.wait_ge(S["omm"], i * BW + (t - 4))
                    else:
                        dve.wait_ge(S["omm"], i * BW)
                    dve.tensor_scalar(o2[:, t % 8, :], iota[:, :], gts[:, 0, 2, t:t + 1], None, ALU.is_equal).then_inc(S["o2r"], 1)
                    dve.tensor_scalar(og[:, t % 8, :], iota[:, :], gts[:, 0, 1, t:t + 1], gts[:, 0, 0, t:t + 1], ALU.is_equal, ALU.mult).then_inc(S["ogr"], 1)
                    if t % 4 == 3 and t >= 7:
                        spread(t // 4 - 1)
                spread(BW // 4 - 1)
                dve.wait_ge(S["ogr"], i * BW + BW)
                dve.sem_inc(S["ofree"], 1)

def stage_f(nc, m, ins, outs):
    at, sem = m.at, m.sem
    b = m.x0 + KT * T * 4
    SZ = GRP * T * 4
    a4 = [at(f"a4{s}", [P, GRP, T], F32, off=b + s * SZ) for s in range(2)]
    g4 = [at(f"g4{s}", [P, NB, GRP, BW], F32, off=b + (2 + s) * SZ) for s in range(2)]
    vh = [at(f"vh{s}", [P, GRP, T], F32R, off=b + (4 + s) * SZ) for s in range(2)]
    vl = [at(f"vl{s}", [P, GRP, T], F32R, off=b + (6 + s) * SZ) for s in range(2)]
    m.top = m.free
    sq = at("sq3", [P, 4, T]); rs = at("rs3", [P, T])
    S = {n: sem("g_" + n) for n in "xin ain0 ain1 gin0 gin1 w wh wl mmd macc v sqr squ rtr xf st".split()}
    ain, gin = [S["ain0"], S["ain1"]], [S["gin0"], S["gin1"]]
    with nc.Block() as block:
        def turn_loads(sp, i, last):
            for gg in range(2):
                g = i * 2 + gg
                if last is not None:
                    pass
                for n in range(4):
                    if last and gg == 1 and n >= 2:
                        continue
                    load_unit(m, sp, i * 8 + (U_EXP_V + 4 * gg + n + 2), n % 2)
                    if n == 1 and not (last and gg == 1):
                        loads_ag(sp, g + 1, 1 - gg, i + (1 if gg == 1 else 0))

        def loads_ag(sp, g, s, pair):
            sp.wait_ge(S["mmd"], g)
            sp.dma_start(a4[s][:, :, :], m.aD[ds(g * GRP, GRP), :, :].rearrange("e p n -> p e n")).then_inc(ain[s], 16)
            sp.dma_start(g4[s][:, :, :, :].rearrange("p b e n -> p b (e n)"), m.gD[:, :, ds(g * GRP, GRP), :].rearrange("b p e n -> p b (e n)")).then_inc(gin[s], 16)

        @block.sync
        def _(sp):
            sp.dma_start(m.xt[:, :, :], m.x2[:, :, :]).then_inc(S["xin"], 16)
            sp.sem_inc(S["mmd"], 1)
            sp.dma_start(a4[0][:, :, :], m.aD[0:GRP, :, :].rearrange("e p n -> p e n")).then_inc(ain[0], 16)
            sp.dma_start(g4[0][:, :, :, :].rearrange("p b e n -> p b (e n)"), m.gD[:, :, 0:GRP, :].rearrange("b p e n -> p b (e n)")).then_inc(gin[0], 16)
            with sp.Fori(0, NG // 2 - 1) as i:
                turn_loads(sp, i, False)
            turn_loads(sp, NG // 2 - 1, True)
            for k in range(KT):
                sp.wait_ge(S["xf"], k + 1)
                sp.dma_start(outs["y_t"][:, k, :], m.xt[:, k, :]).then_inc(S["st"], 16)
            sp.wait_ge(S["st"], 16 * KT)

        @block.gpsimd
        def _(pool):
            def turn(i, last):
                for n in range(6 if last else 8):
                    split_lo(m, pool, i * 8 + (U_EXP_V + n + 2), n % 2)
            with pool.Fori(0, NG // 2 - 1) as i:
                turn(i, False)
            turn(NG // 2 - 1, True)

        @block.scalar
        def _(act):
            def w_hi(g, s):
                act.wait_ge(S["w"], g + 1)
                act.wait_ge(S["mmd"], g)
                act.activation(vh[s][:, :, :], a4[s][:, :, :], ACT.Copy).then_inc(S["wh"], 1)
            w_hi(0, 0)
            def turn(i, last):
                for gg in range(2):
                    if not (last and gg == 1):
                        w_hi(i * 2 + (gg + 1), 1 - gg)
                    for n in range(4):
                        if last and gg == 1 and n >= 2:
                            continue
                        split_hi(m, act, i * 8 + (U_EXP_V + 4 * gg + n + 2), n % 2, i * 4 + (U_EXP_V // 2 + 2 * gg + n // 2 + 1))
            with act.Fori(0, NG // 2 - 1) as i:
                turn(i, False)
            turn(NG // 2 - 1, True)
            act.wait_ge(S["macc"], 2 + 16 * NG)
            norm_sums_act(m, act, m.xt, sq, rs, S["sqr"], S["squ"], S["rtr"])

        @block.tensor
        def _(pe):
            def turn(i):
                for gg in range(2):
                    g = i * 2 + gg
                    pe.wait_ge(S["wl"], g + 1)
                    for n in range(4):
                        u = i * 8 + (U_EXP_V + 4 * gg + n)
                        s = n % 2
                        pe.wait_ge(m.lo_done, u + 3)
                        for d in range(4):
                            r = i * 32 + (16 * gg + 4 * n + d)
                            pe.wait_ge(S["macc"], r + 1)
                            for hf, (c0, w) in enumerate(HALVES):
                                o = m.acc[:, d % 2, hf, 0:w]
                                for e in range(GRP):
                                    pe.matmul(o, m.wh[s][:, 4 * e + d, :], vh[gg][:, e, c0:c0 + w], start=(e == 0), stop=False)
                                    pe.matmul(o, m.wh[s][:, 4 * e + d, :], vl[gg][:, e, c0:c0 + w], start=False, stop=False)
                                    mm = pe.matmul(o, m.wl[s][:, 4 * e + d, :], vh[gg][:, e, c0:c0 + w], start=False, stop=(e == GRP - 1))
                            mm.then_inc(S["v"], 1)
                        pe.wait_ge(S["v"], i * 32 + (16 * gg + 4 * n + 4))
                        pe.sem_inc(m.mm_done, 1)
                    pe.sem_inc(S["mmd"], 1)
            with pe.Fori(0, NG // 2) as i:
                turn(i)
            norm_sums_pe(m, pe, sq, S["sqr"], S["squ"])

        @block.vector
        def _(dve):
            dve.sem_inc(S["macc"], 2)
            def weigh(g, s, pair):
                dve.wait_ge(ain[s], pair * 16 + 16)
                dve.wait_ge(gin[s], pair * 16 + 16)
                a = a4[s][:, :, :].rearrange("p e (b n) -> p e b n", b=NB)
                dve.tensor_tensor(a, a, g4[s][:, :, :, :].rearrange("p b e n -> p e b n"), ALU.mult).then_inc(S["w"], 1)
            def low(g, s):
                dve.wait_ge(S["wh"], g + 1)
                dve.tensor_tensor(vl[s][:, :, :], a4[s][:, :, :], vh[s][:, :, :].bitcast(F32), ALU.subtract).then_inc(S["wl"], 1)
            weigh(0, 0, 0)
            low(0, 0)
            dve.wait_ge(S["xin"], 16)
            def turn(i, last):
                for gg in range(2):
                    more = not (last and gg == 1)
                    for n in range(4):
                        for d in range(4):
                            r = i * 32 + (16 * gg + 4 * n + d)
                            dve.wait_ge(S["v"], r + 1)
                            for hf, (c0, w) in enumerate(HALVES):
                                x = m.xt[:, 4 * n + d, c0:c0 + w]
                                x = dve.tensor_tensor(x, x, m.acc[:, d % 2, hf, 0:w], ALU.add)
                            x.then_inc(S["macc"], 1)
                        if n == 1 and more:
                            weigh(i * 2 + (gg + 1), 1 - gg, i + (1 if gg == 1 else 0))
                        if n == 2 and more:
                            low(i * 2 + (gg + 1), 1 - gg)
            with dve.Fori(0, NG // 2 - 1) as i:
                turn(i, False)
            turn(NG // 2 - 1, True)
            dve.wait_ge(S["rtr"], 2)
            dve.reciprocal(rs[:, :], rs[:, :]).then_inc(S["v"], 1)
            dve.wait_ge(S["v"], 16 * NG + 1)
            for k in range(KT):
                dve.wait_ge(S["squ"], KT)
                dve.scalar_tensor_tensor(m.xt[:, k, :], m.xt[:, k, :], m.gains[:, 2, k:k + 1], rs[:, :], ALU.mult, ALU.mult).then_inc(S["xf"], 1)


def program(nc, ins, outs):
    with ExitStack() as ctx:
        m = common(nc, ctx, ins, outs)
        dram = lambda n, s: nc.dram_tensor(n, s, F32).ap()
        m.qT, m.uT, m.yT = (dram(n, [8, P, T]) for n in ("q_rows", "u_rows", "y_rows"))
        m.kT, m.vT = outs["k_t"], outs["v_t"]
        m.x2 = dram("x_mid", [P, KT, T])
        m.aD = dram("expert_acts", [P, P, T])
        m.gD = dram("expert_gates", [NB, P, P, BW])
        for stage in (stage_a, stage_b1, stage_b2, stage_s5, stage_d, stage_e, stage_f):
            own = []

            def new(name):
                own.append(nc.alloc_semaphore(name))
                return own[-1]

            m.sem = new
            stage(nc, m, ins, outs)
            nc.clear_and_free_semaphores(own)
            nc.all_engine_barrier()


def _units(w, width):
    k, n = w.shape
    return w.reshape(k // P, P, n // width, width).transpose(2, 1, 0, 3).reshape(n // width, P, -1)


def _states(a):
    rest = a.shape[2:]
    return a.reshape(GP, 2, NST, *rest).transpose(1, 2, 0, *range(3, 3 + len(rest))).reshape(P, GP, *rest)


def _cols(a):
    return a.reshape(-1, P).T


def _constants():
    c = {"ident": np.eye(P), "ones": np.ones((P, P)), "eps": np.full((P, 1), EPS), "iota": np.tile(np.arange(P), (P, 1))}
    rot = np.zeros((P, P))
    for b in (0, 64):
        for j in range(32):
            rot[b + 32 + j, b + j], rot[b + j, b + 32 + j] = -1, 1
    c["rot"] = rot
    f = np.float32
    inv = f(1.0) / (f(10000.0) ** (np.arange(32, dtype=f) * f(2) / f(64)))
    pos = np.concatenate([np.full(NS, PAST), np.arange(NT)]).astype(f)
    ang = (pos[None, :] * np.tile(inv, 4)[:, None]).astype(f)
    c["cos_t"], c["sin_t"] = np.cos(ang), np.sin(ang)
    c["dmask"] = np.concatenate([np.eye(64), np.eye(64)])
    c["cmask"] = np.kron(np.eye(2), np.ones((64, 1)))
    c["cmask4"] = np.concatenate([c["cmask"], -c["cmask"]], 1)
    c["causal"] = np.where(np.arange(P)[:, None] >= np.arange(P)[None, :], 0, -1e30)
    return {n: np.ascontiguousarray(a, dtype=f) for n, a in c.items()}


_OUTS = {"k_t": (8, P, T), "v_t": (8, P, T), "ssm_prompt": (P, 2, GP), "ssm_sample": (P, NS, 2, GP), "y_t": (P, KT, T)}


def kernel(x_prompt, x_sample, cache_k, cache_v, state_ssm_re, state_ssm_im, page_table,
           g_mix, w_in, lambda_q1, lambda_k1, lambda_q2, lambda_k2, g_sub,
           ssm_a_re, ssm_a_im, ssm_log_dt, ssm_b_re, ssm_b_im, ssm_c_re, ssm_c_im, ssm_d,
           w_glu, b_glu, w_out, g_ffn, peer_w_q, peer_sub_keys, peer_u, peer_v, g_final):
    import concourse.bacc as _bacc
    from concourse.bass_utils import run_bass_kernel_spmd as _run

    order = list(range(8)) + [8 + 8 * j + n for n in range(8) for j in range(3)]
    experts = peer_u[0].reshape(P, P, KT, P).transpose(0, 3, 2, 1).reshape(P, P, D)
    values = peer_v[0].reshape(NG, GRP, P, 4, 512).transpose(0, 3, 2, 1, 4).reshape(P, P, D)
    arrays = {
        "x_t": np.concatenate([x_sample[:, 0], x_prompt[0]]).T.reshape(KT, P, T).transpose(1, 0, 2),
        "gains": np.stack([_cols(g_mix[0]), _cols(g_ffn[0]), _cols(g_final)], 1),
        "units": np.concatenate([_units(w_in[0], P)[order], _units(w_glu[0], 2 * P), _units(w_out[0], P), _units(peer_w_q[0], P), experts, values]),
        "page_table": page_table.reshape(1, P),
        "cache_k": cache_k[0].reshape(-1, PAGE, H * P), "cache_v": cache_v[0].reshape(-1, PAGE, H * P),
        "lambdas": np.stack([lambda_q1[0], lambda_k1[0], lambda_q2[0], lambda_k2[0]]),
        "a_re": _states(ssm_a_re[0]), "a_im": _states(ssm_a_im[0]),
        "log_dt": _states(np.repeat(ssm_log_dt[0][:, None], NST, 1)),
        "b_re": _states(ssm_b_re[0]), "b_im": _states(ssm_b_im[0]),
        "c_re": _states(ssm_c_re[0].transpose(0, 2, 1)), "c_im": _states(ssm_c_im[0].transpose(0, 2, 1)),
        "h0_re": _states(state_ssm_re[0].transpose(1, 2, 0)).transpose(0, 2, 1),
        "h0_im": _states(state_ssm_im[0].transpose(1, 2, 0)).transpose(0, 2, 1),
        "d_t": ssm_d[0].T, "b_glu": _cols(b_glu[0]), "g_sub": g_sub[0].reshape(P, 1),
        "keys_t": peer_sub_keys[0].reshape(16, P, P).transpose(2, 0, 1),
        **_constants(),
    }
    arrays = {n: np.ascontiguousarray(a) for n, a in arrays.items()}
    nc = _bacc.Bacc("TRN2", target_bir_lowering=False, num_devices=1)
    ins = {n: nc.dram_tensor(n, a.shape, mybir.dt.from_np(a.dtype), kind="ExternalInput").ap() for n, a in arrays.items()}
    outs = {n: nc.dram_tensor(n, s, F32, kind="ExternalOutput").ap() for n, s in _OUTS.items()}
    program(nc, ins, outs)
    r = _run(nc, [arrays], core_ids=[0]).results[0]

    y = r["y_t"].transpose(2, 1, 0).reshape(T, D)
    k, v = (r[n].transpose(2, 0, 1) for n in ("k_t", "v_t"))
    hp = r["ssm_prompt"].reshape(2, NST, 2, GP).transpose(2, 3, 0, 1).reshape(2, 1, 1, G, NST)
    hs = r["ssm_sample"].reshape(2, NST, NS, 2, GP).transpose(3, 2, 4, 0, 1).reshape(2, 1, NS, G, NST)
    c = np.ascontiguousarray
    return (c(y[None, NS:]), c(y[:NS, None]), c(k[None, None, NS:]), c(v[None, None, NS:]), c(hp[0]), c(hp[1]),
            c(k[None, :NS, None]), c(v[None, :NS, None]), c(hs[0]), c(hs[1]))
```

```python
from contextlib import ExitStack

import math
import numpy as np

import concourse.bass as bass
from concourse import mybir

F32 = mybir.dt.float32
F32R = mybir.dt.float32r
I32 = mybir.dt.int32
U32 = mybir.dt.uint32
ALU = mybir.AluOpType
ACT = mybir.ActivationFunctionType
AX = mybir.AxisListType
ds = bass.ds

P = 128
D = 2048
KT = D // P
NS, NT = 8, 512
T = NS + NT
HALVES = ((0, 264), (264, 256))
H = 8
PAST, PAGE = 2048, 128
NPG = PAST // PAGE
N_IN, N_GLU, N_OUT, N_PQ, N_EXP = 32, 4, 16, 16, 128
U_GLU = N_IN
U_OUT = U_GLU + N_GLU
U_PQ = U_OUT + N_OUT
U_EXP_U = U_PQ + N_PQ
U_EXP_V = U_EXP_U + N_EXP
N_UNITS = U_EXP_V + N_EXP
EPS = 1e-6
G = 64
GP = G // 2
CH, NST = 16, 64
CL = 8
NCH = NT // CL
LAM0 = 0.2


class Chain:

    def __init__(self, eng, sem):
        self.eng, self.sem, self.base, self.n = eng, sem, 0, 0

    def __call__(self, ins):
        self.n += 1
        ins.then_inc(self.sem, 1)
        self.eng.wait_ge(self.sem, self.base + self.n)

    def enter(self, i, per):
        self.outer, self.per = self.base + self.n, per
        self.base, self.n = self.outer + i * per, 0

    def leave(self, turns):
        assert self.n == self.per, (self.n, self.per)
        self.base, self.n = self.outer + turns * self.per, 0


def common(nc, ctx, ins, outs):
    class K: pass
    m = K()
    base = (nc.sbuf_base + 63) // 64 * 64
    m.top = base
    def at(name, shape, dt=F32, off=None):
        size = int(np.prod(shape[1:])) * 4
        size = (size + 31) // 32 * 32
        if off is None:
            off = m.top = (m.top + 31) // 32 * 32
            m.top += size
        assert off + size <= nc.sbuf_usable_end, (name, off, size, nc.sbuf_usable_end)
        t = nc.alloc_sbuf_tensor_at(name, shape, dt, offset=off)
        m.end = off + size
        return t
    m.at = at
    m.sem = lambda n: ctx.enter_context(nc.semaphore(n))
    m.ident = at("ident", [P, P]); m.ones = at("ones", [P, P]); m.rot = at("rot", [P, P])
    m.gains = at("gains", [P, 3, KT]); m.eps = at("eps", [P, 1]); m.pages = at("pages", [1, P], I32); m.lam = at("lam", [P, 8])
    m.qs = at("qs", [P, H, NS])
    m.x0 = m.top
    m.xt = at("xt", [P, KT, T]); m.hh = at("hh", [P, KT, T], F32R); m.hl = at("hl", [P, KT, T], F32R)
    m.raw = [at(f"raw{s}", [P, KT, P]) for s in range(2)]
    m.wh = [at(f"wh{s}", [P, KT, P], F32R) for s in range(2)]
    m.wl = [at(f"wl{s}", [P, KT, P], F32R) for s in range(2)]
    m.scd = at("scd", [P, NPG, P])
    m.free = m.top
    m.acc = ctx.enter_context(nc.psum_tensor("acc", [P, 2, 2, 512], F32))
    m.aux = ctx.enter_context(nc.psum_tensor("aux", [P, 4, 512], F32))
    m.raw_in = [m.sem(f"raw_in{s}") for s in range(2)]
    m.hi_done = m.sem("hi_done"); m.lo_done = m.sem("lo_done"); m.mm_done = m.sem("mm_done"); m.acc_free = m.sem("acc_free")
    m.units = ins["units"]
    return m

def load_unit(m, sp, u, s):
    sp.wait_ge(m.lo_done, u + 1)
    sp.dma_start(m.raw[s][:, :, :].rearrange("p k n -> p (k n)"), m.units[ds(u, 1), :, :].rearrange("a p n -> (a p) n")).then_inc(m.raw_in[s], 16)

def split_hi(m, act, u, s, pair, used=None):
    act.wait_ge(m.raw_in[s], pair * 16 + 16)
    act.wait_ge(*(used or (m.mm_done, u + 1)))
    act.activation(m.wh[s][:, :, :], m.raw[s][:, :, :], ACT.Copy).then_inc(m.hi_done, 1)

def split_lo(m, pool, u, s):
    pool.wait_ge(m.hi_done, u + 1)
    pool.tensor_tensor(m.wl[s][:, :, :], m.raw[s][:, :, :], m.wh[s][:, :, :].bitcast(F32), ALU.subtract).then_inc(m.lo_done, 1)

def unit_matmuls(m, pe, u, s, rhs_hi, rhs_lo, acc_slot, k_range=range(KT), first=True, wait_k=None, out=None):
    pe.wait_ge(m.lo_done, u + 3)
    pe.wait_ge(m.acc_free, u + 1)
    if wait_k is None:
        order = [(h, k) for h in range(2) for k in k_range]
    else:
        order = [(h, k) for k in k_range for h in range(2)]
    k_range = list(k_range)
    for h, k in order:
        if wait_k is not None and h == 0:
            pe.wait_ge(wait_k, k + 1)
        c0, n = HALVES[h]
        o = m.acc[:, acc_slot, h, 0:n]
        pe.matmul(o, m.wh[s][:, k, :], rhs_hi[:, k, c0:c0 + n], start=(k == k_range[0]), stop=False)
        pe.matmul(o, m.wh[s][:, k, :], rhs_lo[:, k, c0:c0 + n], start=False, stop=False)
        mm = pe.matmul(o, m.wl[s][:, k, :], rhs_hi[:, k, c0:c0 + n], start=False, stop=(k == k_range[-1]))
    mm.then_inc(m.mm_done, 1)

def halves_copy(eng_op, out, m, slot):
    for h, (c0, n) in enumerate(HALVES):
        ins = eng_op(out[:, c0:c0 + n], m.acc[:, slot, h, 0:n])
    return ins

def stage_a(nc, m, ins, outs):
    at, sem = m.at, m.sem
    m.top = m.free
    cosT = at("cosT", [P, T]); sinT = at("sinT", [P, T])
    zst = [at(f"zst{j}", [P, T]) for j in range(3)]
    zo = [at(f"zo{j}", [P, T]) for j in range(2)]
    t1 = at("t1", [P, T]); t2 = at("t2", [P, T])
    kring = at("kring", [P, 4, 1024]); sq = at("sq", [P, 4, T], F32, off=m.top - 4 * 4096)
    prod = [at(f"prod{j}", [P, 1024]) for j in range(3)]; rs = at("rs", [P, T])
    qb = at("qb", [P, NS, 1024], F32, off=m.x0)
    c_in, x_in = sem("c_in"), [sem(f"x_in{j}") for j in range(4)]
    sq_ready, sq_used = sem("sq_ready"), sem("sq_used")
    rt_ready, h_ready, hh_ready, hl_ready = sem("rt_ready"), sem("h_ready"), sem("hh_ready"), sem("hl_ready")
    z_ready = sem("z_ready")
    rope_done, rot_ready, rot_free = sem("rope_done"), sem("rot_ready"), sem("rot_free")
    st_zo = [sem(f"st_zo{j}") for j in range(2)]; st_v, st_u, st_k = sem("st_v"), sem("st_u"), sem("st_k")
    qs_done, qb_mm, qb_ready = sem("qs_done"), sem("qb_mm"), sem("qb_ready")
    kp_in, kv_used, kg_used = [sem(f"kp_in{j}") for j in range(4)], sem("kv_used"), sem("kg_used")
    scored, turn_taken = sem("scored"), sem("turn_taken")
    s_v = sem("s_v")
    qT, kT, vT, uT = m.qT, m.kT, m.vT, m.uT
    keys = ins["cache_k"]
    PQ = 4
    PM = 4
    with nc.Block() as block:
        @block.sync
        def _(sp):
            for j in range(4):
                sp.dma_start(m.xt[:, 4 * j:4 * j + 4, :], ins["x_t"][:, 4 * j:4 * j + 4, :]).then_inc(x_in[j], 16)
            for a, b in ((m.ident, "ident"), (m.ones, "ones"), (m.rot, "rot"), (cosT, "cos_t"), (sinT, "sin_t"), (m.gains, "gains"), (m.pages, "page_table"), (m.eps, "eps")):
                sp.dma_start(a[:], ins[b][:]).then_inc(c_in, 16)
            for u in range(2):
                load_unit(m, sp, u, u)
            with sp.Fori(0, PQ) as i:
                for s in range(2):
                    load_unit(m, sp, i * 2 + (s + 2), s)
            def turn(i, last):
                for n in range(6):
                    if not (last and n >= 4):
                        load_unit(m, sp, i * 6 + (8 + n + 2), n % 2)
                    for j in range(32 * n // 6, 32 * (n + 1) // 6):
                        page = sp.value_load(m.pages[0:1, ds(i * 32 + j, 1)], min_val=0, max_val=keys.shape[0] - 1)
                        if j % 4 == 3:
                            sp.wait_ge(kg_used, i * 8 + (j // 4 + 1))
                        else:
                            sp.wait_ge(kv_used, i * 24 + (3 * (j // 4) + j % 4 + 1))
                        sp.dma_start(kring[:, j % 4, :], keys[ds(page, 1), :, :].rearrange("a p n -> (a p) n")).then_inc(kp_in[j % 4], 16)

            with sp.Fori(0, PM - 1) as i:
                turn(i, False)
            turn(PM - 1, True)

        @block.scalar
        def _(act):
            act.wait_ge(c_in, 16 * 8)
            for k in range(KT):
                if k % 4 == 0:
                    act.wait_ge(x_in[k // 4], 16)
                if k >= 4:
                    act.wait_ge(sq_used, k - 3)
                act.activation(sq[:, k % 4, :], m.xt[:, k, :], ACT.Square).then_inc(sq_ready, 1)
            act.wait_ge(sq_used, KT)
            for h, (c0, n) in enumerate(HALVES):
                r = act.activation(rs[:, c0:c0 + n], m.aux[:, h, 0:n], ACT.Sqrt, bias=m.eps[:, 0:1], scale=1.0 / D)
                r.then_inc(rt_ready, 1)
            for k in range(KT):
                act.wait_ge(h_ready, k + 1)
                act.activation(m.hh[:, k, :], m.xt[:, k, :], ACT.Copy).then_inc(hh_ready, 1)
            for u in range(2):
                split_hi(m, act, u, u, 0)

            def evac(u, slot, dst, permuted=False):
                act.wait_ge(m.mm_done, u + 3)
                if not permuted:
                    act.activation(dst[:, 0:264], m.acc[:, slot, 0, 0:264], ACT.Copy).then_inc(z_ready, 1)
                    act.activation(dst[:, 264:520], m.acc[:, slot, 1, 0:256], ACT.Copy).then_inc(m.acc_free, 1)
                else:
                    act.activation(dst[:, 0:8], m.acc[:, slot, 0, 0:8], ACT.Copy)
                    v = dst[:, 8:520].rearrange("p (s n) -> p n s", s=CL)
                    act.activation(v[:, 0:32, :], m.acc[:, slot, 0, 8:264].rearrange("p (n s) -> p n s", s=CL), ACT.Copy).then_inc(z_ready, 1)
                    act.activation(v[:, 32:64, :], m.acc[:, slot, 1, 0:256].rearrange("p (n s) -> p n s", s=CL), ACT.Copy).then_inc(m.acc_free, 1)

            with act.Fori(0, PQ) as i:
                for s in range(2):
                    u = i * 2 + s
                    act.wait_ge(rope_done, u + 1)
                    evac(u, s, zst[s])
                    split_hi(m, act, u + 2, s, i + 1)
                for s in range(2):
                    act.wait_ge(rope_done, i * 2 + (s + 3))
                    act.dma_start(qT[ds(i * 2 + s, 1), :, :].rearrange("a p n -> (a p) n"), zo[s][:, :]).then_inc(st_zo[s], 16)
            for b in range(NS):
                for g in range(2):
                    act.wait_ge(qb_mm, 2 * b + g + 1)
                    act.activation(qb[:, b, 512 * g:512 * g + 512], m.aux[:, 2 + g, :], ACT.Copy).then_inc(qb_ready, 1)
            def turn(i, last):
                for n in range(6):
                    u = i * 6 + (8 + n)
                    kind, half = n % 3, n // 3
                    if kind == 0:
                        act.wait_ge(rope_done, i * 2 + (half + 8 + 2))
                    elif kind == 1:
                        act.wait_ge(st_v, i * 32 + (half + 1) * 16)
                    else:
                        act.wait_ge(st_u, i * 32 + (half + 1) * 16)
                    evac(u, n % 2, zst[kind], permuted=(kind == 2))
                    if not (last and n >= 4):
                        split_hi(m, act, u + 2, n % 2, i * 3 + (4 + n // 2 + 1))
                    tile = i * 2 + half
                    if kind == 1:
                        act.wait_ge(m.acc_free, u + 3)
                        act.dma_start(vT[ds(tile, 1), :, :].rearrange("a p n -> (a p) n"), zst[1][:, :]).then_inc(st_v, 16)
                        act.wait_ge(rope_done, i * 2 + (half + 8 + 3))
                        act.dma_start(kT[ds(tile, 1), :, :].rearrange("a p n -> (a p) n"), zo[half][:, :]).then_inc(st_zo[half], 16)
                    if kind == 2:
                        act.wait_ge(m.acc_free, u + 3)
                        act.dma_start(uT[ds(tile, 1), :, :].rearrange("a p n -> (a p) n"), zst[2][:, :]).then_inc(st_u, 16)

            with act.Fori(0, PM - 1) as i:
                turn(i, False)
            turn(PM - 1, True)
            act.wait_ge(st_v, 16 * 9)
            act.wait_ge(st_u, 16 * 9)
            for s in range(2):
                act.wait_ge(st_zo[s], 16 * 9)

        @block.gpsimd
        def _(pool):
            pool.sem_inc(m.lo_done, 2); pool.sem_inc(m.mm_done, 2); pool.sem_inc(m.acc_free, 2)
            pool.sem_inc(rope_done, 2); pool.sem_inc(rot_free, 1); pool.sem_inc(kv_used, 3); pool.sem_inc(kg_used, 1); pool.sem_inc(scored, 1)
            for s in (st_v, st_u, st_zo[0], st_zo[1]):
                pool.sem_inc(s, 16)
            for k in range(KT):
                pool.wait_ge(hh_ready, k + 1)
                pool.tensor_tensor(m.hl[:, k, :], m.xt[:, k, :], m.hh[:, k, :].bitcast(F32), ALU.subtract).then_inc(hl_ready, 1)
            for u in range(2):
                split_lo(m, pool, u, u)
            with pool.Fori(0, PQ) as i:
                for s in range(2):
                    split_lo(m, pool, i * 2 + (s + 2), s)
            def turn(i, last):
                for n in range(6):
                    if not (last and n >= 4):
                        split_lo(m, pool, i * 6 + (8 + n + 2), n % 2)
                    for j in range(32 * n // 6, 32 * (n + 1) // 6):
                        if j % 4 == 3:
                            pool.wait_ge(kp_in[3], i * 128 + (16 * (j // 4) + 16))
                            pool.wait_ge(qb_ready, i * 4 + (2 * (j // 16) + 2))
                            pool.wait_ge(scored, i * 32 + (j - 2))
                            pool.sem_inc(turn_taken, 1)
                            pool.tensor_tensor(prod[2][:, :], kring[:, 3, :], qb[:, ds(i * 2 + j // 16, 1), :].rearrange("p a b -> p (a b)"), ALU.mult).then_inc(kg_used, 1)

            with pool.Fori(0, PM - 1) as i:
                turn(i, False)
            turn(PM - 1, True)

        @block.tensor
        def _(pe):
            pe.wait_ge(c_in, 16 * 8)
            for k in range(KT):
                pe.wait_ge(sq_ready, k + 1)
                for h, (c0, n) in enumerate(HALVES):
                    mm = pe.matmul(m.aux[:, h, 0:n], m.ones[:, :], sq[:, k % 4, c0:c0 + n], start=(k == 0), stop=(k == KT - 1))
                mm.then_inc(sq_used, 1)

            pe.wait_ge(hl_ready, KT)

            def rotate(src, r, z_count):
                pe.wait_ge(z_ready, z_count)
                pe.wait_ge(m.acc_free, z_count + 2)
                pe.wait_ge(rot_free, r + 1)
                for h, (c0, n) in enumerate(HALVES):
                    mm = pe.matmul(m.aux[:, h, 0:n], m.rot[:, :], src[:, c0:c0 + n], start=True, stop=True)
                mm.then_inc(rot_ready, 1)

            with pe.Fori(0, PQ) as i:
                for s in range(2):
                    unit_matmuls(m, pe, i * 2 + s, s, m.hh, m.hl, s)
                for s in range(2):
                    rotate(zst[s], i * 2 + s, i * 2 + (s + 1))
            pe.wait_ge(qs_done, 8)
            for b in range(NS):
                for g in range(2):
                    if b > 0:
                        pe.wait_ge(qb_ready, 2 * b + g - 1)
                    for q in range(4):
                        mm = pe.matmul(m.aux[:, 2 + g, 128 * q:128 * q + 128], m.qs[:, 4 * g + q, b:b + 1].broadcast_to([P, P]),
                                       m.ident[:, :], start=True, stop=True)
                    mm.then_inc(qb_mm, 1)
            with pe.Fori(0, PM) as i:
                for n in range(6):
                    unit_matmuls(m, pe, i * 6 + (8 + n), n % 2, m.hh, m.hl, n % 2)
                    if n % 3 == 1:
                        rotate(zst[0], i * 2 + (8 + n // 3), i * 6 + (8 + n))

        @block.vector
        def _(dve):
            ch = Chain(dve, s_v)
            dve.wait_ge(c_in, 16 * 8)
            dve.wait_ge(rt_ready, 2)
            ch(dve.reciprocal(rs[:, :], rs[:, :]))
            for k in range(KT):
                dve.scalar_tensor_tensor(m.xt[:, k, :], m.xt[:, k, :], m.gains[:, 0, k:k + 1], rs[:, :], ALU.mult, ALU.mult).then_inc(h_ready, 1)

            def rope(src, dst, r, z_count, dst_free, dst_count):
                dve.wait_ge(m.acc_free, z_count + 2)
                dve.tensor_tensor(t1[:, :], src[:, :], cosT[:, :], ALU.mult)
                dve.wait_ge(rot_ready, r + 1)
                for h, (c0, n) in enumerate(HALVES):
                    x = dve.tensor_tensor(t2[:, c0:c0 + n], m.aux[:, h, 0:n], sinT[:, c0:c0 + n], ALU.mult)
                    if h == 0:
                        ch(x)
                x.then_inc(rot_free, 1)
                dve.wait_ge(rot_free, r + 2)
                dve.wait_ge(dst_free, dst_count)
                dve.tensor_tensor(dst[:, :], t1[:, :], t2[:, :], ALU.add).then_inc(rope_done, 1)

            with dve.Fori(0, PQ) as i:
                ch.enter(i, 2)
                for s in range(2):
                    rope(zst[s], zo[s], i * 2 + s, i * 2 + (s + 1), st_zo[s], i * 16 + 16)
                    dve.wait_ge(rope_done, i * 2 + (s + 3))
                    dve.tensor_copy(m.qs[:, ds(i * 2 + s, 1), :].rearrange("p a b -> p (a b)"), zo[s][:, 0:NS]).then_inc(qs_done, 1)
                ch.leave(PQ)
            with dve.Fori(0, PM) as i:
                ch.enter(i, 2)

                def multiply(j):
                    if j % 4 != 3:
                        x = 3 * (j // 4) + j % 4
                        dve.wait_ge(kp_in[j % 4], i * 128 + (16 * (j // 4) + 16))
                        dve.wait_ge(qb_ready, i * 4 + (2 * (j // 16) + 2))
                        dve.wait_ge(scored, i * 32 + (4 * ((x - 2) // 3) + (x - 2) % 3 + 2 if x >= 2 else 1))
                        dve.tensor_tensor(prod[x % 2][:, :], kring[:, j % 4, :], qb[:, ds(i * 2 + j // 16, 1), :].rearrange("p a b -> p (a b)"), ALU.mult).then_inc(kv_used, 1)

                def total(j):
                    x = 3 * (j // 4) + j % 4
                    dst = m.scd[:, j % 16, :].rearrange("p (c b h) -> p b h c", c=2, b=NS)
                    if j % 4 == 3:
                        dve.wait_ge(kg_used, i * 8 + (j // 4 + 2))
                    else:
                        dve.wait_ge(kv_used, i * 24 + (x + 4))
                    dve.tensor_reduce(dst[:, ds(i * 2 + j // 16, 1), :, :].rearrange("p a h c -> p (a h) c"), prod[2 if j % 4 == 3 else x % 2][:, :].rearrange("p (h c d) -> p h c d", c=2, d=64),
                                      AX.X, ALU.add).then_inc(scored, 1)

                multiply(0)
                for j in range(32):
                    if j < 31:
                        multiply(j + 1)
                    total(j)
                    if j % 16 == 8:
                        n = j // 16
                        rope(zst[0], zo[n], i * 2 + (8 + n), i * 6 + (9 + 3 * n), st_zo[n], i * 16 + (16 * 5))
                        dve.wait_ge(rope_done, i * 2 + (8 + n + 3))
                ch.leave(PM)


TAU_HI = 6.28125
TAU_MID = 0.0019350051879882812
TAU_LO = 2 * math.pi - TAU_HI - TAU_MID
MAGIC = 1.5 * 2.0 ** 23
QP = 4
PPQ = GP // QP
NC = NCH + NS


def mixer_plan(m):
    at = m.at
    m.top = m.x0
    m.hs = at("hs", [P, NC + 1, 3, GP])
    m.vv = at("vv", [P, NC, 2, GP])
    m.yall = at("yall", [P, G, NC], F32, off=m.end - NC * 2 * GP * 4)
    m.pw = at("pw", [P, 2, 9, GP]); m.bb = at("bb", [P, 2, GP, CH]); m.bc = at("bc", [P, 4, GP, CH])
    m.s5sm = at("s5sm", [P, 24, GP]); m.a1 = at("a1", [P, 2, 2, GP]); m.a2 = at("a2", [P, 2, 2, GP])
    m.u1 = at("u1", [P, 2, GP]); m.u2 = at("u2", [P, 2, GP])
    m.hn = at("hn", [P, NS, 2, GP]); m.hn2 = at("hn2", [P, NS, 2, GP]); m.dk = at("dk", [CH, G]); m.cm5 = at("cm5", [P, 4])
    m.room1, m.room1_end = m.top, m.x0 + 3 * KT * T * 4
    m.top = m.free
    m.ot = at("ot", [P, H, T])
    m.wtk_off = m.top
    m.wtk = at("wtk", [P, NPG, NS * H]); m.nv = at("nv", [P, H, NS])
    m.room2 = m.top
    m.raw_off = m.room1_end
    m.qq = at("qq", [P, QP, 2, PPQ, 9, CH], F32, off=m.raw_off + 2 * KT * P * 4)


def cplx(eng, ch, dst, a, b, c, d, t, op):
    ch(eng.tensor_tensor(t, c, d, ALU.mult))
    ch(eng.tensor_tensor(dst, a, b, ALU.mult))
    return eng.tensor_tensor(dst, dst, t, op)


def pair_coeffs(x, g, n):
    return x[:, g, :].unsqueeze(2).broadcast_to([P, PPQ, n, CH])


def pair_powers(m, r, g, n):
    return m.pw[:, r, 0:n, g].rearrange("p j g -> p g j").unsqueeze(3).broadcast_to([P, PPQ, n, CH])


def load_ug(m, sp, ug, ug_in, ug_zero):
    uv = m.uT[:, :, :].rearrange("a (g c) n -> c (a g) n", c=CH)
    for j in range(CL):
        s0 = NS + (CL - 1 - j) * NCH
        sp.dma_start(ug[CH * j:CH * j + CH, :, NS:NC], uv[:, :, s0:s0 + NCH]).then_inc(ug_in, 16)
    sp.wait_ge(ug_zero, 2)
    sp.dma_start(ug[0:CH, :, 0:NS], uv[:, :, 0:NS]).then_inc(ug_in, 16)
    sp.dma_start(ug[P - CH:P, :, NC:NC + NS], uv[:, :, 0:NS]).then_inc(ug_in, 16)


def stage_p1(nc, m, ins, outs):
    at, sem = m.at, m.sem
    mixer_plan(m)
    pw, bb, bc, vv, hs, lam = m.pw, m.bb, m.bc, m.vv, m.hs, m.lam
    m.top = m.room1
    ug = at("ug", [P, G, NC + NS]); ti = at("ti", [P, PPQ, CL, CH]); tr = at("tr", [P, GP * CH])
    assert m.top <= m.room1_end
    m.top = m.room2
    e = at("e", [P, 2, PPQ, CL, CH]); et = at("et", [P, 2, PPQ, P]); stT = at("stT", [P, 2052])
    lamv = at("lamv", [P, 4, 64]); lamp = at("lamp", [P, 2, 64])
    ksv = at("ksv", [P, 2, H, NS]); tmp = at("tmp", [P, H, NS]); qk2 = at("qk2", [P, 2, NS, H]); dm = at("dm", [P, NS * H]); mm_ = at("mm_", [P, NS * H]); cm = at("cm", [P, 2]); dsm = at("dsm", [P, 8])
    tr2 = at("tr2", [P, PPQ, CL, CH], F32, off=m.raw_off)
    f = lambda j: m.s5sm[:, j, :]
    S = {n: sem("h_" + n) for n in ("small bcin hin c2in ksin ugz ugin aexp dx asin dr pw bb ere eim etr eev vmm vev "
                                    "tr ev lame lams qk ns nm ex m wtmm wtev wn v p").split()}
    with nc.Block() as block:
        @block.sync
        def _(sp):
            for j, n in enumerate(("a_re", "a_im", "log_dt")):
                sp.dma_start(m.s5sm[:, j, :], ins[n][:, :]).then_inc(S["small"], 16)
            sp.dma_start(m.cm5[:, :], ins["cmask4"][:, :]).then_inc(S["small"], 16)
            sp.dma_start(dm[:, :], ins["dmask"][:, :]).then_inc(S["c2in"], 16)
            sp.dma_start(cm[:, :], ins["cmask"][:, :]).then_inc(S["c2in"], 16)
            for j in range(4):
                sp.dma_start(lamv[:, j, :], ins["lambdas"][j:j + 1, :].broadcast_to([P, 64])).then_inc(S["c2in"], 16)
            sp.dma_start(ksv[:, 0, :, :], m.kT[:, :, 0:NS].rearrange("h p b -> p h b")).then_inc(S["ksin"], 16)
            sp.dma_start(ksv[:, 1, :, :], m.vT[:, :, 0:NS].rearrange("h p b -> p h b")).then_inc(S["ksin"], 16)
            for j, n in enumerate(("b_re", "b_im", "c_re", "c_im")):
                sp.dma_start(bc[:, j, :, :], ins[n][:, :, :]).then_inc(S["bcin"], 16)
            load_ug(m, sp, ug, S["ugin"], S["ugz"])
            for r, n in enumerate(("h0_re", "h0_im")):
                sp.dma_start(hs[:, NCH:NC, r, :], ins[n][:, :, :]).then_inc(S["hin"], 16)
            sp.dma_start(m.dk[:, :], ins["d_t"][:, :]).then_inc(S["hin"], 16)
            sp.wait_ge(S["hin"], 48)

        @block.gpsimd
        def _(pool):
            ch = Chain(pool, S["p"])
            pool.memset(ug[:, :, 0:NS], 0.0).then_inc(S["ugz"], 1)
            pool.memset(ug[:, :, NC:NC + NS], 0.0).then_inc(S["ugz"], 1)
            pool.wait_ge(S["bb"], 1)
            pool.wait_ge(S["pw"], 1)
            for q in range(QP):
                g = slice(PPQ * q, PPQ * q + PPQ)
                if q >= 1:
                    pool.wait_ge(S["etr"], 4 * q)
                cplx(pool, ch, e[:, 1, :, :, :], pair_coeffs(bb[:, 0], g, CL), pair_powers(m, 1, g, CL), pair_coeffs(bb[:, 1], g, CL), pair_powers(m, 0, g, CL),
                     ti[:, :, :, :], ALU.add).then_inc(S["eim"], 1)
                pool.wait_ge(S["eim"], q + 1)

        @block.scalar
        def _(act):
            act.wait_ge(S["small"], 64)
            act.activation(f(3), f(2), ACT.Exp).then_inc(S["aexp"], 1)
            act.wait_ge(S["dx"], 1)
            act.activation(f(6), f(4), ACT.Exp).then_inc(S["aexp"], 1)
            act.wait_ge(S["lams"], 1)
            act.activation(lam[:, 2:4], lam[:, 0:2], ACT.Exp).then_inc(S["lame"], 1)
            act.wait_ge(S["nm"], 1)
            act.activation(stT[:, 0:2049], stT[:, 0:2049], ACT.Exp, bias=dsm[:, 1:2], scale=0.125, accum_out=dsm[:, 2:3]).then_inc(S["ex"], 1)
            act.wait_ge(S["dr"], 1)
            act.activation(f(9), f(7), ACT.Sin).then_inc(S["asin"], 1)
            act.activation(f(10), f(8), ACT.Sin).then_inc(S["asin"], 1)
            for q in range(QP):
                for n in range(4):
                    act.wait_ge(S["etr"], 4 * q + n + 1)
                    if q >= 1:
                        act.wait_ge(S["vmm"], 4 * q)
                    act.activation(et[:, n // 2, 4 * (n % 2):4 * (n % 2) + 4, :].rearrange("p a b -> p (a b)"), m.aux[:, n, :], ACT.Copy).then_inc(S["eev"], 1)
                for n in range(4):
                    act.wait_ge(S["vmm"], 4 * q + n + 1)
                    g0 = PPQ * q + 4 * (n % 2)
                    act.activation(vv[:, :, n // 2, g0:g0 + 4].rearrange("p n g -> p g n"), m.acc[:, n // 2, n % 2, 0:4 * NC].rearrange("p (g n) -> p g n", g=4), ACT.Copy).then_inc(S["vev"], 1)

        @block.tensor
        def _(pe):
            for j in range(NPG):
                if j % 4 == 0 and j >= 8:
                    pe.wait_ge(S["ev"], j // 4 - 1)
                mm = pe.transpose(m.aux[:, (j // 4) % 2, P * (j % 4):P * (j % 4) + P], m.scd[:, j, :], m.ident[:, :])
                if j % 4 == 3:
                    mm.then_inc(S["tr"], 1)
            pe.wait_ge(S["qk"], 1)
            pe.matmul(m.aux[:, 2, 0:1], qk2[:, :, :, :].rearrange("p c b h -> p (c b h)"), m.ones[:, 0:1], start=True, stop=True).then_inc(S["ns"], 1)
            pe.wait_ge(S["m"], 1)
            pe.wait_ge(S["ex"], 1)
            for j in range(NPG):
                mm = pe.matmul(m.aux[:, j // 8, 64 * (j % 8):64 * (j % 8) + 64], stT[:, P * j:P * j + P], mm_[:, :], start=True, stop=True)
                if j % 8 == 7:
                    mm.then_inc(S["wtmm"], 1)
            pe.matmul(m.aux[:, 2, 64:128], stT[:, 2048:2049].broadcast_to([P, P]), mm_[:, :], start=True, stop=True).then_inc(S["wn"], 1)
            pe.wait_ge(S["wtev"], 3)
            for q in range(QP):
                pe.wait_ge(S["ere"], q + 1)
                pe.wait_ge(S["eim"], q + 1)
                for n in range(4):
                    if q >= 1:
                        pe.wait_ge(S["eev"], 4 * (q - 1) + n + 1)
                    for a in range(4):
                        mm = pe.transpose(m.aux[:, n, P * a:P * a + P], e[:, n // 2, 4 * (n % 2) + a, :, :].rearrange("p j c -> p (j c)"), m.ident[:, :])
                    mm.then_inc(S["etr"], 1)
                pe.wait_ge(S["ugin"], 16 * (CL + 2))
                for n in range(4):
                    pe.wait_ge(S["eev"], 4 * q + n + 1)
                    if q >= 1:
                        pe.wait_ge(S["vev"], 4 * (q - 1) + n + 1)
                    for a in range(4):
                        gp = PPQ * q + 4 * (n % 2) + a
                        for g2 in range(2):
                            mm = pe.matmul(m.acc[64 * g2:64 * g2 + 64, n // 2, n % 2, NC * a:NC * a + NC], et[:, n // 2, 4 * (n % 2) + a, 64 * g2:64 * g2 + 64],
                                           ug[:, 2 * gp + g2, 0:NC], start=True, stop=True)
                    mm.then_inc(S["vmm"], 1)

        @block.vector
        def _(dve):
            ch = Chain(dve, S["v"])
            tt = lambda o, a, b, op: ch(dve.tensor_tensor(o, a, b, op))
            ts = lambda o, a, s1, s2, o1, o2=None: ch(dve.tensor_scalar(o, a, s1, s2, o1, o2) if o2 is not None else dve.tensor_scalar(o, a, s1, None, o1))
            dve.wait_ge(S["small"], 64)
            dve.wait_ge(S["aexp"], 1)
            tt(f(5), f(1), f(3), ALU.mult)
            dve.tensor_tensor(f(4), f(0), f(3), ALU.mult).then_inc(S["dx"], 1)
            dve.wait_ge(S["c2in"], 16 * 6)
            ch(dve.tensor_tensor(lamp[:, :, :], lamv[:, 0:4:2, :], lamv[:, 1:4:2, :], ALU.mult))
            dve.tensor_reduce(lam[:, 0:2], lamp[:, :, :], AX.X, ALU.add).then_inc(S["lams"], 1)
            dve.wait_ge(S["ksin"], 32)
            ch(dve.tensor_tensor(tmp[:, :, :], m.qs[:, :, :], ksv[:, 0, :, :], ALU.mult))
            for c in range(2):
                x = dve.tensor_scalar(qk2[:, c, :, :].rearrange("p b h -> p h b"), tmp[:, :, :], cm[:, c:c + 1], None, ALU.mult)
                if c == 0:
                    ch(x)
            x.then_inc(S["qk"], 1)
            for g in range(4):
                dve.wait_ge(S["tr"], g + 1)
                dve.tensor_copy(stT[:, 512 * g:512 * g + 512], m.aux[:, g % 2, :]).then_inc(S["ev"], 1)
            dve.wait_ge(S["ns"], 1)
            dve.wait_ge(S["ev"], 4)
            ch(dve.tensor_copy(stT[:, 2048:2049], m.aux[:, 2, 0:1]))
            ch(dve.tensor_reduce(dsm[:, 0:1], stT[:, 0:2049], AX.X, ALU.max))
            dve.tensor_scalar(dsm[:, 1:2], dsm[:, 0:1], -0.125, None, ALU.mult).then_inc(S["nm"], 1)
            for out, quarter in ((7, 0.0), (8, 0.25)):
                ts(f(11), f(5), 1 / (2 * math.pi), quarter, ALU.mult, ALU.add)
                ts(f(11), f(11), MAGIC, None, ALU.add)
                ts(f(11), f(11), -MAGIC, None, ALU.add)
                ch(dve.scalar_tensor_tensor(f(12), f(11), -TAU_HI, f(5), ALU.mult, ALU.add))
                ch(dve.scalar_tensor_tensor(f(12), f(11), -TAU_MID, f(12), ALU.mult, ALU.add))
                ch(dve.scalar_tensor_tensor(f(12), f(11), -TAU_LO, f(12), ALU.mult, ALU.add))
                if quarter:
                    ts(f(12), f(12), math.pi / 2, None, ALU.add)
                ts(f(out), f(12), 3.1415925, -3.1415925, ALU.min, ALU.max)
            ch(dve.memset(pw[:, 0, 0, :], 1.0))
            dve.memset(pw[:, 1, 0, :], 0.0).then_inc(S["dr"], 1)
            dve.wait_ge(S["lame"], 1)
            ch(dve.tensor_tensor(lam[:, 4:5], lam[:, 3:4], lam[:, 2:3], ALU.subtract))
            ch(dve.tensor_scalar(lam[:, 4:5], lam[:, 4:5], -LAM0, None, ALU.add))
            ch(dve.scalar_tensor_tensor(dsm[:, 4:5], cm[:, 1:2], lam[:, 4:5], cm[:, 0:1], ALU.mult, ALU.add))
            dve.wait_ge(S["ex"], 1)
            ch(dve.reciprocal(dsm[:, 5:6], dsm[:, 2:3]))
            ch(dve.tensor_tensor(dsm[:, 6:7], dsm[:, 5:6], dsm[:, 4:5], ALU.mult))
            dve.tensor_scalar(mm_[:, :], dm[:, :], dsm[:, 6:7], None, ALU.mult).then_inc(S["m"], 1)
            dve.wait_ge(S["dr"], 1)
            dve.wait_ge(S["asin"], 2)
            dve.wait_ge(S["aexp"], 2)
            tt(pw[:, 0, 1, :], f(6), f(10), ALU.mult)
            tt(pw[:, 1, 1, :], f(6), f(9), ALU.mult)

            def powers(lo, n, by):
                a = [pw[:, r, lo:lo + n, :] for r in range(2)]
                b = [pw[:, r, by:by + 1, :].broadcast_to([P, n, GP]) for r in range(2)]
                t = m.s5sm[:, 13:13 + n, :]
                ch(cplx(dve, ch, pw[:, 0, by + lo:by + lo + n, :], a[0], b[0], a[1], b[1], t, ALU.subtract))
                return cplx(dve, ch, pw[:, 1, by + lo:by + lo + n, :], a[0], b[1], a[1], b[0], t, ALU.add)

            ch(powers(1, 1, 1))
            ch(powers(1, 2, 2))
            powers(1, 4, 4).then_inc(S["pw"], 1)
            dve.wait_ge(S["pw"], 1)
            tt(f(13), f(0), f(0), ALU.mult)
            tt(f(14), f(1), f(1), ALU.mult)
            tt(f(13), f(13), f(14), ALU.add)
            ch(dve.reciprocal(f(13), f(13)))
            ts(f(14), pw[:, 0, 1, :], -1.0, None, ALU.add)
            ch(cplx(dve, ch, f(15), f(14), f(0), pw[:, 1, 1, :], f(1), f(17), ALU.add))
            ch(cplx(dve, ch, f(16), pw[:, 1, 1, :], f(0), f(14), f(1), f(17), ALU.subtract))
            tt(f(15), f(15), f(13), ALU.mult)
            tt(f(16), f(16), f(13), ALU.mult)
            fr = [f(15 + r).unsqueeze(2).broadcast_to([P, GP, CH]) for r in range(2)]
            tb = tr[:, :].rearrange("p (g c) -> p g c", c=CH)
            dve.wait_ge(S["bcin"], 64)
            ch(cplx(dve, ch, bb[:, 0, :, :], fr[0], bc[:, 0, :, :], fr[1], bc[:, 1, :, :], tb, ALU.subtract))
            cplx(dve, ch, bb[:, 1, :, :], fr[0], bc[:, 1, :, :], fr[1], bc[:, 0, :, :], tb, ALU.add).then_inc(S["bb"], 1)
            dve.wait_ge(S["bb"], 1)
            for q in range(QP):
                g = slice(PPQ * q, PPQ * q + PPQ)
                if q >= 1:
                    dve.wait_ge(S["etr"], 4 * q)
                cplx(dve, ch, e[:, 0, :, :, :], pair_coeffs(bb[:, 0], g, CL), pair_powers(m, 0, g, CL), pair_coeffs(bb[:, 1], g, CL), pair_powers(m, 1, g, CL),
                     tr2[:, :, :, :], ALU.subtract).then_inc(S["ere"], 1)
                dve.wait_ge(S["ere"], q + 1)
                if q == 0:
                    for j in range(2):
                        dve.wait_ge(S["wtmm"], j + 1)
                        dve.tensor_copy(m.wtk[:, 8 * j:8 * j + 8, :].rearrange("p j n -> p (j n)"), m.aux[:, j, :]).then_inc(S["wtev"], 1)
                    dve.wait_ge(S["wn"], 1)
                    dve.tensor_tensor(m.nv[:, :, :], m.aux[:, 2, 64:128].rearrange("p (b h) -> p h b", h=H), ksv[:, 1, :, :], ALU.mult).then_inc(S["wtev"], 1)
            for k, j in ((0, CL), (1, 1)):
                for r in range(2):
                    ch(dve.tensor_copy(m.a1[:, k, r, :], pw[:, 0, j, :]))
                ts(m.a2[:, k, 0, :], pw[:, 1, j, :], -1.0, None, ALU.mult)
                ch(dve.tensor_copy(m.a2[:, k, 1, :], pw[:, 1, j, :]))
            ch(dve.memset(hs[:, 0, :, :], 0.0))


VR = 16
HW = H * P // 2
PV_STEPS = ((0, 0, 6), (0, 6, 12), (0, 12, 16), (1, 0, 8), (1, 8, 16))

def stage_l1(nc, m, ins, outs):
    at, sem = m.at, m.sem
    lam = m.lam
    m.top = m.room1
    qkv = at("qkv", [P, 2, 3, NT])
    vtok = at("vtok", [P, 2, 4, P]); ex = at("ex", [P, 2, 2, NT]); wT = at("wT", [P, 2, 4, P])
    st = at("stt", [P, 2, 2, 8])
    assert m.top <= m.room1_end, (m.top, m.room1_end)
    m.top = m.room2
    vr = [at(f"vr{j}", [P, HW], F32, off=m.raw_off + 4 * HW * j if j < 8 else None) for j in range(VR)]
    wb = at("wb", [P, NPG, H]); pvs = at("pvs", [H, HW])
    qt = at("qt", [P, PPQ, 9, CH]); npw = at("npw", [P, 9, GP]); cmk = at("causal", [P, P]); dg = at("dg", [P, 2, 2, P])
    vp_in, vp_free = [sem(f"vp_in{j}") for j in range(VR)], sem("vp_free")
    pvs_r, wb_r, pv_done, pv_ev, sc_u, sc_h, sc_v, hn_d, so = [sem("l_" + x) for x in "pvs wb pv pvev u h v hn so".split()]
    vals = ins["cache_v"]
    q_in = [sem(f"q_in{j}") for j in range(2)]; cm_in = sem("cm_in")
    v_tr, v_ev, s_mm, s_free, nm_r, e_r, d_r, w_mm, w_ev, o_mm, o_ev, e_free, s_v3 = [sem("p_" + x) for x in "vtr vev smm sfree nm e d wmm wev omm oev efree v3".split()]
    R = H * 4
    with nc.Block() as block:
        @block.sync
        def _(sp):
            sp.dma_start(cmk[:, :], ins["causal"][:, :]).then_inc(cm_in, 16)
            with sp.Fori(0, H // 2) as hh:
                for s in range(2):
                    for half in range(2):
                        for j in range(NPG):
                            page = sp.value_load(m.pages[0:1, ds(hh * 32 + (16 * s + j), 1)], min_val=0, max_val=vals.shape[0] - 1)
                            sp.wait_ge(vp_free, hh * 64 + (32 * s + 16 * half + j + 1))
                            sp.dma_start(vr[j][:, :], vals[ds(page, 1), :, HW * half:HW * half + HW].rearrange("a p n -> (a p) n")).then_inc(vp_in[j], 16)

        @block.gpsimd
        def _(pool):
            for s, n in ((s_free, 2), (e_free, 2), (v_ev, 1), (w_ev, 2), (o_ev, 2), (o_mm, 2), (vp_free, VR), (pv_ev, 1), (pv_done, 1)):
                pool.sem_inc(s, n)
            ch = Chain(pool, sc_v)
            hs, vv, a1, a2, u1, u2 = m.hs, m.vv, m.a1, m.a2, m.u1, m.u2

            def step(src, dst, add):
                pool.tensor_tensor(u1[:, :, :], src[:, 0:2, :], a1[:, 0, :, :], ALU.mult)
                ch(pool.tensor_tensor(u2[:, :, :], src[:, 1:3, :], a2[:, 0, :, :], ALU.mult))
                ch(pool.tensor_tensor(u1[:, :, :], u1[:, :, :], add, ALU.add))
                pool.tensor_tensor(dst[:, 0:2, :], u1[:, :, :], u2[:, :, :], ALU.add)
                ch(pool.tensor_tensor(dst[:, 2, :], u1[:, 0, :], u2[:, 0, :], ALU.add))

            row = lambda t, i: t[:, ds(i, 1), :, :].rearrange("p a r g -> p (a r) g")
            with pool.Fori(0, NCH - 1) as i:
                ch.enter(i, 3)
                step(row(hs, i), row(hs, i + 1), row(vv, i + NS))
                ch.leave(NCH - 1)
            step(hs[:, NCH - 1, :, :], hs[:, NC, :, :], vv[:, NC - 1, :, :])
            bcs = lambda x: x.unsqueeze(1).broadcast_to([P, NS, GP])
            hn, hn2 = m.hn, m.hn2
            for r in range(2):
                ch(pool.tensor_tensor(hn[:, :, r, :], hs[:, NCH:NC, r, :], bcs(a1[:, 1, r, :]), ALU.mult))
                ch(pool.tensor_tensor(hn2[:, :, r, :], hs[:, NCH:NC, 1 - r, :], bcs(a2[:, 1, r, :]), ALU.mult))
            ch(pool.tensor_tensor(hn[:, :, :, :], hn[:, :, :, :], hn2[:, :, :, :], ALU.add))
            pool.tensor_tensor(hn[:, :, :, :], hn[:, :, :, :], vv[:, 0:NS, :, :], ALU.add).then_inc(hn_d, 1)
            pool.wait_ge(hn_d, 1)
            ch(pool.memset(npw[:, :, :], 0.0))
            ch(pool.tensor_tensor(npw[:, :, :], npw[:, :, :], m.pw[:, 1, :, :], ALU.subtract))
            for q in range(QP):
                g = slice(PPQ * q, PPQ * q + PPQ)
                neg = npw[:, :, g].rearrange("p j g -> p g j").unsqueeze(3).broadcast_to([P, PPQ, 9, CH])
                ch(cplx(pool, ch, m.qq[:, q, 0, :, :, :], pair_coeffs(m.bc[:, 2], g, 9), pair_powers(m, 0, g, 9), pair_coeffs(m.bc[:, 3], g, 9), pair_powers(m, 1, g, 9),
                        qt[:, :, :, :], ALU.subtract))
                ch(cplx(pool, ch, m.qq[:, q, 1, :, :, :], pair_coeffs(m.bc[:, 2], g, 9), neg, pair_coeffs(m.bc[:, 3], g, 9), pair_powers(m, 0, g, 9),
                        qt[:, :, :, :], ALU.subtract))

        @block.tensor
        def _(pe):
            with pe.Fori(0, H // 2) as hh:
                for s in range(2):
                    pe.wait_ge(q_in[s], hh * 48 + 48)
                    it = lambda q: hh * 8 + (4 * s + q)
                    for step in range(4 + 2):
                        if step < 4:
                            q = step
                            pe.wait_ge(s_free, it(q) + 1)
                            for c in range(2):
                                mm = pe.matmul(m.acc[:, q % 2, c, 0:128 * (q + 1)], qkv[64 * c:64 * c + 64, s, 0, 128 * q:128 * q + 128],
                                               qkv[64 * c:64 * c + 64, s, 1, 0:128 * (q + 1)], start=True, stop=True)
                            mm.then_inc(s_mm, 1)
                            if step == 0:
                                pe.wait_ge(w_ev, it(q) + 2)
                                pe.wait_ge(v_ev, hh * 2 + (s + 1))
                                for kb in range(4):
                                    mm = pe.transpose(m.aux[:, 1, 128 * kb:128 * kb + 128], qkv[:, s, 2, 128 * kb:128 * kb + 128], m.ident[:, :])
                                mm.then_inc(v_tr, 1)
                        if 1 <= step <= 4:
                            q = step - 1
                            pe.wait_ge(d_r, it(q) + 1)
                            pe.wait_ge(e_r, hh * 16 + (8 * s + 2 * q + 2))
                            pe.wait_ge(w_ev, it(q) + 1)
                            if q == 1:
                                pe.wait_ge(v_ev, hh * 2 + (s + 2))
                            for kb in range(q + 1):
                                for c in range(2):
                                    mm = pe.matmul(m.aux[:, q % 2, 128 * kb:128 * kb + 128], ex[:, q % 2, c, 128 * kb:128 * kb + 128], dg[:, q % 2, c, :],
                                                   start=(c == 0), stop=(c == 1))
                            mm.then_inc(w_mm, 1)
                        if step >= 2:
                            q = step - 2
                            pe.wait_ge(w_ev, it(q) + 3)
                            pe.wait_ge(v_ev, hh * 2 + (s + 2))
                            pe.wait_ge(o_ev, it(q) + 2)
                            for kb in range(q + 1):
                                mm = pe.matmul(m.aux[:, 2, 0:128], vtok[:, s, kb, :], wT[:, q % 2, kb, :], start=(kb == 0), stop=(kb == q))
                            mm.then_inc(o_mm, 1)
                        if step in (3, 5):
                            half = step // 2 - 1
                            pe.wait_ge(pvs_r, hh * 4 + (2 * s + half + 1))
                            for i in range(H // 2):
                                mm = pe.matmul(m.aux[:, 3, i:i + 1], pvs[:, P * i:P * i + P], m.ident[0:H, H // 2 * half + i:H // 2 * half + i + 1],
                                               start=(i == 0), stop=(i == H // 2 - 1), skip_group_check=True)
                            mm.then_inc(pv_done, 1)
                        if step < 5:
                            half, lo, hi = PV_STEPS[step]
                            if step == 0:
                                pe.wait_ge(wb_r, hh * 2 + (s + 1))
                            if lo == 0:
                                pe.wait_ge(pv_ev, hh * 4 + (2 * s + half + 1))
                            for j in range(lo, hi):
                                pe.wait_ge(vp_in[j], hh * 64 + (32 * s + 16 * half + 16))
                                pe.matmul(m.aux[0:H, 3, 0:HW], wb[:, j, :], vr[j][:, :], start=(j == 0), stop=(j == NPG - 1)).then_inc(vp_free, 1)
        @block.scalar
        def _(act):
            def load_head(h, s):
                for n, t in enumerate((m.qT, m.kT, m.vT)):
                    act.dma_start(qkv[:, s, n, :], t[ds(h, 1), :, NS:T].rearrange("a p n -> (a p) n")).then_inc(q_in[s], 16)
            for s in range(2):
                load_head(s, s)
            def turn(hh, last):
                for s in range(2):
                    it = lambda q: hh * 8 + (4 * s + q)
                    for step in range(4 + 2):
                        if step < 4:
                            q = step
                            act.wait_ge(nm_r, it(q) + 1)
                            act.wait_ge(e_free, it(q) + 1)
                            for c in range(2):
                                x = act.activation(ex[:, q % 2, c, 0:128 * (q + 1)], m.acc[:, q % 2, c, 0:128 * (q + 1)], ACT.Exp, bias=st[:, q % 2, c, 1:2], scale=0.125,
                                               accum_out=st[:, q % 2, c, 2:3])
                                x.then_inc(e_r, 1)
                            act.wait_ge(e_r, hh * 16 + (8 * s + 2 * q + 2))
                            act.sem_inc(s_free, 1)
                        if step == 1:
                            act.wait_ge(v_tr, hh * 2 + (s + 1))
                            act.wait_ge(o_mm, hh * 8 + (4 * s + 2))
                            act.activation(vtok[:, s, :, :].rearrange("p a b -> p (a b)"), m.aux[:, 1, :], ACT.Copy).then_inc(v_ev, 1)
                        if 1 <= step <= 4:
                            q = step - 1
                            act.wait_ge(w_mm, it(q) + 1)
                            act.sem_inc(e_free, 1)
                            act.wait_ge(o_mm, it(q) + 1)
                            act.activation(wT[:, q % 2, 0:q + 1, :].rearrange("p a b -> p (a b)"), m.aux[:, q % 2, 0:128 * (q + 1)], ACT.Copy).then_inc(w_ev, 1)
                        if step >= 2:
                            q = step - 2
                            act.wait_ge(o_mm, it(q) + 3)
                            act.activation(m.ot[:, ds(hh * 2 + s, 1), NS + 128 * q:NS + 128 * q + 128].rearrange("p a b -> p (a b)"), m.aux[:, 2, 0:128], ACT.Copy).then_inc(o_ev, 1)
                        if step in (2, 4):
                            half = step // 2 - 1
                            act.wait_ge(vp_free, hh * 64 + (32 * s + 16 * half + 32))
                            act.activation(pvs[:, :], m.aux[0:H, 3, 0:HW], ACT.Copy).then_inc(pvs_r, 1)
                        if step in (3, 5):
                            half = step // 2 - 1
                            act.wait_ge(pv_done, hh * 4 + (2 * s + half + 2))
                            act.activation(m.ot[:, H // 2 * half:H // 2 * half + H // 2, ds(hh * 2 + s, 1)].rearrange("p h a -> p (h a)"), m.aux[:, 3, 0:H // 2], ACT.Copy).then_inc(pv_ev, 1)
                    if not last:
                        act.wait_ge(o_mm, hh * 8 + (4 * s + 6))
                        load_head(hh * 2 + (s + 2), s)

            with act.Fori(0, H // 2 - 1) as hh:
                turn(hh, False)
            turn(H // 2 - 1, True)

        @block.vector
        def _(dve):
            ch = Chain(dve, s_v3)
            dve.wait_ge(cm_in, 16)
            with dve.Fori(0, H // 2) as hh:
                ch.enter(hh, 2 * (4 * 3 * 2 + 4 * 3))
                for s in range(2):
                    it = lambda q: hh * 8 + (4 * s + q)
                    dve.wait_ge(pv_done, hh * 4 + (2 * s + 1))
                    dve.tensor_copy(wb[:, :, :], m.wtk[:, :, ds((hh * 2 + s) * H, H)]).then_inc(wb_r, 1)
                    for q in range(4):
                        dve.wait_ge(s_mm, it(q) + 1)
                        for c in range(2):
                            sc = m.acc[:, q % 2, c, :]
                            ch(dve.tensor_tensor(sc[:, 128 * q:128 * q + 128], sc[:, 128 * q:128 * q + 128], cmk[:, :], ALU.add))
                            ch(dve.tensor_reduce(st[:, q % 2, c, 0:1], sc[:, 0:128 * (q + 1)], AX.X, ALU.max))
                            ch(dve.tensor_scalar(st[:, q % 2, c, 1:2], st[:, q % 2, c, 0:1], -0.125, None, ALU.mult))
                        dve.sem_inc(nm_r, 1)
                        dve.wait_ge(e_r, hh * 16 + (8 * s + 2 * q + 2))
                        dve.wait_ge(e_free, it(q) + 1)
                        for c in range(2):
                            x = dve.reciprocal(st[:, q % 2, c, 3:4], st[:, q % 2, c, 2:3])
                            if c == 1:
                                ch(x)
                                ch(dve.tensor_tensor(st[:, q % 2, c, 3:4], st[:, q % 2, c, 3:4], lam[:, 4:5], ALU.mult))
                            else:
                                ch(x)
                        for c in range(2):
                            x = dve.tensor_scalar(dg[:, q % 2, c, :], m.ident[:, :], st[:, q % 2, c, 3:4], None, ALU.mult)
                        x.then_inc(d_r, 1)
                ch.leave(H // 2)
            dve.wait_ge(pv_ev, 2 * H + 1)
            ch(dve.tensor_tensor(m.ot[:, :, 0:NS], m.ot[:, :, 0:NS], m.nv[:, :, :], ALU.add))


def stage_p3(nc, m, ins, outs):
    at, sem = m.at, m.sem
    bb, qq, hs, yall, dk = m.bb, m.qq, m.hs, m.yall, m.dk
    m.top = m.room1
    ug = at("ug3", [P, G, NC + NS])
    assert m.top <= m.room1_end, (m.top, m.room1_end)
    m.top = m.wtk_off
    tz = [at(f"tz{j}", [P, 2 * PPQ, P]) for j in range(2)]; km = [at(f"km{j}", [CH, 2 * PPQ, P]) for j in range(2)]
    de = [at(f"de{j}", [CH, 2 * PPQ, CH]) for j in range(2)]
    ug_zero, ug_in, y_out, tz_zero = [sem("y_" + x) for x in "ugzero ugin out tzzero".split()]; shift_in = [sem(f"y_shift{j}") for j in range(2)]
    k_mm, k_ev, k_d, y_mm, y_ev, s_v = [sem("y_" + x) for x in "kmm kev kd ymm yev v".split()]
    m.top = m.raw_off
    sq = at("head_sq", [P, 4, T]); rs = at("head_rs", [P, 2, T]); gsub = at("gsub", [P, 2])
    assert m.end <= m.raw_off + 2 * KT * P * 4
    gs_in, sq_ready, sum_ready, root_ready, scaled = [sem("n_" + x) for x in "gsin sq sum root scaled".split()]
    in_bank = lambda n, g0=0: slice(g0 + 8 * (n // 2) + n % 2, g0 + 8 * (n // 2) + n % 2 + 7, 2)
    with nc.Block() as block:
        @block.sync
        def _(sp):
            load_ug(m, sp, ug, ug_in, ug_zero)
            sp.dma_start(gsub[:, 0:1], ins["g_sub"][:, :]).then_inc(gs_in, 16)
            for q in range(QP):
                sp.wait_ge(tz_zero, min(q, 1) + 1)
                sp.wait_ge(k_d, q + 1)
                if q >= 2:
                    sp.wait_ge(y_mm, 4 * (q - 1))
                for j in range(CL):
                    sp.dma_start(tz[q % 2][CH * j:CH * j + CH, :, CH * (CL - 1 - j):P], km[q % 2][:, :, 0:CH * (j + 1)]).then_inc(shift_in[q % 2], 16)
            yv = m.yT[:, :, :].rearrange("a (g c) n -> c (a g) n", c=CH)
            for half in range(2):
                g = slice(G // 2 * half, G // 2 * half + G // 2)
                sp.wait_ge(y_ev, 2 * QP * (half + 1))
                for s in range(CL):
                    sp.dma_start(yv[:, g, NS + s * NCH:NS + (s + 1) * NCH], yall[CH * s:CH * s + CH, g, 0:NCH]).then_inc(y_out, 16)
                sp.dma_start(yv[:, g, 0:NS], yall[0:CH, g, NCH:NC]).then_inc(y_out, 16)
            sp.dma_start(outs["ssm_prompt"][:, :, :], hs[:, NC, 0:2, :]).then_inc(y_out, 16)
            sp.dma_start(outs["ssm_sample"][:, :, :, :], m.hn[:, :, :, :]).then_inc(y_out, 16)
            sp.wait_ge(y_out, 16 * (2 * CL + 4))

        @block.gpsimd
        def _(pool):
            pool.memset(tz[0][:, :, :], 0.0).then_inc(tz_zero, 1)
            pool.memset(tz[1][:, :, :], 0.0).then_inc(tz_zero, 1)
            for h in range(H):
                if h >= 4:
                    pool.wait_ge(sum_ready, h - 3)
                pool.tensor_tensor(sq[:, h % 4, :], m.ot[:, h, :], m.ot[:, h, :], ALU.mult).then_inc(sq_ready, 1)

        @block.scalar
        def _(act):
            def copy_k(q):
                for n in range(4):
                    act.wait_ge(k_mm, 4 * q + n + 1)
                    if q >= 2:
                        act.wait_ge(shift_in[q % 2], 16 * CL * (q // 2))
                    act.activation(km[q % 2][:, in_bank(n), :], m.aux[0:CH, n, :].rearrange("p (a b) -> p a b", b=P), ACT.Copy).then_inc(k_ev, 1)

            copy_k(0)
            for q in range(QP):
                if q < QP - 1:
                    copy_k(q + 1)
                for n in range(4):
                    if q == QP - 1:
                        for h in (2 * n, 2 * n + 1):
                            act.wait_ge(sum_ready, h + 1)
                            if h >= 2:
                                act.wait_ge(scaled, h - 1)
                            for hf, (c0, w) in enumerate(HALVES):
                                act.activation(rs[:, h % 2, c0:c0 + w], m.aux[:, 2 * (h % 2) + hf, 0:w], ACT.Sqrt, bias=m.eps[:, 0:1], scale=1.0 / P).then_inc(root_ready, 1)
                    act.wait_ge(y_mm, 4 * q + n + 1)
                    act.activation(yall[:, in_bank(n, 16 * q), :], m.acc[:, n // 2, n % 2, 0:4 * NC].rearrange("p (g n) -> p g n", g=4), ACT.Copy).then_inc(y_ev, 1)

        @block.tensor
        def _(pe):
            def first_rows(q):
                for n in range(4):
                    if q >= 1:
                        pe.wait_ge(k_ev, 4 * (q - 1) + n + 1)
                    for a in range(4):
                        g = in_bank(n).start + 2 * a
                        rows = slice(NST * (g % 2), NST * (g % 2) + NST)
                        for r in range(2):
                            mm = pe.matmul(m.aux[0:CH, n, P * a:P * a + P], bb[rows, r, PPQ * q + g // 2, :], qq[rows, q, r, g // 2, 0:CL, :].rearrange("p j c -> p (j c)"),
                                           start=(r == 0), stop=(r == 1))
                    mm.then_inc(k_mm, 1)

            first_rows(0)
            for q in range(QP):
                if q < QP - 1:
                    first_rows(q + 1)
                pe.wait_ge(ug_in, 16 * (CL + 2))
                for n in range(4):
                    if q >= 1:
                        pe.wait_ge(y_ev, 4 * (q - 1) + n + 1)
                    if q == QP - 1:
                        pe.wait_ge(k_ev, 4 * QP)
                        for h in (2 * n, 2 * n + 1):
                            pe.wait_ge(sq_ready, h + 1)
                            if h >= 2:
                                pe.wait_ge(root_ready, 2 * (h - 1))
                            for hf, (c0, w) in enumerate(HALVES):
                                mm = pe.matmul(m.aux[:, 2 * (h % 2) + hf, 0:w], m.ones[:, :], sq[:, h % 4, c0:c0 + w], start=True, stop=True)
                            mm.then_inc(sum_ready, 1)
                    if n == 0:
                        pe.wait_ge(shift_in[q % 2], 16 * CL * (q // 2 + 1))
                    for a in range(4):
                        g = in_bank(n).start + 2 * a
                        rows = slice(NST * (g % 2), NST * (g % 2) + NST)
                        o = m.acc[:, n // 2, n % 2, NC * a:NC * a + NC]
                        pe.matmul(o, tz[q % 2][:, g, :], ug[:, 16 * q + g, NS:NC + NS], start=True, stop=False)
                        for r in range(2):
                            mm = pe.matmul(o, qq[rows, q, r, g // 2, 1:9, :].rearrange("p j c -> p (j c)"), hs[rows, 0:NC, r, PPQ * q + g // 2], start=False, stop=(r == 1))
                    mm.then_inc(y_mm, 1)

        @block.vector
        def _(dve):
            ch = Chain(dve, s_v)
            dve.memset(ug[:, :, 0:NS], 0.0).then_inc(ug_zero, 1)
            dve.memset(ug[:, :, NC:NC + NS], 0.0).then_inc(ug_zero, 1)
            for q in range(QP):
                ch(dve.tensor_tensor(de[q % 2][:, :, :], dk[:, 16 * q:16 * q + 16].unsqueeze(2).broadcast_to([CH, 2 * PPQ, CH]),
                                     m.ident[0:CH, 0:CH].unsqueeze(1).broadcast_to([CH, 2 * PPQ, CH]), ALU.mult))
                dve.wait_ge(k_ev, 4 * q + 4)
                dve.tensor_tensor(km[q % 2][:, :, 0:CH], km[q % 2][:, :, 0:CH], de[q % 2][:, :, :], ALU.add).then_inc(k_d, 1)
                dve.wait_ge(k_d, q + 1)
            dve.wait_ge(gs_in, 16)
            ch(dve.tensor_scalar(gsub[:, 1:2], gsub[:, 0:1], 1.0 - LAM0, None, ALU.mult))
            for h in range(H):
                dve.wait_ge(root_ready, 2 * h + 2)
                ch(dve.reciprocal(rs[:, h % 2, :], rs[:, h % 2, :]))
                dve.scalar_tensor_tensor(m.ot[:, h, :], m.ot[:, h, :], gsub[:, 1:2], rs[:, h % 2, :], ALU.mult, ALU.mult).then_inc(scaled, 1)
            dve.wait_ge(scaled, H)


TT, TW = 5, T // 5

def norm_sums_act(m, act, src, sq, rs, sq_ready, sq_used, rt_ready):
    for k in range(KT):
        if k >= 4:
            act.wait_ge(sq_used, k - 3)
        act.activation(sq[:, k % 4, :], src[:, k, :], ACT.Square).then_inc(sq_ready, 1)
    act.wait_ge(sq_used, KT)
    for h, (c0, n) in enumerate(HALVES):
        act.activation(rs[:, c0:c0 + n], m.aux[:, h, 0:n], ACT.Sqrt, bias=m.eps[:, 0:1], scale=1.0 / D).then_inc(rt_ready, 1)

def norm_sums_pe(m, pe, sq, sq_ready, sq_used):
    for k in range(KT):
        pe.wait_ge(sq_ready, k + 1)
        for h, (c0, n) in enumerate(HALVES):
            mm = pe.matmul(m.aux[:, h, 0:n], m.ones[:, :], sq[:, k % 4, c0:c0 + n], start=(k == 0), stop=(k == KT - 1))
        mm.then_inc(sq_used, 1)

def stage_d(nc, m, ins, outs):
    at, sem = m.at, m.sem
    m.top = m.free
    ot = m.ot
    f0 = m.free
    yg = at("yg", [P, 8, T], F32, off=f0 + H * T * 4)
    sq = at("sq2", [P, 4, T], F32, off=f0 + 2 * H * T * 4)
    stg = at("stg", [P, 2, T], F32, off=f0 + 2 * H * T * 4 + 4 * T * 4)
    rs = at("rs2", [P, T], F32, off=f0 + 2 * H * T * 4 + 6 * T * 4)
    bgl = at("bgl", [P, 8], F32, off=f0 + 2 * H * T * 4 + 7 * T * 4)
    sc = m.sc = at("sc", [TW, TT, 16, P], F32, off=f0)
    keysT = at("keysT", [P, 16, P], F32, off=m.free - NPG * P * 4)
    yr = at("yr", [P, 8, T], F32, off=m.x0 + (2 * KT + 8) * T * 4)
    gh = at("gh", [P, 8, T], F32R, off=m.x0); gl = at("gl", [P, 8, T], F32R, off=m.x0 + 8 * T * 4)
    sems = {n: sem("d_" + n) for n in "cin xin keys gel gh gl ohi olo sig mixf mixh mixl sqr squ rtr hr hhr hlr qev smm sev v stx xres".split()}
    S = lambda n: sems[n]
    y_in = [sem(f"d_yin{k}") for k in range(8)]
    with nc.Block() as block:
        @block.sync
        def _(sp):
            load_y = lambda k: sp.dma_start(yr[:, k, :], m.yT[k, :, :]).then_inc(y_in[k], 16)
            load_y(0)
            for u in range(U_GLU, U_GLU + 2):
                load_unit(m, sp, u, u % 2)
            for k in range(1, 8):
                load_y(k)
            sp.dma_start(bgl[:, :], ins["b_glu"][:, :]).then_inc(S("cin"), 16)
            sp.dma_start(keysT[:, :, :], ins["keys_t"][:, :, :]).then_inc(S("keys"), 16)
            for u in range(U_GLU, U_OUT):
                load_unit(m, sp, u + 2, u % 2)
            sp.wait_ge(m.mm_done, U_OUT + 2)
            sp.wait_ge(S("gl"), 8)
            sp.dma_start(m.xt[:, :, :], ins["x_t"][:, :, :]).then_inc(S("xin"), 16)
            with sp.Fori(0, (N_OUT + N_PQ) // 2) as i:
                for s in range(2):
                    load_unit(m, sp, i * 2 + (U_OUT + s + 2), s)
            sp.wait_ge(S("xres"), N_OUT)
            sp.dma_start(m.x2[:, :, :], m.xt[:, :, :]).then_inc(S("stx"), 16)
            sp.wait_ge(S("stx"), 16)

        @block.gpsimd
        def _(pool):
            for u in range(U_GLU, U_GLU + 2):
                split_lo(m, pool, u, u % 2)
            for h in range(H):
                pool.wait_ge(S("ohi"), h + 1)
                pool.tensor_tensor(m.hl[:, h, :], ot[:, h, :], m.hh[:, h, :].bitcast(F32), ALU.subtract).then_inc(S("olo"), 1)
            for u in range(U_GLU, U_OUT):
                split_lo(m, pool, u + 2, u % 2)
            with pool.Fori(0, N_OUT // 2) as i:
                for s in range(2):
                    split_lo(m, pool, i * 2 + (U_OUT + s + 2), s)
            for k in range(KT):
                pool.wait_ge(S("hhr"), k + 1)
                pool.tensor_tensor(m.hl[:, k, :], stg[:, k % 2, :], m.hh[:, k, :].bitcast(F32), ALU.subtract).then_inc(S("hlr"), 1)
            with pool.Fori(0, N_PQ // 2) as i:
                for s in range(2):
                    split_lo(m, pool, i * 2 + (U_PQ + s + 2), s)

        @block.scalar
        def _(act):
            for k in range(8 + 1):
                if k < 8:
                    act.wait_ge(y_in[k], 16)
                    act.activation(yg[:, k, 0:NS], yr[:, k, 0:NS], ACT.Gelu_apprx_tanh)
                    act.activation(yg[:, k, NS:T].rearrange("p (n s) -> p n s", s=CL), yr[:, k, NS:T].rearrange("p (s n) -> p n s", s=CL), ACT.Gelu_apprx_tanh).then_inc(S("gel"), 1)
                if k >= 1:
                    act.wait_ge(S("gel"), k)
                    act.activation(gh[:, k - 1, :], yg[:, k - 1, :], ACT.Copy).then_inc(S("gh"), 1)
                if k == 1:
                    split_hi(m, act, U_GLU, U_GLU % 2, U_GLU // 2)
            split_hi(m, act, U_GLU + 1, (U_GLU + 1) % 2, U_GLU // 2)
            for h in range(H):
                act.activation(m.hh[:, h, :], ot[:, h, :], ACT.Copy).then_inc(S("ohi"), 1)
            for n in range(N_GLU):
                u = U_GLU + n
                act.wait_ge(m.mm_done, u + 3)
                act.wait_ge(S("cin"), 16)
                for t in range(2):
                    if n >= 1:
                        act.wait_ge(S("mixf"), 2 * n + t - 1)
                    for hf, (c0, w) in enumerate(HALVES):
                        x = act.activation(stg[:, t, c0:c0 + w], m.acc[:, t, hf, 0:w], ACT.Sigmoid, bias=bgl[:, 2 * n + t:2 * n + t + 1])
                    x.then_inc(S("sig"), 1)
                act.wait_ge(S("sig"), 2 * n + 2)
                act.sem_inc(m.acc_free, 1)
                split_hi(m, act, u + 2, u % 2, (u + 2) // 2)
                for t in range(2):
                    act.wait_ge(S("mixf"), 2 * n + t + 1)
                    act.activation(m.hh[:, 8 + 2 * n + t, :], yg[:, 2 * n + t, :], ACT.Copy).then_inc(S("mixh"), 1)
            with act.Fori(0, N_OUT // 2) as i:
                for s in range(2):
                    split_hi(m, act, i * 2 + (U_OUT + s + 2), s, i + (U_OUT // 2 + 1))
                    act.wait_ge(S("xres"), i * 2 + (s + 1))
                    act.wait_ge(S("squ"), i * 2 + (s + 1))
                    act.activation(sq[:, s, :], m.xt[:, ds(i * 2 + s, 1), :].rearrange("p a n -> p (a n)"), ACT.Square).then_inc(S("sqr"), 1)
            act.wait_ge(S("squ"), KT + 2)
            for h, (c0, n) in enumerate(HALVES):
                act.activation(rs[:, c0:c0 + n], m.aux[:, h, 0:n], ACT.Sqrt, bias=m.eps[:, 0:1], scale=1.0 / D).then_inc(S("rtr"), 1)
            for k in range(KT):
                act.wait_ge(S("hr"), k + 1)
                act.activation(m.hh[:, k, :], stg[:, k % 2, :], ACT.Copy).then_inc(S("hhr"), 1)
            with act.Fori(0, N_PQ // 2) as i:
                for s in range(2):
                    u = i * 2 + (U_PQ + s)
                    act.wait_ge(m.mm_done, u + 3)
                    act.wait_ge(S("smm"), i * 2 + (s + 1))
                    for hf, (c0, w) in enumerate(HALVES):
                        x = act.activation(stg[:, s, c0:c0 + w], m.acc[:, s, hf, 0:w], ACT.Copy)
                    x.then_inc(S("qev"), 1)
                    act.wait_ge(S("qev"), i * 2 + (s + 1))
                    act.sem_inc(m.acc_free, 1)
                    split_hi(m, act, u + 2, s, i + (U_PQ // 2 + 1))
                    if s == 1:
                        for v in range(2):
                            act.wait_ge(S("smm"), i * 2 + (v + 3))
                            act.activation(sc[:, 0:4, ds(i * 2 + v, 1), :].rearrange("p t a n -> p (t a) n"), m.aux[0:TW, 2 * v, :].rearrange("p (t n) -> p t n", t=4), ACT.Copy)
                            act.activation(sc[:, 4, ds(i * 2 + v, 1), :].rearrange("p a n -> p (a n)"), m.aux[0:TW, 2 * v + 1, 0:P], ACT.Copy).then_inc(S("sev"), 1)

        @block.tensor
        def _(pe):
            for u in range(U_GLU, U_OUT):
                s = u % 2
                pe.wait_ge(m.lo_done, u + 3)
                pe.wait_ge(m.acc_free, u + 2)
                tiles = [(t, hf) for t in range(2) for hf in range(2)]
                order = [(t, hf, k) for k in range(8) for t, hf in tiles] if u == U_GLU else [(t, hf, k) for t, hf in tiles for k in range(8)]
                for t, hf, k in order:
                            (c0, n), o = HALVES[hf], m.acc[:, t, hf, 0:HALVES[hf][1]]
                            if u == U_GLU and t == hf == 0:
                                pe.wait_ge(S("gl"), k + 1)
                            pe.matmul(o, m.wh[s][:, 2 * k + t, :], gh[:, k, c0:c0 + n], start=(k == 0), stop=False)
                            pe.matmul(o, m.wh[s][:, 2 * k + t, :], gl[:, k, c0:c0 + n], start=False, stop=False)
                            mm = pe.matmul(o, m.wl[s][:, 2 * k + t, :], gh[:, k, c0:c0 + n], start=False, stop=(k == 7))
                mm.then_inc(m.mm_done, 1)
            pe.wait_ge(S("olo"), H)
            pe.wait_ge(S("mixl"), 8)
            def add_squares(s, count, first=False, last=False):
                pe.wait_ge(S("sqr"), count)
                for h, (c0, n) in enumerate(HALVES):
                    mm = pe.matmul(m.aux[:, h, 0:n], m.ones[:, :], sq[:, s, c0:c0 + n], start=first, stop=last, skip_group_check=True)
                mm.then_inc(S("squ"), 1)

            for s in range(2):
                unit_matmuls(m, pe, U_OUT + s, s, m.hh, m.hl, s)
            add_squares(0, 1, first=True)
            with pe.Fori(0, N_OUT // 2 - 1) as i:
                for s in range(2):
                    unit_matmuls(m, pe, i * 2 + (U_OUT + s + 2), s, m.hh, m.hl, s)
                    add_squares(1 - s, i * 2 + (s + 2))
            add_squares(1, KT, last=True)
            pe.wait_ge(S("keys"), 16)
            def queries(i, first):
                for s in range(2):
                    unit_matmuls(m, pe, i * 2 + (U_PQ + s), s, m.hh, m.hl, s, wait_k=S("hlr") if first and s == 0 else None)
                for s in range(2):
                    pe.wait_ge(S("qev"), i * 2 + (s + 1))
                    pe.wait_ge(S("sev"), i * 2 + (s + 1))
                    for t in range(TT):
                        mm = pe.matmul(m.aux[0:TW, 2 * s + t // 4, P * (t % 4):P * (t % 4) + P], stg[:, s, TW * t:TW * t + TW],
                                       keysT[:, ds(i * 2 + s, 1), :].rearrange("p a n -> p (a n)"), start=True, stop=True)
                    mm.then_inc(S("smm"), 1)

            queries(0, True)
            with pe.Fori(0, N_PQ // 2 - 1) as i:
                queries(i + 1, False)

        @block.vector
        def _(dve):
            ch = Chain(dve, S("v"))
            dve.sem_inc(S("smm"), 2)
            dve.sem_inc(S("sev"), 2)
            dve.sem_inc(S("squ"), 2)
            for k in range(8):
                dve.wait_ge(S("gh"), k + 1)
                dve.tensor_tensor(gl[:, k, :], yg[:, k, :], gh[:, k, :].bitcast(F32), ALU.subtract).then_inc(S("gl"), 1)
            for t in range(8):
                dve.wait_ge(S("sig"), t + 1)
                dve.wait_ge(S("gl"), 8)
                dve.tensor_tensor(yg[:, t, :], yg[:, t, :], stg[:, t % 2, :], ALU.mult).then_inc(S("mixf"), 1)
                dve.wait_ge(S("mixh"), t + 1)
                dve.tensor_tensor(m.hl[:, 8 + t, :], yg[:, t, :], m.hh[:, 8 + t, :].bitcast(F32), ALU.subtract).then_inc(S("mixl"), 1)
            dve.wait_ge(S("xin"), 16)
            with dve.Fori(0, N_OUT // 2) as i:
                for s in range(2):
                    dve.wait_ge(m.mm_done, i * 2 + (U_OUT + s + 3))
                    for hf, (c0, n) in enumerate(HALVES):
                        x = m.xt[:, ds(i * 2 + s, 1), c0:c0 + n].rearrange("p a n -> p (a n)")
                        x = dve.tensor_tensor(x, x, m.acc[:, s, hf, 0:n], ALU.add)
                    x.then_inc(S("xres"), 1)
                    dve.wait_ge(S("xres"), i * 2 + (s + 1))
                    dve.sem_inc(m.acc_free, 1)
            dve.wait_ge(S("rtr"), 2)
            ch(dve.reciprocal(rs[:, :], rs[:, :]))
            for k in range(KT):
                if k >= 2:
                    dve.wait_ge(S("hlr"), k - 1)
                dve.scalar_tensor_tensor(stg[:, k % 2, :], m.xt[:, k, :], m.gains[:, 1, k:k + 1], rs[:, :], ALU.mult, ALU.mult).then_inc(S("hr"), 1)


TK = 16
HK = H * TK
NB, BW = 13, T // 13
NEG = -3.0e38
GRP, NG = 4, 32

def stage_e(nc, m, ins, outs):
    at, sem = m.at, m.sem
    f0 = m.free
    at_ = lambda n, s, d=F32: at(n, s, d)
    m.top = m.x0
    sct = at("sct", [TW, 16, P]); cand = at("cand", [TW, H, TK, TK]); eq = at("eq", [TW, HK, TK])
    assert m.end <= m.x0 + KT * T * 4
    m.top = f0 - NPG * P * 4
    wk = at("wk", [TW, 2, 256]); vals = at("vals", [TW, 16, TK]); idx = at("idx", [TW, 16, TK], U32); idf = at("idf", [TW, 16, TK])
    tv = at("tv", [TW, H, TK])
    assert m.end <= f0, (m.end, f0)
    sc = m.sc
    gs = [at(f"gs{j}", [P, P, BW], F32, off=f0 + j * P * BW * 4) for j in range(2)]
    m.top = f0 + 2 * P * BW * 4
    tp = at("tp", [TW, H, TK], U32); tpa = at("tpa", [TW, H, TK], U32); pf = at("pf", [TW, HK])
    gx = at("gx", [TW, 3, HK]); sm = at("esm", [TW, 2, H]); iota = at("iota", [P, P]); gt = at("gt", [P, 3, T])
    m.top = m.x0
    at("skip", [P, 3, 2048]) if False else None
    o2 = at("o2", [P, 8, P], F32, off=m.x0); og = at("og", [P, 8, P], F32, off=m.x0 + 4096); gts = at("gts", [P, 2, 3, BW], F32, off=m.x0 + 8192)
    m.top = m.x0 + 3 * 8192
    ast = at("ast", [P, 2, T])
    assert m.end <= m.x0 + KT * T * 4
    S = {n: sem("e_" + n) for n in "cin scv gel st0 st1 exp tvd gx gtr gev v gts o2r ogr omm oev gst0 gst1 ofree".split()}
    st, gst = [S["st0"], S["st1"]], [S["gst0"], S["gst1"]]
    PA, UA = TT, 8
    PB, UB = NB, 4
    UC = N_EXP - PA * UA - PB * UB
    B0 = U_EXP_U + PA * UA
    C0 = B0 + PB * UB
    PC = UC // 2
    TPU = BW // UB
    gD, aD = m.gD, m.aD
    with nc.Block() as block:
        @block.sync
        def _(sp):
            sp.dma_start(iota[:, :], ins["iota"][:, :]).then_inc(S["cin"], 16)
            for x in ("gx", "ofree", "gev", "gtr", "oev"):
                sp.sem_inc(S[x], 1)
            sp.sem_inc(S["omm"], 4)
            sp.sem_inc(st[0], 16); sp.sem_inc(st[1], 16); sp.sem_inc(gst[0], 16); sp.sem_inc(gst[1], 16)
            with sp.Fori(0, N_EXP // 2) as i:
                for s in range(2):
                    load_unit(m, sp, i * 2 + (U_EXP_U + s + 2), s)

        @block.gpsimd
        def _(pool):
            def los(n, first, turns):
                with pool.Fori(0, turns) as i:
                    for k in range(n):
                        split_lo(m, pool, i * n + (first + k + 2), k % 2)
            los(UA, U_EXP_U, PA)
            los(UB, B0, PB)
            los(2, C0, PC)

        @block.scalar
        def _(act):
            def take(u, s, e, row, done):
                act.wait_ge(m.mm_done, u + 3)
                act.wait_ge(st[s], row * 16 + 16)
                for hf, (c0, w) in enumerate(HALVES):
                    x = act.activation(ast[:, s, c0:c0 + w], m.acc[:, s, hf, 0:w], ACT.Gelu_apprx_tanh)
                x.then_inc(S["gel"], 1)
                act.wait_ge(S["gel"], done)
                act.sem_inc(m.acc_free, 1)
                act.dma_start(aD[ds(e, 1), :, :].rearrange("a p n -> (a p) n"), ast[:, s, :]).then_inc(st[s], 16)

            with act.Fori(0, PA) as i:
                act.wait_ge(S["gx"], i + 1)
                act.activation(sct[:, :, :], sc[:, ds(i, 1), :, :].rearrange("p a b c -> p (a b) c"), ACT.Copy).then_inc(S["scv"], 1)
                for n in range(UA):
                    u = i * UA + (U_EXP_U + n)
                    if n == UA - 1:
                        act.wait_ge(S["tvd"], i + 1)
                        act.activation(tv[:, :, :], tv[:, :, :], ACT.Exp).then_inc(S["exp"], 1)
                    take(u, n % 2, i * UA + n, i * (UA // 2) + n // 2, i * UA + (n + 1))
                    split_hi(m, act, u + 2, n % 2, i * (UA // 2) + (U_EXP_U // 2 + n // 2 + 1))
                act.wait_ge(S["gtr"], i + 2)
                act.activation(gt[:, :, :].rearrange("p x (t n) -> p t x n", t=TT)[:, ds(i, 1), :, :].rearrange("p a x n -> p (a x) n"),
                               m.aux[:, 0, 0:3 * TW].rearrange("p (x n) -> p x n", x=3), ACT.Copy).then_inc(S["gev"], 1)
            with act.Fori(0, PB) as i:
                act.wait_ge(S["gev"], TT + 1)
                act.wait_ge(S["ofree"], i + 1)
                act.activation(gts[:, 0, :, :], gt[:, :, :].rearrange("p x (t n) -> p t x n", t=NB)[:, ds(i, 1), :, :].rearrange("p a x n -> p (a x) n"), ACT.Copy).then_inc(S["gts"], 1)
                for n in range(UB):
                    u = i * UB + (B0 + n)
                    take(u, n % 2, i * UB + (PA * UA + n), i * (UB // 2) + (PA * UA // 2 + n // 2), i * UB + (PA * UA + n + 1))
                    split_hi(m, act, u + 2, n % 2, i * (UB // 2) + (B0 // 2 + n // 2 + 1))
                act.wait_ge(S["oev"], i * (BW // 4) + (BW // 4 + 1))
                act.dma_start(gD[ds(i, 1), :, :, :].rearrange("a p e n -> (a p) (e n)"), gs[0][:, :, :].rearrange("p e n -> p (e n)")).then_inc(gst[0], 16)
            with act.Fori(0, PC) as i:
                for n in range(2):
                    u = i * 2 + (C0 + n)
                    take(u, n, i * 2 + (C0 - U_EXP_U + n), i + ((C0 - U_EXP_U) // 2), i * 2 + (C0 - U_EXP_U + n + 1))
                    split_hi(m, act, u + 2, n, i + (C0 // 2 + 1))
            for s in range(2):
                act.wait_ge(st[s], 16 + 16 * N_EXP // 2)
            act.wait_ge(gst[0], 16 + 16 * NB)

        @block.tensor
        def _(pe):
            with pe.Fori(0, PA) as i:
                for n in range(UA):
                    unit_matmuls(m, pe, i * UA + (U_EXP_U + n), n % 2, m.hh, m.hl, n % 2)
                pe.wait_ge(S["gx"], i + 2)
                pe.wait_ge(S["gev"], i + 1)
                for x in range(3):
                    mm = pe.transpose(m.aux[:, 0, TW * x:TW * x + TW], gx[:, x, :], m.ident[0:TW, 0:TW])
                mm.then_inc(S["gtr"], 1)
            with pe.Fori(0, PB) as i:
                for n in range(UB):
                    unit_matmuls(m, pe, i * UB + (B0 + n), n % 2, m.hh, m.hl, n % 2)
                    for k in range(TPU):
                        t = n * TPU + k
                        pe.wait_ge(S["o2r"], i * BW + (t + 1))
                        pe.wait_ge(S["ogr"], i * BW + (t + 1))
                        if t % 4 == 0:
                            pe.wait_ge(S["oev"], i * (BW // 4) + max(t // 4, 1))
                        mm = pe.matmul(m.aux[:, 1 + (t // 4) % 2, P * (t % 4):P * (t % 4) + P], o2[:, t % 8, :], og[:, t % 8, :], start=True, stop=True)
                        mm.then_inc(S["omm"], 1)
            with pe.Fori(0, PC) as i:
                for n in range(2):
                    unit_matmuls(m, pe, i * 2 + (C0 + n), n, m.hh, m.hl, n)

        @block.vector
        def _(dve):
            ch = Chain(dve, S["v"])
            dve.wait_ge(S["cin"], 16)
            with dve.Fori(0, PA) as i:
                ch = Chain(dve, S["v"])
                dve.wait_ge(S["scv"], i + 1)
                ch(dve.memset(sm[:, :, :], 0.0))
                for c in range(16):
                    w = wk[:, c % 2, 0:P]
                    ch(dve.max(vals[:, c, 0:8], sct[:, c, :]))
                    ch(dve.max_index(idx[:, c, 0:8], vals[:, c, 0:8], sct[:, c, :]))
                    ch(dve.match_replace(w, vals[:, c, 0:8], sct[:, c, :], NEG))
                    ch(dve.max(vals[:, c, 8:16], w))
                    ch(dve.max_index(idx[:, c, 8:16], vals[:, c, 8:16], w))
                ch(dve.tensor_copy(idf[:, :, :], idx[:, :, :]))
                v = vals[:, :, :].rearrange("p (h c) k -> p h c k", c=2)
                ch(dve.tensor_tensor(cand[:, :, :, :], v[:, :, 0, :].unsqueeze(3).broadcast_to([TW, H, TK, TK]), v[:, :, 1, :].unsqueeze(2).broadcast_to([TW, H, TK, TK]), ALU.add))
                for h in range(H):
                    cd = cand[:, h, :, :].rearrange("p a b -> p (a b)")
                    w = wk[:, h % 2, :]
                    ch(dve.max(tv[:, h, 0:8], cd))
                    ch(dve.max_index(tp[:, h, 0:8], tv[:, h, 0:8], cd))
                    ch(dve.match_replace(w, tv[:, h, 0:8], cd, NEG))
                    ch(dve.max(tv[:, h, 8:16], w))
                    ch(dve.max_index(tp[:, h, 8:16], tv[:, h, 8:16], w))
                ch(dve.tensor_copy(sm[:, 0, :], tv[:, :, 0]))
                dve.tensor_tensor(tv[:, :, :], tv[:, :, :], sm[:, 0, :].unsqueeze(2).broadcast_to([TW, H, TK]), ALU.subtract).then_inc(S["tvd"], 1)
                il = idf[:, :, :].rearrange("p (h c) k -> p h c k", c=2)
                dve.wait_ge(S["gtr"], i + 1)
                for c in range(2):
                    if c == 0:
                        ch(dve.tensor_scalar(tpa[:, :, :], tp[:, :, :], 4, None, ALU.logical_shift_right))
                    else:
                        ch(dve.tensor_scalar(tpa[:, :, :], tp[:, :, :], 15, None, ALU.bitwise_and))
                    ch(dve.tensor_copy(pf[:, :], tpa[:, :, :].rearrange("p h k -> p (h k)")))
                    ch(dve.tensor_tensor(eq[:, :, :], pf[:, :].unsqueeze(2).broadcast_to([TW, HK, TK]), iota[0:TW, 0:TK].unsqueeze(1).broadcast_to([TW, HK, TK]), ALU.is_equal))
                    e4 = eq[:, :, :].rearrange("p (h k) j -> p h k j", h=H)
                    ch(dve.tensor_tensor(e4, e4, il[:, :, c, :].unsqueeze(2).broadcast_to([TW, H, TK, TK]), ALU.mult))
                    ch(dve.tensor_reduce(gx[:, 1 + c, :], eq[:, :, :], AX.X, ALU.add))
                dve.wait_ge(S["exp"], i + 1)
                ch(dve.tensor_reduce(sm[:, 0, :], tv[:, :, :], AX.X, ALU.add))
                ch(dve.reciprocal(sm[:, 1, :], sm[:, 0, :]))
                ch(dve.tensor_tensor(gx[:, 0, :].rearrange("p (h k) -> p h k", h=H), tv[:, :, :], sm[:, 1, :].unsqueeze(2).broadcast_to([TW, H, TK]), ALU.mult))
                dve.sem_inc(S["gx"], 1)
                dve.sem_clear(S["v"])
            with dve.Fori(0, PB) as i:
                dve.wait_ge(S["gts"], i + 1)
                def spread(g):
                    dve.wait_ge(S["omm"], i * BW + (4 * g + 8))
                    if g == 0:
                        dve.wait_ge(gst[0], i * 16 + 16)
                    dve.tensor_copy(gs[0][:, :, 4 * g:4 * g + 4].rearrange("p e t -> p t e"), m.aux[:, 1 + g % 2, :].rearrange("p (t e) -> p t e", t=4)).then_inc(S["oev"], 1)
                for t in range(BW):
                    if t % 4 == 0:
                        dve.wait_ge(S["omm"], i * BW + t)
                    dve.tensor_scalar(o2[:, t % 8, :], iota[:, :], gts[:, 0, 2, t:t + 1], None, ALU.is_equal).then_inc(S["o2r"], 1)
                    dve.tensor_scalar(og[:, t % 8, :], iota[:, :], gts[:, 0, 1, t:t + 1], gts[:, 0, 0, t:t + 1], ALU.is_equal, ALU.mult).then_inc(S["ogr"], 1)
                    if t % 4 == 3 and t >= 7:
                        spread(t // 4 - 1)
                spread(BW // 4 - 1)
                dve.wait_ge(S["ogr"], i * BW + BW)
                dve.sem_inc(S["ofree"], 1)

def stage_f(nc, m, ins, outs):
    at, sem = m.at, m.sem
    b = m.x0 + KT * T * 4
    SZ = GRP * T * 4
    a4 = [at(f"a4{s}", [P, GRP, T], F32, off=b + s * SZ) for s in range(2)]
    g4 = [at(f"g4{s}", [P, NB, GRP, BW], F32, off=b + (2 + s) * SZ) for s in range(2)]
    vh = [at(f"vh{s}", [P, GRP, T], F32R, off=b + (4 + s) * SZ) for s in range(2)]
    vl = [at(f"vl{s}", [P, GRP, T], F32R, off=b + (6 + s) * SZ) for s in range(2)]
    m.top = m.free
    sq = at("sq3", [P, 4, T]); rs = at("rs3", [P, T])
    S = {n: sem("g_" + n) for n in "xin ain0 ain1 gin0 gin1 w wh wl mmd macc v sqr squ rtr xf st".split()}
    ain, gin = [S["ain0"], S["ain1"]], [S["gin0"], S["gin1"]]
    with nc.Block() as block:
        def turn_loads(sp, i, last):
            for gg in range(2):
                g = i * 2 + gg
                if last is not None:
                    pass
                for n in range(4):
                    if last and gg == 1 and n >= 2:
                        continue
                    load_unit(m, sp, i * 8 + (U_EXP_V + 4 * gg + n + 2), n % 2)
                    if n == 1 and not (last and gg == 1):
                        loads_ag(sp, g + 1, 1 - gg, i + (1 if gg == 1 else 0))

        def loads_ag(sp, g, s, pair):
            sp.wait_ge(S["v"], g * 16 - 15)
            sp.dma_start(a4[s][:, :, :], m.aD[ds(g * GRP, GRP), :, :].rearrange("e p n -> p e n")).then_inc(ain[s], 16)
            sp.dma_start(g4[s][:, :, :, :].rearrange("p b e n -> p b (e n)"), m.gD[:, :, ds(g * GRP, GRP), :].rearrange("b p e n -> p b (e n)")).then_inc(gin[s], 16)

        @block.sync
        def _(sp):
            sp.dma_start(m.xt[:, :, :], m.x2[:, :, :]).then_inc(S["xin"], 16)
            sp.dma_start(a4[0][:, :, :], m.aD[0:GRP, :, :].rearrange("e p n -> p e n")).then_inc(ain[0], 16)
            sp.dma_start(g4[0][:, :, :, :].rearrange("p b e n -> p b (e n)"), m.gD[:, :, 0:GRP, :].rearrange("b p e n -> p b (e n)")).then_inc(gin[0], 16)
            with sp.Fori(0, NG // 2 - 1) as i:
                turn_loads(sp, i, False)
            turn_loads(sp, NG // 2 - 1, True)
            for k in range(KT):
                sp.wait_ge(S["xf"], k + 1)
                sp.dma_start(outs["y_t"][:, k, :], m.xt[:, k, :]).then_inc(S["st"], 16)
            sp.wait_ge(S["st"], 16 * KT)

        @block.gpsimd
        def _(pool):
            def turn(i, last):
                for n in range(6 if last else 8):
                    split_lo(m, pool, i * 8 + (U_EXP_V + n + 2), n % 2)
            with pool.Fori(0, NG // 2 - 1) as i:
                turn(i, False)
            turn(NG // 2 - 1, True)

        @block.scalar
        def _(act):
            def w_hi(g, s, first=False):
                act.wait_ge(S["w"], g + 1)
                if not first:
                    act.wait_ge(S["v"], g * 16 - 15)
                act.activation(vh[s][:, :, :], a4[s][:, :, :], ACT.Copy).then_inc(S["wh"], 1)
            w_hi(0, 0, True)
            def turn(i, last):
                for gg in range(2):
                    for n in range(4):
                        if not (last and gg == 1 and n >= 2):
                            split_hi(m, act, i * 8 + (U_EXP_V + 4 * gg + n + 2), n % 2, i * 4 + (U_EXP_V // 2 + 2 * gg + n // 2 + 1),
                                     (S["v"], i * 32 + (16 * gg + 4 * n + 4)))
                        if n == 1 and not (last and gg == 1):
                            w_hi(i * 2 + (gg + 1), 1 - gg)
            with act.Fori(0, NG // 2 - 1) as i:
                turn(i, False)
            turn(NG // 2 - 1, True)
            act.wait_ge(S["macc"], 2 + 16 * NG)
            norm_sums_act(m, act, m.xt, sq, rs, S["sqr"], S["squ"], S["rtr"])

        @block.tensor
        def _(pe):
            def turn(i):
                for gg in range(2):
                    g = i * 2 + gg
                    pe.wait_ge(S["wl"], g + 1)
                    for n in range(4):
                        u = i * 8 + (U_EXP_V + 4 * gg + n)
                        s = n % 2
                        pe.wait_ge(m.lo_done, u + 3)
                        for d in range(4):
                            r = i * 32 + (16 * gg + 4 * n + d)
                            pe.wait_ge(S["macc"], r + 1)
                            for hf, (c0, w) in enumerate(HALVES):
                                o = m.acc[:, d % 2, hf, 0:w]
                                for e in range(GRP):
                                    pe.matmul(o, m.wh[s][:, 4 * e + d, :], vh[gg][:, e, c0:c0 + w], start=(e == 0), stop=False)
                                    pe.matmul(o, m.wh[s][:, 4 * e + d, :], vl[gg][:, e, c0:c0 + w], start=False, stop=False)
                                    mm = pe.matmul(o, m.wl[s][:, 4 * e + d, :], vh[gg][:, e, c0:c0 + w], start=False, stop=(e == GRP - 1))
                            mm.then_inc(S["v"], 1)
            with pe.Fori(0, NG // 2) as i:
                turn(i)
            norm_sums_pe(m, pe, sq, S["sqr"], S["squ"])

        @block.vector
        def _(dve):
            dve.sem_inc(S["macc"], 2)
            def weigh(g, s, pair):
                dve.wait_ge(ain[s], pair * 16 + 16)
                dve.wait_ge(gin[s], pair * 16 + 16)
                a = a4[s][:, :, :].rearrange("p e (b n) -> p e b n", b=NB)
                dve.tensor_tensor(a, a, g4[s][:, :, :, :].rearrange("p b e n -> p e b n"), ALU.mult).then_inc(S["w"], 1)
            def low(g, s):
                dve.wait_ge(S["wh"], g + 1)
                dve.tensor_tensor(vl[s][:, :, :], a4[s][:, :, :], vh[s][:, :, :].bitcast(F32), ALU.subtract).then_inc(S["wl"], 1)
            weigh(0, 0, 0)
            low(0, 0)
            dve.wait_ge(S["xin"], 16)
            def turn(i, last):
                for gg in range(2):
                    more = not (last and gg == 1)
                    for n in range(4):
                        for d in range(4):
                            r = i * 32 + (16 * gg + 4 * n + d)
                            dve.wait_ge(S["v"], r + 1)
                            for hf, (c0, w) in enumerate(HALVES):
                                x = m.xt[:, 4 * n + d, c0:c0 + w]
                                x = dve.tensor_tensor(x, x, m.acc[:, d % 2, hf, 0:w], ALU.add)
                            x.then_inc(S["macc"], 1)
                        if n == 1 and more:
                            weigh(i * 2 + (gg + 1), 1 - gg, i + (1 if gg == 1 else 0))
                        if n == 2 and more:
                            low(i * 2 + (gg + 1), 1 - gg)
            with dve.Fori(0, NG // 2 - 1) as i:
                turn(i, False)
            turn(NG // 2 - 1, True)
            dve.wait_ge(S["rtr"], 2)
            dve.reciprocal(rs[:, :], rs[:, :]).then_inc(S["v"], 1)
            dve.wait_ge(S["v"], 16 * NG + 1)
            for k in range(KT):
                dve.wait_ge(S["squ"], KT)
                dve.scalar_tensor_tensor(m.xt[:, k, :], m.xt[:, k, :], m.gains[:, 2, k:k + 1], rs[:, :], ALU.mult, ALU.mult).then_inc(S["xf"], 1)


def program(nc, ins, outs):
    with ExitStack() as ctx:
        m = common(nc, ctx, ins, outs)
        dram = lambda n, s: nc.dram_tensor(n, s, F32).ap()
        m.qT, m.uT, m.yT = (dram(n, [8, P, T]) for n in ("q_rows", "u_rows", "y_rows"))
        m.kT, m.vT = outs["k_t"], outs["v_t"]
        m.x2 = dram("x_mid", [P, KT, T])
        m.aD = dram("expert_acts", [P, P, T])
        m.gD = dram("expert_gates", [NB, P, P, BW])
        for stage in (stage_a, stage_p1, stage_l1, stage_p3, stage_d, stage_e, stage_f):
            own = []

            def new(name):
                own.append(nc.alloc_semaphore(name))
                return own[-1]

            m.sem = new
            stage(nc, m, ins, outs)
            nc.clear_and_free_semaphores(own)
            nc.all_engine_barrier()


def _units(w, width):
    k, n = w.shape
    return w.reshape(k // P, P, n // width, width).transpose(2, 1, 0, 3).reshape(n // width, P, -1)


def _states(a):
    rest = a.shape[2:]
    return a.reshape(GP, 2, NST, *rest).transpose(1, 2, 0, *range(3, 3 + len(rest))).reshape(P, GP, *rest)


def _cols(a):
    return a.reshape(-1, P).T


def _constants():
    c = {"ident": np.eye(P), "ones": np.ones((P, P)), "eps": np.full((P, 1), EPS), "iota": np.tile(np.arange(P), (P, 1))}
    rot = np.zeros((P, P))
    for b in (0, 64):
        for j in range(32):
            rot[b + 32 + j, b + j], rot[b + j, b + 32 + j] = -1, 1
    c["rot"] = rot
    f = np.float32
    inv = f(1.0) / (f(10000.0) ** (np.arange(32, dtype=f) * f(2) / f(64)))
    pos = np.concatenate([np.full(NS, PAST), np.arange(NT)]).astype(f)
    ang = (pos[None, :] * np.tile(inv, 4)[:, None]).astype(f)
    c["cos_t"], c["sin_t"] = np.cos(ang), np.sin(ang)
    c["dmask"] = np.concatenate([np.eye(64), np.eye(64)])
    c["cmask"] = np.kron(np.eye(2), np.ones((64, 1)))
    c["cmask4"] = np.concatenate([c["cmask"], -c["cmask"]], 1)
    c["causal"] = np.where(np.arange(P)[:, None] >= np.arange(P)[None, :], 0, -1e30)
    return {n: np.ascontiguousarray(a, dtype=f) for n, a in c.items()}


_OUTS = {"k_t": (8, P, T), "v_t": (8, P, T), "ssm_prompt": (P, 2, GP), "ssm_sample": (P, NS, 2, GP), "y_t": (P, KT, T)}


def kernel(x_prompt, x_sample, cache_k, cache_v, state_ssm_re, state_ssm_im, page_table,
           g_mix, w_in, lambda_q1, lambda_k1, lambda_q2, lambda_k2, g_sub,
           ssm_a_re, ssm_a_im, ssm_log_dt, ssm_b_re, ssm_b_im, ssm_c_re, ssm_c_im, ssm_d,
           w_glu, b_glu, w_out, g_ffn, peer_w_q, peer_sub_keys, peer_u, peer_v, g_final):
    import concourse.bacc as _bacc
    from concourse.bass_utils import run_bass_kernel_spmd as _run

    order = list(range(8)) + [8 + 8 * j + n for n in range(8) for j in range(3)]
    experts = peer_u[0].reshape(P, P, KT, P).transpose(0, 3, 2, 1).reshape(P, P, D)
    values = peer_v[0].reshape(NG, GRP, P, 4, 512).transpose(0, 3, 2, 1, 4).reshape(P, P, D)
    arrays = {
        "x_t": np.concatenate([x_sample[:, 0], x_prompt[0]]).T.reshape(KT, P, T).transpose(1, 0, 2),
        "gains": np.stack([_cols(g_mix[0]), _cols(g_ffn[0]), _cols(g_final)], 1),
        "units": np.concatenate([_units(w_in[0], P)[order], _units(w_glu[0], 2 * P), _units(w_out[0], P), _units(peer_w_q[0], P), experts, values]),
        "page_table": page_table.reshape(1, P),
        "cache_k": cache_k[0].reshape(-1, PAGE, H * P), "cache_v": cache_v[0].reshape(-1, PAGE, H * P),
        "lambdas": np.stack([lambda_q1[0], lambda_k1[0], lambda_q2[0], lambda_k2[0]]),
        "a_re": _states(ssm_a_re[0]), "a_im": _states(ssm_a_im[0]),
        "log_dt": _states(np.repeat(ssm_log_dt[0][:, None], NST, 1)),
        "b_re": _states(ssm_b_re[0]), "b_im": _states(ssm_b_im[0]),
        "c_re": _states(ssm_c_re[0].transpose(0, 2, 1)), "c_im": _states(ssm_c_im[0].transpose(0, 2, 1)),
        "h0_re": _states(state_ssm_re[0].transpose(1, 2, 0)).transpose(0, 2, 1),
        "h0_im": _states(state_ssm_im[0].transpose(1, 2, 0)).transpose(0, 2, 1),
        "d_t": ssm_d[0].T, "b_glu": _cols(b_glu[0]), "g_sub": g_sub[0].reshape(P, 1),
        "keys_t": peer_sub_keys[0].reshape(16, P, P).transpose(2, 0, 1),
        **_constants(),
    }
    arrays = {n: np.ascontiguousarray(a) for n, a in arrays.items()}
    nc = _bacc.Bacc("TRN2", target_bir_lowering=False, num_devices=1)
    ins = {n: nc.dram_tensor(n, a.shape, mybir.dt.from_np(a.dtype), kind="ExternalInput").ap() for n, a in arrays.items()}
    outs = {n: nc.dram_tensor(n, s, F32, kind="ExternalOutput").ap() for n, s in _OUTS.items()}
    program(nc, ins, outs)
    r = _run(nc, [arrays], core_ids=[0]).results[0]

    y = r["y_t"].transpose(2, 1, 0).reshape(T, D)
    k, v = (r[n].transpose(2, 0, 1) for n in ("k_t", "v_t"))
    hp = r["ssm_prompt"].reshape(2, NST, 2, GP).transpose(2, 3, 0, 1).reshape(2, 1, 1, G, NST)
    hs = r["ssm_sample"].reshape(2, NST, NS, 2, GP).transpose(3, 2, 4, 0, 1).reshape(2, 1, NS, G, NST)
    c = np.ascontiguousarray
    return (c(y[None, NS:]), c(y[:NS, None]), c(k[None, None, NS:]), c(v[None, None, NS:]), c(hp[0]), c(hp[1]),
            c(k[None, :NS, None]), c(v[None, :NS, None]), c(hs[0]), c(hs[1]))
```

```python
from contextlib import ExitStack

import math
import numpy as np

import concourse.bass as bass
from concourse import mybir

F32 = mybir.dt.float32
F32R = mybir.dt.float32r
I32 = mybir.dt.int32
U32 = mybir.dt.uint32
ALU = mybir.AluOpType
ACT = mybir.ActivationFunctionType
AX = mybir.AxisListType
ds = bass.ds

P = 128
D = 2048
KT = D // P
NS, NT = 8, 512
T = NS + NT
HALVES = ((0, 264), (264, 256))
H = 8
PAST, PAGE = 2048, 128
NPG = PAST // PAGE
N_IN, N_GLU, N_OUT, N_PQ, N_EXP = 32, 4, 16, 16, 128
U_GLU = N_IN
U_OUT = U_GLU + N_GLU
U_PQ = U_OUT + N_OUT
U_EXP_U = U_PQ + N_PQ
U_EXP_V = U_EXP_U + N_EXP
N_UNITS = U_EXP_V + N_EXP
EPS = 1e-6
G = 64
GP = G // 2
CH, NST = 16, 64
CL = 8
NCH = NT // CL
LAM0 = 0.2


class Chain:

    def __init__(self, eng, sem):
        self.eng, self.sem, self.base, self.n = eng, sem, 0, 0

    def __call__(self, ins):
        self.n += 1
        ins.then_inc(self.sem, 1)
        self.eng.wait_ge(self.sem, self.base + self.n)

    def enter(self, i, per):
        self.outer, self.per = self.base + self.n, per
        self.base, self.n = self.outer + i * per, 0

    def leave(self, turns):
        assert self.n == self.per, (self.n, self.per)
        self.base, self.n = self.outer + turns * self.per, 0


def common(nc, ctx, ins, outs):
    class K: pass
    m = K()
    base = (nc.sbuf_base + 63) // 64 * 64
    m.top = base
    def at(name, shape, dt=F32, off=None):
        size = int(np.prod(shape[1:])) * 4
        size = (size + 31) // 32 * 32
        if off is None:
            off = m.top = (m.top + 31) // 32 * 32
            m.top += size
        assert off + size <= nc.sbuf_usable_end, (name, off, size, nc.sbuf_usable_end)
        t = nc.alloc_sbuf_tensor_at(name, shape, dt, offset=off)
        m.end = off + size
        return t
    m.at = at
    m.sem = lambda n: ctx.enter_context(nc.semaphore(n))
    m.ident = at("ident", [P, P]); m.ones = at("ones", [P, P]); m.rot = at("rot", [P, P])
    m.gains = at("gains", [P, 3, KT]); m.eps = at("eps", [P, 1]); m.pages = at("pages", [1, P], I32); m.lam = at("lam", [P, 8])
    m.qs = at("qs", [P, H, NS])
    m.x0 = m.top
    m.xt = at("xt", [P, KT, T]); m.hh = at("hh", [P, KT, T], F32R); m.hl = at("hl", [P, KT, T], F32R)
    m.raw = [at(f"raw{s}", [P, KT, P]) for s in range(2)]
    m.wh = [at(f"wh{s}", [P, KT, P], F32R) for s in range(2)]
    m.wl = [at(f"wl{s}", [P, KT, P], F32R) for s in range(2)]
    m.scd = at("scd", [P, NPG, P])
    m.free = m.top
    m.acc = ctx.enter_context(nc.psum_tensor("acc", [P, 2, 2, 512], F32))
    m.aux = ctx.enter_context(nc.psum_tensor("aux", [P, 4, 512], F32))
    m.raw_in = [m.sem(f"raw_in{s}") for s in range(2)]
    m.hi_done = m.sem("hi_done"); m.lo_done = m.sem("lo_done"); m.mm_done = m.sem("mm_done"); m.acc_free = m.sem("acc_free")
    m.units = ins["units"]
    return m

def load_unit(m, sp, u, s):
    sp.wait_ge(m.lo_done, u + 1)
    sp.dma_start(m.raw[s][:, :, :].rearrange("p k n -> p (k n)"), m.units[ds(u, 1), :, :].rearrange("a p n -> (a p) n")).then_inc(m.raw_in[s], 16)

def split_hi(m, act, u, s, pair, used=None):
    act.wait_ge(m.raw_in[s], pair * 16 + 16)
    act.wait_ge(*(used or (m.mm_done, u + 1)))
    act.activation(m.wh[s][:, :, :], m.raw[s][:, :, :], ACT.Copy).then_inc(m.hi_done, 1)

def split_lo(m, pool, u, s):
    pool.wait_ge(m.hi_done, u + 1)
    pool.tensor_tensor(m.wl[s][:, :, :], m.raw[s][:, :, :], m.wh[s][:, :, :].bitcast(F32), ALU.subtract).then_inc(m.lo_done, 1)

def unit_matmuls(m, pe, u, s, rhs_hi, rhs_lo, acc_slot, k_range=range(KT), first=True, wait_k=None, out=None):
    pe.wait_ge(m.lo_done, u + 3)
    pe.wait_ge(m.acc_free, u + 1)
    if wait_k is None:
        order = [(h, k) for h in range(2) for k in k_range]
    else:
        order = [(h, k) for k in k_range for h in range(2)]
    k_range = list(k_range)
    for h, k in order:
        if wait_k is not None and h == 0:
            pe.wait_ge(wait_k, k + 1)
        c0, n = HALVES[h]
        o = m.acc[:, acc_slot, h, 0:n]
        pe.matmul(o, m.wh[s][:, k, :], rhs_hi[:, k, c0:c0 + n], start=(k == k_range[0]), stop=False)
        pe.matmul(o, m.wh[s][:, k, :], rhs_lo[:, k, c0:c0 + n], start=False, stop=False)
        mm = pe.matmul(o, m.wl[s][:, k, :], rhs_hi[:, k, c0:c0 + n], start=False, stop=(k == k_range[-1]))
    mm.then_inc(m.mm_done, 1)

def halves_copy(eng_op, out, m, slot):
    for h, (c0, n) in enumerate(HALVES):
        ins = eng_op(out[:, c0:c0 + n], m.acc[:, slot, h, 0:n])
    return ins

def stage_a(nc, m, ins, outs):
    at, sem = m.at, m.sem
    m.top = m.free
    cosT = at("cosT", [P, T]); sinT = at("sinT", [P, T])
    zst = [at(f"zst{j}", [P, T]) for j in range(3)]
    zo = [at(f"zo{j}", [P, T]) for j in range(2)]
    t1 = at("t1", [P, T]); t2 = at("t2", [P, T])
    kring = at("kring", [P, 4, 1024]); sq = at("sq", [P, 4, T], F32, off=m.top - 4 * 4096)
    prod = [at(f"prod{j}", [P, 1024]) for j in range(3)]; rs = at("rs", [P, T])
    qb = at("qb", [P, NS, 1024], F32, off=m.x0)
    c_in, x_in = sem("c_in"), [sem(f"x_in{j}") for j in range(4)]
    sq_ready, sq_used = sem("sq_ready"), sem("sq_used")
    rt_ready, h_ready, hh_ready, hl_ready = sem("rt_ready"), sem("h_ready"), sem("hh_ready"), sem("hl_ready")
    z_ready = sem("z_ready")
    rope_done, rot_ready, rot_free = sem("rope_done"), sem("rot_ready"), sem("rot_free")
    st_zo = [sem(f"st_zo{j}") for j in range(2)]; st_v, st_u, st_k = sem("st_v"), sem("st_u"), sem("st_k")
    qs_done, qb_mm, qb_ready = sem("qs_done"), sem("qb_mm"), sem("qb_ready")
    kp_in, kv_used, kg_used = [sem(f"kp_in{j}") for j in range(4)], sem("kv_used"), sem("kg_used")
    scored, turn_taken = sem("scored"), sem("turn_taken")
    s_v = sem("s_v")
    qT, kT, vT, uT = m.qT, m.kT, m.vT, m.uT
    keys = ins["cache_k"]
    PQ = 4
    PM = 4
    with nc.Block() as block:
        @block.sync
        def _(sp):
            for j in range(4):
                sp.dma_start(m.xt[:, 4 * j:4 * j + 4, :], ins["x_t"][:, 4 * j:4 * j + 4, :]).then_inc(x_in[j], 16)
            for a, b in ((m.ident, "ident"), (m.ones, "ones"), (m.rot, "rot"), (cosT, "cos_t"), (sinT, "sin_t"), (m.gains, "gains"), (m.pages, "page_table"), (m.eps, "eps")):
                sp.dma_start(a[:], ins[b][:]).then_inc(c_in, 16)
            for u in range(2):
                load_unit(m, sp, u, u)
            with sp.Fori(0, PQ) as i:
                for s in range(2):
                    load_unit(m, sp, i * 2 + (s + 2), s)
            def turn(i, last):
                for n in range(6):
                    if not (last and n >= 4):
                        load_unit(m, sp, i * 6 + (8 + n + 2), n % 2)
                    for j in range(32 * n // 6, 32 * (n + 1) // 6):
                        page = sp.value_load(m.pages[0:1, ds(i * 32 + j, 1)], min_val=0, max_val=keys.shape[0] - 1)
                        if j % 4 == 3:
                            sp.wait_ge(kg_used, i * 8 + (j // 4 + 1))
                        else:
                            sp.wait_ge(kv_used, i * 24 + (3 * (j // 4) + j % 4 + 1))
                        sp.dma_start(kring[:, j % 4, :], keys[ds(page, 1), :, :].rearrange("a p n -> (a p) n")).then_inc(kp_in[j % 4], 16)

            with sp.Fori(0, PM - 1) as i:
                turn(i, False)
            turn(PM - 1, True)

        @block.scalar
        def _(act):
            act.wait_ge(c_in, 16 * 8)
            for k in range(KT):
                if k % 4 == 0:
                    act.wait_ge(x_in[k // 4], 16)
                if k >= 4:
                    act.wait_ge(sq_used, k - 3)
                act.activation(sq[:, k % 4, :], m.xt[:, k, :], ACT.Square).then_inc(sq_ready, 1)
            act.wait_ge(sq_used, KT)
            for h, (c0, n) in enumerate(HALVES):
                r = act.activation(rs[:, c0:c0 + n], m.aux[:, h, 0:n], ACT.Sqrt, bias=m.eps[:, 0:1], scale=1.0 / D)
                r.then_inc(rt_ready, 1)
            for u in range(2):
                split_hi(m, act, u, u, 0)
            for k in range(KT):
                act.wait_ge(h_ready, k + 1)
                act.activation(m.hh[:, k, :], m.xt[:, k, :], ACT.Copy).then_inc(hh_ready, 1)

            def evac(u, slot, dst, permuted=False):
                act.wait_ge(m.mm_done, u + 3)
                if not permuted:
                    act.activation(dst[:, 0:264], m.acc[:, slot, 0, 0:264], ACT.Copy).then_inc(z_ready, 1)
                    act.activation(dst[:, 264:520], m.acc[:, slot, 1, 0:256], ACT.Copy).then_inc(m.acc_free, 1)
                else:
                    act.activation(dst[:, 0:8], m.acc[:, slot, 0, 0:8], ACT.Copy)
                    v = dst[:, 8:520].rearrange("p (s n) -> p n s", s=CL)
                    act.activation(v[:, 0:32, :], m.acc[:, slot, 0, 8:264].rearrange("p (n s) -> p n s", s=CL), ACT.Copy).then_inc(z_ready, 1)
                    act.activation(v[:, 32:64, :], m.acc[:, slot, 1, 0:256].rearrange("p (n s) -> p n s", s=CL), ACT.Copy).then_inc(m.acc_free, 1)

            with act.Fori(0, PQ) as i:
                for s in range(2):
                    u = i * 2 + s
                    act.wait_ge(rope_done, u + 1)
                    evac(u, s, zst[s])
                    split_hi(m, act, u + 2, s, i + 1)
                for s in range(2):
                    act.wait_ge(rope_done, i * 2 + (s + 3))
                    act.dma_start(qT[ds(i * 2 + s, 1), :, :].rearrange("a p n -> (a p) n"), zo[s][:, :]).then_inc(st_zo[s], 16)
            for b in range(NS):
                for g in range(2):
                    act.wait_ge(qb_mm, 2 * b + g + 1)
                    act.activation(qb[:, b, 512 * g:512 * g + 512], m.aux[:, 2 + g, :], ACT.Copy).then_inc(qb_ready, 1)
            def turn(i, last):
                for n in range(6):
                    u = i * 6 + (8 + n)
                    kind, half = n % 3, n // 3
                    if kind == 0:
                        act.wait_ge(rope_done, i * 2 + (half + 8 + 2))
                    elif kind == 1:
                        act.wait_ge(st_v, i * 32 + (half + 1) * 16)
                    else:
                        act.wait_ge(st_u, i * 32 + (half + 1) * 16)
                    evac(u, n % 2, zst[kind], permuted=(kind == 2))
                    if not (last and n >= 4):
                        split_hi(m, act, u + 2, n % 2, i * 3 + (4 + n // 2 + 1))
                    tile = i * 2 + half
                    if kind == 1:
                        act.wait_ge(m.acc_free, u + 3)
                        act.dma_start(vT[ds(tile, 1), :, :].rearrange("a p n -> (a p) n"), zst[1][:, :]).then_inc(st_v, 16)
                        act.wait_ge(rope_done, i * 2 + (half + 8 + 3))
                        act.dma_start(kT[ds(tile, 1), :, :].rearrange("a p n -> (a p) n"), zo[half][:, :]).then_inc(st_zo[half], 16)
                    if kind == 2:
                        act.wait_ge(m.acc_free, u + 3)
                        act.dma_start(uT[ds(tile, 1), :, :].rearrange("a p n -> (a p) n"), zst[2][:, :]).then_inc(st_u, 16)

            with act.Fori(0, PM - 1) as i:
                turn(i, False)
            turn(PM - 1, True)
            act.wait_ge(st_v, 16 * 9)
            act.wait_ge(st_u, 16 * 9)
            for s in range(2):
                act.wait_ge(st_zo[s], 16 * 9)

        @block.gpsimd
        def _(pool):
            pool.sem_inc(m.lo_done, 2); pool.sem_inc(m.mm_done, 2); pool.sem_inc(m.acc_free, 2)
            pool.sem_inc(rope_done, 2); pool.sem_inc(rot_free, 1); pool.sem_inc(kv_used, 3); pool.sem_inc(kg_used, 1); pool.sem_inc(scored, 1)
            for s in (st_v, st_u, st_zo[0], st_zo[1]):
                pool.sem_inc(s, 16)
            split_lo(m, pool, 0, 0)
            for k in range(KT):
                pool.wait_ge(hh_ready, k + 1)
                pool.tensor_tensor(m.hl[:, k, :], m.xt[:, k, :], m.hh[:, k, :].bitcast(F32), ALU.subtract).then_inc(hl_ready, 1)
            split_lo(m, pool, 1, 1)
            with pool.Fori(0, PQ) as i:
                for s in range(2):
                    split_lo(m, pool, i * 2 + (s + 2), s)
            def turn(i, last):
                for n in range(6):
                    if not (last and n >= 4):
                        split_lo(m, pool, i * 6 + (8 + n + 2), n % 2)
                    for j in range(32 * n // 6, 32 * (n + 1) // 6):
                        if j % 4 == 3:
                            pool.wait_ge(kp_in[3], i * 128 + (16 * (j // 4) + 16))
                            pool.wait_ge(qb_ready, i * 4 + (2 * (j // 16) + 2))
                            pool.wait_ge(scored, i * 32 + (j - 2))
                            pool.sem_inc(turn_taken, 1)
                            pool.tensor_tensor(prod[2][:, :], kring[:, 3, :], qb[:, ds(i * 2 + j // 16, 1), :].rearrange("p a b -> p (a b)"), ALU.mult).then_inc(kg_used, 1)

            with pool.Fori(0, PM - 1) as i:
                turn(i, False)
            turn(PM - 1, True)

        @block.tensor
        def _(pe):
            pe.wait_ge(c_in, 16 * 8)
            for k in range(KT):
                pe.wait_ge(sq_ready, k + 1)
                for h, (c0, n) in enumerate(HALVES):
                    mm = pe.matmul(m.aux[:, h, 0:n], m.ones[:, :], sq[:, k % 4, c0:c0 + n], start=(k == 0), stop=(k == KT - 1))
                mm.then_inc(sq_used, 1)

            def rotate(src, r, z_count):
                pe.wait_ge(z_ready, z_count)
                pe.wait_ge(m.acc_free, z_count + 2)
                pe.wait_ge(rot_free, r + 1)
                for h, (c0, n) in enumerate(HALVES):
                    mm = pe.matmul(m.aux[:, h, 0:n], m.rot[:, :], src[:, c0:c0 + n], start=True, stop=True)
                mm.then_inc(rot_ready, 1)

            def queries(i, first):
                for s in range(2):
                    unit_matmuls(m, pe, i * 2 + s, s, m.hh, m.hl, s, wait_k=hl_ready if first and s == 0 else None)
                for s in range(2):
                    rotate(zst[s], i * 2 + s, i * 2 + (s + 1))

            queries(0, True)
            with pe.Fori(0, PQ - 1) as i:
                queries(i + 1, False)
            pe.wait_ge(qs_done, 8)
            for b in range(NS):
                for g in range(2):
                    if b > 0:
                        pe.wait_ge(qb_ready, 2 * b + g - 1)
                    for q in range(4):
                        mm = pe.matmul(m.aux[:, 2 + g, 128 * q:128 * q + 128], m.qs[:, 4 * g + q, b:b + 1].broadcast_to([P, P]),
                                       m.ident[:, :], start=True, stop=True)
                    mm.then_inc(qb_mm, 1)
            with pe.Fori(0, PM) as i:
                for n in range(6):
                    unit_matmuls(m, pe, i * 6 + (8 + n), n % 2, m.hh, m.hl, n % 2)
                    if n % 3 == 1:
                        rotate(zst[0], i * 2 + (8 + n // 3), i * 6 + (8 + n))

        @block.vector
        def _(dve):
            ch = Chain(dve, s_v)
            dve.wait_ge(c_in, 16 * 8)
            dve.wait_ge(rt_ready, 2)
            ch(dve.reciprocal(rs[:, :], rs[:, :]))
            for k in range(KT):
                dve.scalar_tensor_tensor(m.xt[:, k, :], m.xt[:, k, :], m.gains[:, 0, k:k + 1], rs[:, :], ALU.mult, ALU.mult).then_inc(h_ready, 1)

            def rope(src, dst, r, z_count, dst_free, dst_count):
                dve.wait_ge(m.acc_free, z_count + 2)
                dve.tensor_tensor(t1[:, :], src[:, :], cosT[:, :], ALU.mult)
                dve.wait_ge(rot_ready, r + 1)
                for h, (c0, n) in enumerate(HALVES):
                    x = dve.tensor_tensor(t2[:, c0:c0 + n], m.aux[:, h, 0:n], sinT[:, c0:c0 + n], ALU.mult)
                    if h == 0:
                        ch(x)
                x.then_inc(rot_free, 1)
                dve.wait_ge(rot_free, r + 2)
                dve.wait_ge(dst_free, dst_count)
                dve.tensor_tensor(dst[:, :], t1[:, :], t2[:, :], ALU.add).then_inc(rope_done, 1)

            with dve.Fori(0, PQ) as i:
                ch.enter(i, 2)
                for s in range(2):
                    rope(zst[s], zo[s], i * 2 + s, i * 2 + (s + 1), st_zo[s], i * 16 + 16)
                    dve.wait_ge(rope_done, i * 2 + (s + 3))
                    dve.tensor_copy(m.qs[:, ds(i * 2 + s, 1), :].rearrange("p a b -> p (a b)"), zo[s][:, 0:NS]).then_inc(qs_done, 1)
                ch.leave(PQ)
            with dve.Fori(0, PM) as i:
                ch.enter(i, 2)

                def multiply(j):
                    if j % 4 != 3:
                        x = 3 * (j // 4) + j % 4
                        dve.wait_ge(kp_in[j % 4], i * 128 + (16 * (j // 4) + 16))
                        dve.wait_ge(qb_ready, i * 4 + (2 * (j // 16) + 2))
                        dve.wait_ge(scored, i * 32 + (4 * ((x - 2) // 3) + (x - 2) % 3 + 2 if x >= 2 else 1))
                        dve.tensor_tensor(prod[x % 2][:, :], kring[:, j % 4, :], qb[:, ds(i * 2 + j // 16, 1), :].rearrange("p a b -> p (a b)"), ALU.mult).then_inc(kv_used, 1)

                def total(j):
                    x = 3 * (j // 4) + j % 4
                    dst = m.scd[:, j % 16, :].rearrange("p (c b h) -> p b h c", c=2, b=NS)
                    if j % 4 == 3:
                        dve.wait_ge(kg_used, i * 8 + (j // 4 + 2))
                    else:
                        dve.wait_ge(kv_used, i * 24 + (x + 4))
                    dve.tensor_reduce(dst[:, ds(i * 2 + j // 16, 1), :, :].rearrange("p a h c -> p (a h) c"), prod[2 if j % 4 == 3 else x % 2][:, :].rearrange("p (h c d) -> p h c d", c=2, d=64),
                                      AX.X, ALU.add).then_inc(scored, 1)

                multiply(0)
                for j in range(32):
                    if j < 31:
                        multiply(j + 1)
                    total(j)
                    if j % 16 == 8:
                        n = j // 16
                        rope(zst[0], zo[n], i * 2 + (8 + n), i * 6 + (9 + 3 * n), st_zo[n], i * 16 + (16 * 5))
                        dve.wait_ge(rope_done, i * 2 + (8 + n + 3))
                ch.leave(PM)


TAU_HI = 6.28125
TAU_MID = 0.0019350051879882812
TAU_LO = 2 * math.pi - TAU_HI - TAU_MID
MAGIC = 1.5 * 2.0 ** 23
QP = 4
PPQ = GP // QP
NC = NCH + NS


def mixer_plan(m):
    at = m.at
    m.top = m.x0
    m.hs = at("hs", [P, NC + 1, 3, GP])
    m.vv = at("vv", [P, NC, 2, GP])
    m.yall = at("yall", [P, G, NC], F32, off=m.end - NC * 2 * GP * 4)
    m.pw = at("pw", [P, 2, 9, GP]); m.bb = at("bb", [P, 2, GP, CH]); m.bc = at("bc", [P, 4, GP, CH])
    m.s5sm = at("s5sm", [P, 24, GP]); m.a1 = at("a1", [P, 2, 2, GP]); m.a2 = at("a2", [P, 2, 2, GP])
    m.u1 = at("u1", [P, 2, GP]); m.u2 = at("u2", [P, 2, GP])
    m.hn = at("hn", [P, NS, 2, GP]); m.hn2 = at("hn2", [P, NS, 2, GP]); m.dk = at("dk", [CH, G]); m.cm5 = at("cm5", [P, 4])
    m.room1, m.room1_end = m.top, m.x0 + 3 * KT * T * 4
    m.top = m.free
    m.ot = at("ot", [P, H, T])
    m.wtk_off = m.top
    m.wtk = at("wtk", [P, NPG, NS * H]); m.nv = at("nv", [P, H, NS])
    m.room2 = m.top
    m.raw_off = m.room1_end
    m.qq = at("qq", [P, QP, 2, PPQ, 9, CH], F32, off=m.raw_off + 2 * KT * P * 4)


def cplx(eng, ch, dst, a, b, c, d, t, op):
    ch(eng.tensor_tensor(t, c, d, ALU.mult))
    ch(eng.tensor_tensor(dst, a, b, ALU.mult))
    return eng.tensor_tensor(dst, dst, t, op)


def pair_coeffs(x, g, n):
    return x[:, g, :].unsqueeze(2).broadcast_to([P, PPQ, n, CH])


def pair_powers(m, r, g, n):
    return m.pw[:, r, 0:n, g].rearrange("p j g -> p g j").unsqueeze(3).broadcast_to([P, PPQ, n, CH])


def load_ug(m, sp, ug, ug_in, ug_zero):
    uv = m.uT[:, :, :].rearrange("a (g c) n -> c (a g) n", c=CH)
    for j in range(CL):
        s0 = NS + (CL - 1 - j) * NCH
        sp.dma_start(ug[CH * j:CH * j + CH, :, NS:NC], uv[:, :, s0:s0 + NCH]).then_inc(ug_in, 16)
    sp.wait_ge(ug_zero, 2)
    sp.dma_start(ug[0:CH, :, 0:NS], uv[:, :, 0:NS]).then_inc(ug_in, 16)
    sp.dma_start(ug[P - CH:P, :, NC:NC + NS], uv[:, :, 0:NS]).then_inc(ug_in, 16)


def stage_p1(nc, m, ins, outs):
    at, sem = m.at, m.sem
    mixer_plan(m)
    pw, bb, bc, vv, hs, lam = m.pw, m.bb, m.bc, m.vv, m.hs, m.lam
    m.top = m.room1
    ug = at("ug", [P, G, NC + NS]); ti = at("ti", [P, PPQ, CL, CH]); tr = at("tr", [P, GP * CH])
    assert m.top <= m.room1_end
    m.top = m.room2
    e = [at("e0", [P, 2, PPQ, CL, CH]), at("e1", [P, 2, PPQ, CL, CH], F32, off=m.raw_off + 2 * KT * P * 4)]
    et = at("et", [P, 2, PPQ, P]); stT = at("stT", [P, 2052])
    lamv = at("lamv", [P, 4, 64]); lamp = at("lamp", [P, 2, 64])
    ksv = at("ksv", [P, 2, H, NS]); tmp = at("tmp", [P, H, NS]); qk2 = at("qk2", [P, 2, NS, H]); dm = at("dm", [P, NS * H]); mm_ = at("mm_", [P, NS * H]); cm = at("cm", [P, 2]); dsm = at("dsm", [P, 8])
    tr2 = at("tr2", [P, PPQ, CL, CH], F32, off=m.raw_off)
    f = lambda j: m.s5sm[:, j, :]
    S = {n: sem("h_" + n) for n in ("params_in bc_in state_in masks_in new_token_in ug_zero ug_in exps_ready exponents_ready sines_ready angles_ready powers_ready input_matrix_ready e_re e_im e_turned "
                                "e_kept added_done added_kept scores_turned scores_kept lambda_exps lambda_sums new_products new_score max_ready softmax_exps columns_ready weights_done weights_kept new_weight chain_v chain_p").split()}
    with nc.Block() as block:
        @block.sync
        def _(sp):
            for j, n in enumerate(("a_re", "a_im", "log_dt")):
                sp.dma_start(m.s5sm[:, j, :], ins[n][:, :]).then_inc(S["params_in"], 16)
            sp.dma_start(m.cm5[:, :], ins["cmask4"][:, :]).then_inc(S["params_in"], 16)
            sp.dma_start(dm[:, :], ins["dmask"][:, :]).then_inc(S["masks_in"], 16)
            sp.dma_start(cm[:, :], ins["cmask"][:, :]).then_inc(S["masks_in"], 16)
            for j in range(4):
                sp.dma_start(lamv[:, j, :], ins["lambdas"][j:j + 1, :].broadcast_to([P, 64])).then_inc(S["masks_in"], 16)
            sp.dma_start(ksv[:, 0, :, :], m.kT[:, :, 0:NS].rearrange("h p b -> p h b")).then_inc(S["new_token_in"], 16)
            sp.dma_start(ksv[:, 1, :, :], m.vT[:, :, 0:NS].rearrange("h p b -> p h b")).then_inc(S["new_token_in"], 16)
            for j, n in enumerate(("b_re", "b_im", "c_re", "c_im")):
                sp.dma_start(bc[:, j, :, :], ins[n][:, :, :]).then_inc(S["bc_in"], 16)
            load_ug(m, sp, ug, S["ug_in"], S["ug_zero"])
            for r, n in enumerate(("h0_re", "h0_im")):
                sp.dma_start(hs[:, NCH:NC, r, :], ins[n][:, :, :]).then_inc(S["state_in"], 16)
            sp.dma_start(m.dk[:, :], ins["d_t"][:, :]).then_inc(S["state_in"], 16)
            sp.wait_ge(S["state_in"], 48)

        @block.gpsimd
        def _(pool):
            ch = Chain(pool, S["chain_p"])
            pool.memset(ug[:, :, 0:NS], 0.0).then_inc(S["ug_zero"], 1)
            pool.memset(ug[:, :, NC:NC + NS], 0.0).then_inc(S["ug_zero"], 1)
            pool.wait_ge(S["input_matrix_ready"], 1)
            pool.wait_ge(S["powers_ready"], 1)
            for q in range(QP):
                g = slice(PPQ * q, PPQ * q + PPQ)
                if q >= 2:
                    pool.wait_ge(S["e_turned"], 4 * (q - 1))
                cplx(pool, ch, e[q % 2][:, 1, :, :, :], pair_coeffs(bb[:, 0], g, CL), pair_powers(m, 1, g, CL), pair_coeffs(bb[:, 1], g, CL), pair_powers(m, 0, g, CL),
                     ti[:, :, :, :], ALU.add).then_inc(S["e_im"], 1)
                pool.wait_ge(S["e_im"], q + 1)

        @block.scalar
        def _(act):
            act.wait_ge(S["params_in"], 64)
            act.activation(f(3), f(2), ACT.Exp).then_inc(S["exps_ready"], 1)
            act.wait_ge(S["exponents_ready"], 1)
            act.activation(f(6), f(4), ACT.Exp).then_inc(S["exps_ready"], 1)
            act.wait_ge(S["lambda_sums"], 1)
            act.activation(lam[:, 2:4], lam[:, 0:2], ACT.Exp).then_inc(S["lambda_exps"], 1)
            act.wait_ge(S["max_ready"], 1)
            act.activation(stT[:, 0:2049], stT[:, 0:2049], ACT.Exp, bias=dsm[:, 1:2], scale=0.125, accum_out=dsm[:, 2:3]).then_inc(S["softmax_exps"], 1)
            act.wait_ge(S["angles_ready"], 1)
            act.activation(f(9), f(7), ACT.Sin).then_inc(S["sines_ready"], 1)
            act.activation(f(10), f(8), ACT.Sin).then_inc(S["sines_ready"], 1)
            for q in range(QP):
                for n in range(4):
                    act.wait_ge(S["e_turned"], 4 * q + n + 1)
                    if q >= 1:
                        act.wait_ge(S["added_done"], 4 * q)
                    act.activation(et[:, n // 2, 4 * (n % 2):4 * (n % 2) + 4, :].rearrange("p a b -> p (a b)"), m.aux[:, n, :], ACT.Copy).then_inc(S["e_kept"], 1)
                for n in range(4):
                    act.wait_ge(S["added_done"], 4 * q + n + 1)
                    g0 = PPQ * q + 4 * (n % 2)
                    act.activation(vv[:, :, n // 2, g0:g0 + 4].rearrange("p n g -> p g n"), m.acc[:, n // 2, n % 2, 0:4 * NC].rearrange("p (g n) -> p g n", g=4), ACT.Copy).then_inc(S["added_kept"], 1)

        @block.tensor
        def _(pe):
            for j in range(NPG):
                if j % 4 == 0 and j >= 8:
                    pe.wait_ge(S["scores_kept"], j // 4 - 1)
                mm = pe.transpose(m.aux[:, (j // 4) % 2, P * (j % 4):P * (j % 4) + P], m.scd[:, j, :], m.ident[:, :])
                if j % 4 == 3:
                    mm.then_inc(S["scores_turned"], 1)
            pe.wait_ge(S["new_products"], 1)
            pe.matmul(m.aux[:, 2, 0:1], qk2[:, :, :, :].rearrange("p c b h -> p (c b h)"), m.ones[:, 0:1], start=True, stop=True).then_inc(S["new_score"], 1)
            pe.wait_ge(S["columns_ready"], 1)
            pe.wait_ge(S["softmax_exps"], 1)
            for j in range(NPG):
                mm = pe.matmul(m.aux[:, j // 8, 64 * (j % 8):64 * (j % 8) + 64], stT[:, P * j:P * j + P], mm_[:, :], start=True, stop=True)
                if j % 8 == 7:
                    mm.then_inc(S["weights_done"], 1)
            pe.matmul(m.aux[:, 2, 64:128], stT[:, 2048:2049].broadcast_to([P, P]), mm_[:, :], start=True, stop=True).then_inc(S["new_weight"], 1)
            pe.wait_ge(S["weights_kept"], 3)
            for q in range(QP):
                pe.wait_ge(S["e_re"], q + 1)
                pe.wait_ge(S["e_im"], q + 1)
                for n in range(4):
                    if q >= 1:
                        pe.wait_ge(S["e_kept"], 4 * (q - 1) + n + 1)
                    for a in range(4):
                        mm = pe.transpose(m.aux[:, n, P * a:P * a + P], e[q % 2][:, n // 2, 4 * (n % 2) + a, :, :].rearrange("p j c -> p (j c)"), m.ident[:, :])
                    mm.then_inc(S["e_turned"], 1)
                pe.wait_ge(S["ug_in"], 16 * (CL + 2))
                for n in range(4):
                    pe.wait_ge(S["e_kept"], 4 * q + n + 1)
                    if q >= 1:
                        pe.wait_ge(S["added_kept"], 4 * (q - 1) + n + 1)
                    for a in range(4):
                        gp = PPQ * q + 4 * (n % 2) + a
                        for g2 in range(2):
                            mm = pe.matmul(m.acc[64 * g2:64 * g2 + 64, n // 2, n % 2, NC * a:NC * a + NC], et[:, n // 2, 4 * (n % 2) + a, 64 * g2:64 * g2 + 64],
                                           ug[:, 2 * gp + g2, 0:NC], start=True, stop=True)
                    mm.then_inc(S["added_done"], 1)

        @block.vector
        def _(dve):
            ch = Chain(dve, S["chain_v"])
            tt = lambda o, a, b, op: ch(dve.tensor_tensor(o, a, b, op))
            ts = lambda o, a, s1, s2, o1, o2=None: ch(dve.tensor_scalar(o, a, s1, s2, o1, o2) if o2 is not None else dve.tensor_scalar(o, a, s1, None, o1))
            dve.wait_ge(S["params_in"], 64)
            dve.wait_ge(S["exps_ready"], 1)
            tt(f(5), f(1), f(3), ALU.mult)
            dve.tensor_tensor(f(4), f(0), f(3), ALU.mult).then_inc(S["exponents_ready"], 1)
            dve.wait_ge(S["masks_in"], 16 * 6)
            ch(dve.tensor_tensor(lamp[:, :, :], lamv[:, 0:4:2, :], lamv[:, 1:4:2, :], ALU.mult))
            dve.tensor_reduce(lam[:, 0:2], lamp[:, :, :], AX.X, ALU.add).then_inc(S["lambda_sums"], 1)
            dve.wait_ge(S["new_token_in"], 32)
            ch(dve.tensor_tensor(tmp[:, :, :], m.qs[:, :, :], ksv[:, 0, :, :], ALU.mult))
            for c in range(2):
                x = dve.tensor_scalar(qk2[:, c, :, :].rearrange("p b h -> p h b"), tmp[:, :, :], cm[:, c:c + 1], None, ALU.mult)
                if c == 0:
                    ch(x)
            x.then_inc(S["new_products"], 1)
            for g in range(4):
                dve.wait_ge(S["scores_turned"], g + 1)
                dve.tensor_copy(stT[:, 512 * g:512 * g + 512], m.aux[:, g % 2, :]).then_inc(S["scores_kept"], 1)
            dve.wait_ge(S["new_score"], 1)
            dve.wait_ge(S["scores_kept"], 4)
            ch(dve.tensor_copy(stT[:, 2048:2049], m.aux[:, 2, 0:1]))
            ch(dve.tensor_reduce(dsm[:, 0:1], stT[:, 0:2049], AX.X, ALU.max))
            dve.tensor_scalar(dsm[:, 1:2], dsm[:, 0:1], -0.125, None, ALU.mult).then_inc(S["max_ready"], 1)
            for out, quarter in ((7, 0.0), (8, 0.25)):
                ts(f(11), f(5), 1 / (2 * math.pi), quarter, ALU.mult, ALU.add)
                ts(f(11), f(11), MAGIC, None, ALU.add)
                ts(f(11), f(11), -MAGIC, None, ALU.add)
                ch(dve.scalar_tensor_tensor(f(12), f(11), -TAU_HI, f(5), ALU.mult, ALU.add))
                ch(dve.scalar_tensor_tensor(f(12), f(11), -TAU_MID, f(12), ALU.mult, ALU.add))
                ch(dve.scalar_tensor_tensor(f(12), f(11), -TAU_LO, f(12), ALU.mult, ALU.add))
                if quarter:
                    ts(f(12), f(12), math.pi / 2, None, ALU.add)
                ts(f(out), f(12), 3.1415925, -3.1415925, ALU.min, ALU.max)
            ch(dve.memset(pw[:, 0, 0, :], 1.0))
            dve.memset(pw[:, 1, 0, :], 0.0).then_inc(S["angles_ready"], 1)
            dve.wait_ge(S["lambda_exps"], 1)
            ch(dve.tensor_tensor(lam[:, 4:5], lam[:, 3:4], lam[:, 2:3], ALU.subtract))
            ch(dve.tensor_scalar(lam[:, 4:5], lam[:, 4:5], -LAM0, None, ALU.add))
            ch(dve.scalar_tensor_tensor(dsm[:, 4:5], cm[:, 1:2], lam[:, 4:5], cm[:, 0:1], ALU.mult, ALU.add))
            dve.wait_ge(S["softmax_exps"], 1)
            ch(dve.reciprocal(dsm[:, 5:6], dsm[:, 2:3]))
            ch(dve.tensor_tensor(dsm[:, 6:7], dsm[:, 5:6], dsm[:, 4:5], ALU.mult))
            dve.tensor_scalar(mm_[:, :], dm[:, :], dsm[:, 6:7], None, ALU.mult).then_inc(S["columns_ready"], 1)
            dve.wait_ge(S["angles_ready"], 1)
            dve.wait_ge(S["sines_ready"], 2)
            dve.wait_ge(S["exps_ready"], 2)
            tt(pw[:, 0, 1, :], f(6), f(10), ALU.mult)
            tt(pw[:, 1, 1, :], f(6), f(9), ALU.mult)

            def powers(lo, n, by):
                a = [pw[:, r, lo:lo + n, :] for r in range(2)]
                b = [pw[:, r, by:by + 1, :].broadcast_to([P, n, GP]) for r in range(2)]
                t = m.s5sm[:, 13:13 + n, :]
                ch(cplx(dve, ch, pw[:, 0, by + lo:by + lo + n, :], a[0], b[0], a[1], b[1], t, ALU.subtract))
                return cplx(dve, ch, pw[:, 1, by + lo:by + lo + n, :], a[0], b[1], a[1], b[0], t, ALU.add)

            ch(powers(1, 1, 1))
            ch(powers(1, 2, 2))
            powers(1, 4, 4).then_inc(S["powers_ready"], 1)
            dve.wait_ge(S["powers_ready"], 1)
            tt(f(13), f(0), f(0), ALU.mult)
            tt(f(14), f(1), f(1), ALU.mult)
            tt(f(13), f(13), f(14), ALU.add)
            ch(dve.reciprocal(f(13), f(13)))
            ts(f(14), pw[:, 0, 1, :], -1.0, None, ALU.add)
            ch(cplx(dve, ch, f(15), f(14), f(0), pw[:, 1, 1, :], f(1), f(17), ALU.add))
            ch(cplx(dve, ch, f(16), pw[:, 1, 1, :], f(0), f(14), f(1), f(17), ALU.subtract))
            tt(f(15), f(15), f(13), ALU.mult)
            tt(f(16), f(16), f(13), ALU.mult)
            fr = [f(15 + r).unsqueeze(2).broadcast_to([P, GP, CH]) for r in range(2)]
            tb = tr[:, :].rearrange("p (g c) -> p g c", c=CH)
            dve.wait_ge(S["bc_in"], 64)
            ch(cplx(dve, ch, bb[:, 0, :, :], fr[0], bc[:, 0, :, :], fr[1], bc[:, 1, :, :], tb, ALU.subtract))
            cplx(dve, ch, bb[:, 1, :, :], fr[0], bc[:, 1, :, :], fr[1], bc[:, 0, :, :], tb, ALU.add).then_inc(S["input_matrix_ready"], 1)
            dve.wait_ge(S["input_matrix_ready"], 1)
            for q in range(QP):
                g = slice(PPQ * q, PPQ * q + PPQ)
                if q >= 2:
                    dve.wait_ge(S["e_turned"], 4 * (q - 1))
                cplx(dve, ch, e[q % 2][:, 0, :, :, :], pair_coeffs(bb[:, 0], g, CL), pair_powers(m, 0, g, CL), pair_coeffs(bb[:, 1], g, CL), pair_powers(m, 1, g, CL),
                     tr2[:, :, :, :], ALU.subtract).then_inc(S["e_re"], 1)
                dve.wait_ge(S["e_re"], q + 1)
                if q == 0:
                    for j in range(2):
                        dve.wait_ge(S["weights_done"], j + 1)
                        dve.tensor_copy(m.wtk[:, 8 * j:8 * j + 8, :].rearrange("p j n -> p (j n)"), m.aux[:, j, :]).then_inc(S["weights_kept"], 1)
                    dve.wait_ge(S["new_weight"], 1)
                    dve.tensor_tensor(m.nv[:, :, :], m.aux[:, 2, 64:128].rearrange("p (b h) -> p h b", h=H), ksv[:, 1, :, :], ALU.mult).then_inc(S["weights_kept"], 1)
            for k, j in ((0, CL), (1, 1)):
                for r in range(2):
                    ch(dve.tensor_copy(m.a1[:, k, r, :], pw[:, 0, j, :]))
                ts(m.a2[:, k, 0, :], pw[:, 1, j, :], -1.0, None, ALU.mult)
                ch(dve.tensor_copy(m.a2[:, k, 1, :], pw[:, 1, j, :]))
            ch(dve.memset(hs[:, 0, :, :], 0.0))


VR = 16
HW = H * P // 2
PV_STEPS = ((0, 0, 6), (0, 6, 12), (0, 12, 16), (1, 0, 8), (1, 8, 16))

def stage_l1(nc, m, ins, outs):
    at, sem = m.at, m.sem
    lam = m.lam
    m.top = m.room1
    qkv = at("qkv", [P, 2, 3, NT])
    vtok = at("vtok", [P, 2, 4, P]); ex = at("ex", [P, 2, 2, NT]); wT = at("wT", [P, 2, 4, P])
    st = at("stt", [P, 2, 2, 8])
    assert m.top <= m.room1_end, (m.top, m.room1_end)
    m.top = m.room2
    vr = [at(f"vr{j}", [P, HW], F32, off=m.raw_off + 4 * HW * j if j < 8 else None) for j in range(VR)]
    wb = at("wb", [P, NPG, H]); pvs = at("pvs", [H, HW])
    qt = at("qt", [P, PPQ, 9, CH]); npw = at("npw", [P, 9, GP]); cmk = at("causal", [P, P]); dg = at("dg", [P, 2, 2, P])
    page_in, page_used = [sem(f"page_in{j}") for j in range(VR)], sem("page_used")
    all_heads_kept, sample_weights, sample_out, sample_kept, sc_u, sc_h, chain_p, sample_states, so = [sem("l_" + x) for x in "pvs wb pv pvev u h v hn so".split()]
    vals = ins["cache_v"]
    head_in = [sem(f"head_in{j}") for j in range(2)]; mask_in = sem("mask_in")
    value_turned, value_kept, scores_ready, scores_used, max_ready, exps_ready, diag_ready, weights_turned, weights_kept, out_ready, out_kept, exps_used, chain_v = [sem("p_" + x) for x in "vtr vev smm sfree nm e d wmm wev omm oev efree v3".split()]
    R = H * 4
    with nc.Block() as block:
        @block.sync
        def _(sp):
            sp.dma_start(cmk[:, :], ins["causal"][:, :]).then_inc(mask_in, 16)
            with sp.Fori(0, H // 2) as hh:
                for s in range(2):
                    for half in range(2):
                        for j in range(NPG):
                            page = sp.value_load(m.pages[0:1, ds(hh * 32 + (16 * s + j), 1)], min_val=0, max_val=vals.shape[0] - 1)
                            sp.wait_ge(page_used, hh * 64 + (32 * s + 16 * half + j + 1))
                            sp.dma_start(vr[j][:, :], vals[ds(page, 1), :, HW * half:HW * half + HW].rearrange("a p n -> (a p) n")).then_inc(page_in[j], 16)

        @block.gpsimd
        def _(pool):
            for s, n in ((scores_used, 2), (exps_used, 2), (value_kept, 1), (weights_kept, 2), (out_kept, 2), (out_ready, 2), (page_used, VR), (sample_kept, 1), (sample_out, 1)):
                pool.sem_inc(s, n)
            ch = Chain(pool, chain_p)
            hs, vv, a1, a2, u1, u2 = m.hs, m.vv, m.a1, m.a2, m.u1, m.u2

            def step(src, dst, add):
                pool.tensor_tensor(u1[:, :, :], src[:, 0:2, :], a1[:, 0, :, :], ALU.mult)
                ch(pool.tensor_tensor(u2[:, :, :], src[:, 1:3, :], a2[:, 0, :, :], ALU.mult))
                ch(pool.tensor_tensor(u1[:, :, :], u1[:, :, :], add, ALU.add))
                pool.tensor_tensor(dst[:, 0:2, :], u1[:, :, :], u2[:, :, :], ALU.add)
                ch(pool.tensor_tensor(dst[:, 2, :], u1[:, 0, :], u2[:, 0, :], ALU.add))

            row = lambda t, i: t[:, ds(i, 1), :, :].rearrange("p a r g -> p (a r) g")
            with pool.Fori(0, NCH - 1) as i:
                ch.enter(i, 3)
                step(row(hs, i), row(hs, i + 1), row(vv, i + NS))
                ch.leave(NCH - 1)
            step(hs[:, NCH - 1, :, :], hs[:, NC, :, :], vv[:, NC - 1, :, :])
            bcs = lambda x: x.unsqueeze(1).broadcast_to([P, NS, GP])
            hn, hn2 = m.hn, m.hn2
            for r in range(2):
                ch(pool.tensor_tensor(hn[:, :, r, :], hs[:, NCH:NC, r, :], bcs(a1[:, 1, r, :]), ALU.mult))
                ch(pool.tensor_tensor(hn2[:, :, r, :], hs[:, NCH:NC, 1 - r, :], bcs(a2[:, 1, r, :]), ALU.mult))
            ch(pool.tensor_tensor(hn[:, :, :, :], hn[:, :, :, :], hn2[:, :, :, :], ALU.add))
            pool.tensor_tensor(hn[:, :, :, :], hn[:, :, :, :], vv[:, 0:NS, :, :], ALU.add).then_inc(sample_states, 1)
            pool.wait_ge(sample_states, 1)
            ch(pool.memset(npw[:, :, :], 0.0))
            ch(pool.tensor_tensor(npw[:, :, :], npw[:, :, :], m.pw[:, 1, :, :], ALU.subtract))
            for q in range(QP):
                g = slice(PPQ * q, PPQ * q + PPQ)
                neg = npw[:, :, g].rearrange("p j g -> p g j").unsqueeze(3).broadcast_to([P, PPQ, 9, CH])
                ch(cplx(pool, ch, m.qq[:, q, 0, :, :, :], pair_coeffs(m.bc[:, 2], g, 9), pair_powers(m, 0, g, 9), pair_coeffs(m.bc[:, 3], g, 9), pair_powers(m, 1, g, 9),
                        qt[:, :, :, :], ALU.subtract))
                ch(cplx(pool, ch, m.qq[:, q, 1, :, :, :], pair_coeffs(m.bc[:, 2], g, 9), neg, pair_coeffs(m.bc[:, 3], g, 9), pair_powers(m, 0, g, 9),
                        qt[:, :, :, :], ALU.subtract))

        @block.tensor
        def _(pe):
            with pe.Fori(0, H // 2) as hh:
                for s in range(2):
                    pe.wait_ge(head_in[s], hh * 48 + 48)
                    it = lambda q: hh * 8 + (4 * s + q)
                    for step in range(4 + 2):
                        if step < 4:
                            q = step
                            pe.wait_ge(scores_used, it(q) + 1)
                            for c in range(2):
                                mm = pe.matmul(m.acc[:, q % 2, c, 0:128 * (q + 1)], qkv[64 * c:64 * c + 64, s, 0, 128 * q:128 * q + 128],
                                               qkv[64 * c:64 * c + 64, s, 1, 0:128 * (q + 1)], start=True, stop=True)
                            mm.then_inc(scores_ready, 1)
                            if step == 0:
                                pe.wait_ge(weights_kept, it(q) + 2)
                                pe.wait_ge(value_kept, hh * 2 + (s + 1))
                                for kb in range(4):
                                    mm = pe.transpose(m.aux[:, 1, 128 * kb:128 * kb + 128], qkv[:, s, 2, 128 * kb:128 * kb + 128], m.ident[:, :])
                                mm.then_inc(value_turned, 1)
                        if 1 <= step <= 4:
                            q = step - 1
                            pe.wait_ge(diag_ready, it(q) + 1)
                            pe.wait_ge(exps_ready, hh * 16 + (8 * s + 2 * q + 2))
                            pe.wait_ge(weights_kept, it(q) + 1)
                            if q == 1:
                                pe.wait_ge(value_kept, hh * 2 + (s + 2))
                            for kb in range(q + 1):
                                for c in range(2):
                                    mm = pe.matmul(m.aux[:, q % 2, 128 * kb:128 * kb + 128], ex[:, q % 2, c, 128 * kb:128 * kb + 128], dg[:, q % 2, c, :],
                                                   start=(c == 0), stop=(c == 1))
                            mm.then_inc(weights_turned, 1)
                        if step >= 2:
                            q = step - 2
                            pe.wait_ge(weights_kept, it(q) + 3)
                            pe.wait_ge(value_kept, hh * 2 + (s + 2))
                            pe.wait_ge(out_kept, it(q) + 2)
                            for kb in range(q + 1):
                                mm = pe.matmul(m.aux[:, 2, 0:128], vtok[:, s, kb, :], wT[:, q % 2, kb, :], start=(kb == 0), stop=(kb == q))
                            mm.then_inc(out_ready, 1)
                        if step in (3, 5):
                            half = step // 2 - 1
                            pe.wait_ge(all_heads_kept, hh * 4 + (2 * s + half + 1))
                            for i in range(H // 2):
                                mm = pe.matmul(m.aux[:, 3, i:i + 1], pvs[:, P * i:P * i + P], m.ident[0:H, H // 2 * half + i:H // 2 * half + i + 1],
                                               start=(i == 0), stop=(i == H // 2 - 1), skip_group_check=True)
                            mm.then_inc(sample_out, 1)
                        if step < 5:
                            half, lo, hi = PV_STEPS[step]
                            if step == 0:
                                pe.wait_ge(sample_weights, hh * 2 + (s + 1))
                            if lo == 0:
                                pe.wait_ge(sample_kept, hh * 4 + (2 * s + half + 1))
                            for j in range(lo, hi):
                                pe.wait_ge(page_in[j], hh * 64 + (32 * s + 16 * half + 16))
                                pe.matmul(m.aux[0:H, 3, 0:HW], wb[:, j, :], vr[j][:, :], start=(j == 0), stop=(j == NPG - 1)).then_inc(page_used, 1)
        @block.scalar
        def _(act):
            def load_head(h, s):
                for n, t in enumerate((m.qT, m.kT, m.vT)):
                    act.dma_start(qkv[:, s, n, :], t[ds(h, 1), :, NS:T].rearrange("a p n -> (a p) n")).then_inc(head_in[s], 16)
            for s in range(2):
                load_head(s, s)
            def turn(hh, last):
                for s in range(2):
                    it = lambda q: hh * 8 + (4 * s + q)
                    for step in range(4 + 2):
                        if step < 4:
                            q = step
                            act.wait_ge(max_ready, it(q) + 1)
                            act.wait_ge(exps_used, it(q) + 1)
                            for c in range(2):
                                x = act.activation(ex[:, q % 2, c, 0:128 * (q + 1)], m.acc[:, q % 2, c, 0:128 * (q + 1)], ACT.Exp, bias=st[:, q % 2, c, 1:2], scale=0.125,
                                               accum_out=st[:, q % 2, c, 2:3])
                                x.then_inc(exps_ready, 1)
                            act.wait_ge(exps_ready, hh * 16 + (8 * s + 2 * q + 2))
                            act.sem_inc(scores_used, 1)
                        if step == 1:
                            act.wait_ge(value_turned, hh * 2 + (s + 1))
                            act.wait_ge(out_ready, hh * 8 + (4 * s + 2))
                            act.activation(vtok[:, s, :, :].rearrange("p a b -> p (a b)"), m.aux[:, 1, :], ACT.Copy).then_inc(value_kept, 1)
                        if 1 <= step <= 4:
                            q = step - 1
                            act.wait_ge(weights_turned, it(q) + 1)
                            act.sem_inc(exps_used, 1)
                            act.wait_ge(out_ready, it(q) + 1)
                            act.activation(wT[:, q % 2, 0:q + 1, :].rearrange("p a b -> p (a b)"), m.aux[:, q % 2, 0:128 * (q + 1)], ACT.Copy).then_inc(weights_kept, 1)
                        if step >= 2:
                            q = step - 2
                            act.wait_ge(out_ready, it(q) + 3)
                            act.activation(m.ot[:, ds(hh * 2 + s, 1), NS + 128 * q:NS + 128 * q + 128].rearrange("p a b -> p (a b)"), m.aux[:, 2, 0:128], ACT.Copy).then_inc(out_kept, 1)
                        if step in (2, 4):
                            half = step // 2 - 1
                            act.wait_ge(page_used, hh * 64 + (32 * s + 16 * half + 32))
                            act.activation(pvs[:, :], m.aux[0:H, 3, 0:HW], ACT.Copy).then_inc(all_heads_kept, 1)
                        if step in (3, 5):
                            half = step // 2 - 1
                            act.wait_ge(sample_out, hh * 4 + (2 * s + half + 2))
                            act.activation(m.ot[:, H // 2 * half:H // 2 * half + H // 2, ds(hh * 2 + s, 1)].rearrange("p h a -> p (h a)"), m.aux[:, 3, 0:H // 2], ACT.Copy).then_inc(sample_kept, 1)
                    if not last:
                        act.wait_ge(out_ready, hh * 8 + (4 * s + 6))
                        load_head(hh * 2 + (s + 2), s)

            with act.Fori(0, H // 2 - 1) as hh:
                turn(hh, False)
            turn(H // 2 - 1, True)

        @block.vector
        def _(dve):
            ch = Chain(dve, chain_v)
            dve.wait_ge(mask_in, 16)
            with dve.Fori(0, H // 2) as hh:
                ch.enter(hh, 2 * (4 * 3 * 2 + 4 * 3))
                for s in range(2):
                    it = lambda q: hh * 8 + (4 * s + q)
                    dve.wait_ge(sample_out, hh * 4 + (2 * s + 1))
                    dve.tensor_copy(wb[:, :, :], m.wtk[:, :, ds((hh * 2 + s) * H, H)]).then_inc(sample_weights, 1)
                    for q in range(4):
                        dve.wait_ge(scores_ready, it(q) + 1)
                        for c in range(2):
                            sc = m.acc[:, q % 2, c, :]
                            ch(dve.tensor_tensor(sc[:, 128 * q:128 * q + 128], sc[:, 128 * q:128 * q + 128], cmk[:, :], ALU.add))
                            ch(dve.tensor_reduce(st[:, q % 2, c, 0:1], sc[:, 0:128 * (q + 1)], AX.X, ALU.max))
                            ch(dve.tensor_scalar(st[:, q % 2, c, 1:2], st[:, q % 2, c, 0:1], -0.125, None, ALU.mult))
                        dve.sem_inc(max_ready, 1)
                        dve.wait_ge(exps_ready, hh * 16 + (8 * s + 2 * q + 2))
                        dve.wait_ge(exps_used, it(q) + 1)
                        for c in range(2):
                            x = dve.reciprocal(st[:, q % 2, c, 3:4], st[:, q % 2, c, 2:3])
                            if c == 1:
                                ch(x)
                                ch(dve.tensor_tensor(st[:, q % 2, c, 3:4], st[:, q % 2, c, 3:4], lam[:, 4:5], ALU.mult))
                            else:
                                ch(x)
                        for c in range(2):
                            x = dve.tensor_scalar(dg[:, q % 2, c, :], m.ident[:, :], st[:, q % 2, c, 3:4], None, ALU.mult)
                        x.then_inc(diag_ready, 1)
                ch.leave(H // 2)
            dve.wait_ge(sample_kept, 2 * H + 1)
            ch(dve.tensor_tensor(m.ot[:, :, 0:NS], m.ot[:, :, 0:NS], m.nv[:, :, :], ALU.add))


def stage_p3(nc, m, ins, outs):
    at, sem = m.at, m.sem
    bb, qq, hs, yall, dk = m.bb, m.qq, m.hs, m.yall, m.dk
    m.top = m.room1
    ug = at("ug3", [P, G, NC + NS])
    assert m.top <= m.room1_end, (m.top, m.room1_end)
    m.top = m.wtk_off
    tz = [at(f"tz{j}", [P, 2 * PPQ, P]) for j in range(2)]; km = [at(f"km{j}", [CH, 2 * PPQ, P]) for j in range(2)]
    de = [at(f"de{j}", [CH, 2 * PPQ, CH]) for j in range(2)]
    ug_zero, ug_in, y_out, tz_zero = [sem("y_" + x) for x in "ugzero ugin out tzzero".split()]; shift_in = [sem(f"y_shift{j}") for j in range(2)]
    rows_ready, rows_kept, diag_added, sums_ready, sums_kept, s_v = [sem("y_" + x) for x in "kmm kev kd ymm yev v".split()]
    m.top = m.raw_off
    sq = at("head_sq", [P, 4, T]); rs = at("head_rs", [P, 2, T]); gsub = at("gsub", [P, 2])
    assert m.end <= m.raw_off + 2 * KT * P * 4
    gs_in, sq_ready, sum_ready, root_ready, scaled = [sem("n_" + x) for x in "gsin sq sum root scaled".split()]
    in_bank = lambda n, g0=0: slice(g0 + 8 * (n // 2) + n % 2, g0 + 8 * (n // 2) + n % 2 + 7, 2)
    with nc.Block() as block:
        @block.sync
        def _(sp):
            load_ug(m, sp, ug, ug_in, ug_zero)
            sp.dma_start(gsub[:, 0:1], ins["g_sub"][:, :]).then_inc(gs_in, 16)
            for q in range(QP):
                sp.wait_ge(tz_zero, min(q, 1) + 1)
                sp.wait_ge(diag_added, q + 1)
                if q >= 2:
                    sp.wait_ge(sums_ready, 4 * (q - 1))
                for j in range(CL):
                    sp.dma_start(tz[q % 2][CH * j:CH * j + CH, :, CH * (CL - 1 - j):P], km[q % 2][:, :, 0:CH * (j + 1)]).then_inc(shift_in[q % 2], 16)
            yv = m.yT[:, :, :].rearrange("a (g c) n -> c (a g) n", c=CH)
            for half in range(2):
                g = slice(G // 2 * half, G // 2 * half + G // 2)
                sp.wait_ge(sums_kept, 2 * QP * (half + 1))
                for s in range(CL):
                    sp.dma_start(yv[:, g, NS + s * NCH:NS + (s + 1) * NCH], yall[CH * s:CH * s + CH, g, 0:NCH]).then_inc(y_out, 16)
                sp.dma_start(yv[:, g, 0:NS], yall[0:CH, g, NCH:NC]).then_inc(y_out, 16)
            sp.dma_start(outs["ssm_prompt"][:, :, :], hs[:, NC, 0:2, :]).then_inc(y_out, 16)
            sp.dma_start(outs["ssm_sample"][:, :, :, :], m.hn[:, :, :, :]).then_inc(y_out, 16)
            sp.wait_ge(y_out, 16 * (2 * CL + 4))

        @block.gpsimd
        def _(pool):
            pool.memset(tz[0][:, :, :], 0.0).then_inc(tz_zero, 1)
            pool.memset(tz[1][:, :, :], 0.0).then_inc(tz_zero, 1)
            for h in range(H):
                if h >= 4:
                    pool.wait_ge(sum_ready, h - 3)
                pool.tensor_tensor(sq[:, h % 4, :], m.ot[:, h, :], m.ot[:, h, :], ALU.mult).then_inc(sq_ready, 1)

        @block.scalar
        def _(act):
            def copy_k(q):
                for n in range(4):
                    act.wait_ge(rows_ready, 4 * q + n + 1)
                    if q >= 2:
                        act.wait_ge(shift_in[q % 2], 16 * CL * (q // 2))
                    act.activation(km[q % 2][:, in_bank(n), :], m.aux[0:CH, n, :].rearrange("p (a b) -> p a b", b=P), ACT.Copy).then_inc(rows_kept, 1)

            copy_k(0)
            for q in range(QP):
                if q < QP - 1:
                    copy_k(q + 1)
                for n in range(4):
                    if q == QP - 1:
                        for h in (2 * n, 2 * n + 1):
                            act.wait_ge(sum_ready, h + 1)
                            if h >= 2:
                                act.wait_ge(scaled, h - 1)
                            for hf, (c0, w) in enumerate(HALVES):
                                act.activation(rs[:, h % 2, c0:c0 + w], m.aux[:, 2 * (h % 2) + hf, 0:w], ACT.Sqrt, bias=m.eps[:, 0:1], scale=1.0 / P).then_inc(root_ready, 1)
                    act.wait_ge(sums_ready, 4 * q + n + 1)
                    act.activation(yall[:, in_bank(n, 16 * q), :], m.acc[:, n // 2, n % 2, 0:4 * NC].rearrange("p (g n) -> p g n", g=4), ACT.Copy).then_inc(sums_kept, 1)

        @block.tensor
        def _(pe):
            def first_rows(q):
                for n in range(4):
                    if q >= 1:
                        pe.wait_ge(rows_kept, 4 * (q - 1) + n + 1)
                    for a in range(4):
                        g = in_bank(n).start + 2 * a
                        rows = slice(NST * (g % 2), NST * (g % 2) + NST)
                        for r in range(2):
                            mm = pe.matmul(m.aux[0:CH, n, P * a:P * a + P], bb[rows, r, PPQ * q + g // 2, :], qq[rows, q, r, g // 2, 0:CL, :].rearrange("p j c -> p (j c)"),
                                           start=(r == 0), stop=(r == 1))
                    mm.then_inc(rows_ready, 1)

            first_rows(0)
            for q in range(QP):
                if q < QP - 1:
                    first_rows(q + 1)
                pe.wait_ge(ug_in, 16 * (CL + 2))
                for n in range(4):
                    if q >= 1:
                        pe.wait_ge(sums_kept, 4 * (q - 1) + n + 1)
                    if q == QP - 1:
                        pe.wait_ge(rows_kept, 4 * QP)
                        for h in (2 * n, 2 * n + 1):
                            pe.wait_ge(sq_ready, h + 1)
                            if h >= 2:
                                pe.wait_ge(root_ready, 2 * (h - 1))
                            for hf, (c0, w) in enumerate(HALVES):
                                mm = pe.matmul(m.aux[:, 2 * (h % 2) + hf, 0:w], m.ones[:, :], sq[:, h % 4, c0:c0 + w], start=True, stop=True)
                            mm.then_inc(sum_ready, 1)
                    if n == 0:
                        pe.wait_ge(shift_in[q % 2], 16 * CL * (q // 2 + 1))
                    for a in range(4):
                        g = in_bank(n).start + 2 * a
                        rows = slice(NST * (g % 2), NST * (g % 2) + NST)
                        o = m.acc[:, n // 2, n % 2, NC * a:NC * a + NC]
                        pe.matmul(o, tz[q % 2][:, g, :], ug[:, 16 * q + g, NS:NC + NS], start=True, stop=False)
                        for r in range(2):
                            mm = pe.matmul(o, qq[rows, q, r, g // 2, 1:9, :].rearrange("p j c -> p (j c)"), hs[rows, 0:NC, r, PPQ * q + g // 2], start=False, stop=(r == 1))
                    mm.then_inc(sums_ready, 1)

        @block.vector
        def _(dve):
            ch = Chain(dve, s_v)
            dve.memset(ug[:, :, 0:NS], 0.0).then_inc(ug_zero, 1)
            dve.memset(ug[:, :, NC:NC + NS], 0.0).then_inc(ug_zero, 1)
            for q in range(QP):
                ch(dve.tensor_tensor(de[q % 2][:, :, :], dk[:, 16 * q:16 * q + 16].unsqueeze(2).broadcast_to([CH, 2 * PPQ, CH]),
                                     m.ident[0:CH, 0:CH].unsqueeze(1).broadcast_to([CH, 2 * PPQ, CH]), ALU.mult))
                dve.wait_ge(rows_kept, 4 * q + 4)
                dve.tensor_tensor(km[q % 2][:, :, 0:CH], km[q % 2][:, :, 0:CH], de[q % 2][:, :, :], ALU.add).then_inc(diag_added, 1)
                dve.wait_ge(diag_added, q + 1)
            dve.wait_ge(gs_in, 16)
            ch(dve.tensor_scalar(gsub[:, 1:2], gsub[:, 0:1], 1.0 - LAM0, None, ALU.mult))
            for h in range(H):
                dve.wait_ge(root_ready, 2 * h + 2)
                ch(dve.reciprocal(rs[:, h % 2, :], rs[:, h % 2, :]))
                dve.scalar_tensor_tensor(m.ot[:, h, :], m.ot[:, h, :], gsub[:, 1:2], rs[:, h % 2, :], ALU.mult, ALU.mult).then_inc(scaled, 1)
            dve.wait_ge(scaled, H)


TT, TW = 5, T // 5

def stage_d(nc, m, ins, outs):
    at, sem = m.at, m.sem
    m.top = m.free
    ot = m.ot
    f0 = m.free
    yg = at("yg", [P, 8, T], F32, off=f0 + H * T * 4)
    sq = at("sq2", [P, 4, T], F32, off=f0 + 2 * H * T * 4)
    stg = at("stg", [P, 2, T], F32, off=f0 + 2 * H * T * 4 + 4 * T * 4)
    rs = at("rs2", [P, T], F32, off=f0 + 2 * H * T * 4 + 6 * T * 4)
    bgl = at("bgl", [P, 8], F32, off=f0 + 2 * H * T * 4 + 7 * T * 4)
    sc = m.sc = at("sc", [TW, TT, 16, P], F32, off=f0)
    keysT = at("keysT", [P, 16, P], F32, off=m.free - NPG * P * 4)
    yr = at("yr", [P, 8, T], F32, off=m.x0 + (2 * KT + 8) * T * 4)
    gh = at("gh", [P, 8, T], F32R, off=m.x0); gl = at("gl", [P, 8, T], F32R, off=m.x0 + 8 * T * 4)
    S = {n: sem("d_" + n) for n in "const_in x_in keys_in gelu_done gelu_hi gelu_lo heads_hi heads_lo sigmoid_ready mixed mixed_hi mixed_lo squares_ready squares_summed root_ready h_ready h_hi h_lo query_ready scored scores_kept chain x2_stored residual_added".split()}
    y_in = [sem(f"d_yin{k}") for k in range(8)]
    with nc.Block() as block:
        @block.sync
        def _(sp):
            load_y = lambda k: sp.dma_start(yr[:, k, :], m.yT[k, :, :]).then_inc(y_in[k], 16)
            load_y(0)
            for u in range(U_GLU, U_GLU + 2):
                load_unit(m, sp, u, u % 2)
            for k in range(1, 8):
                load_y(k)
            sp.dma_start(bgl[:, :], ins["b_glu"][:, :]).then_inc(S["const_in"], 16)
            sp.dma_start(keysT[:, :, :], ins["keys_t"][:, :, :]).then_inc(S["keys_in"], 16)
            for u in range(U_GLU, U_OUT):
                load_unit(m, sp, u + 2, u % 2)
            sp.wait_ge(m.mm_done, U_OUT + 2)
            sp.wait_ge(S["gelu_lo"], 8)
            sp.dma_start(m.xt[:, :, :], ins["x_t"][:, :, :]).then_inc(S["x_in"], 16)
            with sp.Fori(0, (N_OUT + N_PQ) // 2) as i:
                for s in range(2):
                    load_unit(m, sp, i * 2 + (U_OUT + s + 2), s)
            sp.wait_ge(S["residual_added"], N_OUT)
            sp.dma_start(m.x2[:, :, :], m.xt[:, :, :]).then_inc(S["x2_stored"], 16)
            sp.wait_ge(S["x2_stored"], 16)

        @block.gpsimd
        def _(pool):
            for u in range(U_GLU, U_GLU + 2):
                split_lo(m, pool, u, u % 2)
            for h in range(H):
                pool.wait_ge(S["heads_hi"], h + 1)
                pool.tensor_tensor(m.hl[:, h, :], ot[:, h, :], m.hh[:, h, :].bitcast(F32), ALU.subtract).then_inc(S["heads_lo"], 1)
            for u in range(U_GLU, U_OUT):
                split_lo(m, pool, u + 2, u % 2)
            with pool.Fori(0, N_OUT // 2) as i:
                for s in range(2):
                    split_lo(m, pool, i * 2 + (U_OUT + s + 2), s)
            for k in range(KT):
                pool.wait_ge(S["h_hi"], k + 1)
                pool.tensor_tensor(m.hl[:, k, :], stg[:, k % 2, :], m.hh[:, k, :].bitcast(F32), ALU.subtract).then_inc(S["h_lo"], 1)
            with pool.Fori(0, N_PQ // 2) as i:
                for s in range(2):
                    split_lo(m, pool, i * 2 + (U_PQ + s + 2), s)

        @block.scalar
        def _(act):
            for k in range(8 + 1):
                if k < 8:
                    act.wait_ge(y_in[k], 16)
                    act.activation(yg[:, k, 0:NS], yr[:, k, 0:NS], ACT.Gelu_apprx_tanh)
                    act.activation(yg[:, k, NS:T].rearrange("p (n s) -> p n s", s=CL), yr[:, k, NS:T].rearrange("p (s n) -> p n s", s=CL), ACT.Gelu_apprx_tanh).then_inc(S["gelu_done"], 1)
                if k >= 1:
                    act.wait_ge(S["gelu_done"], k)
                    act.activation(gh[:, k - 1, :], yg[:, k - 1, :], ACT.Copy).then_inc(S["gelu_hi"], 1)
                if k == 1:
                    split_hi(m, act, U_GLU, U_GLU % 2, U_GLU // 2)
            split_hi(m, act, U_GLU + 1, (U_GLU + 1) % 2, U_GLU // 2)
            for h in range(H):
                act.activation(m.hh[:, h, :], ot[:, h, :], ACT.Copy).then_inc(S["heads_hi"], 1)
            for n in range(N_GLU):
                u = U_GLU + n
                act.wait_ge(m.mm_done, u + 3)
                act.wait_ge(S["const_in"], 16)
                for t in range(2):
                    if n >= 1:
                        act.wait_ge(S["mixed"], 2 * n + t - 1)
                    for hf, (c0, w) in enumerate(HALVES):
                        x = act.activation(stg[:, t, c0:c0 + w], m.acc[:, t, hf, 0:w], ACT.Sigmoid, bias=bgl[:, 2 * n + t:2 * n + t + 1])
                    x.then_inc(S["sigmoid_ready"], 1)
                act.wait_ge(S["sigmoid_ready"], 2 * n + 2)
                act.sem_inc(m.acc_free, 1)
                split_hi(m, act, u + 2, u % 2, (u + 2) // 2)
                for t in range(2):
                    act.wait_ge(S["mixed"], 2 * n + t + 1)
                    act.activation(m.hh[:, 8 + 2 * n + t, :], yg[:, 2 * n + t, :], ACT.Copy).then_inc(S["mixed_hi"], 1)
            with act.Fori(0, N_OUT // 2) as i:
                for s in range(2):
                    split_hi(m, act, i * 2 + (U_OUT + s + 2), s, i + (U_OUT // 2 + 1))
                    act.wait_ge(S["residual_added"], i * 2 + (s + 1))
                    act.wait_ge(S["squares_summed"], i * 2 + (s + 1))
                    act.activation(sq[:, s, :], m.xt[:, ds(i * 2 + s, 1), :].rearrange("p a n -> p (a n)"), ACT.Square).then_inc(S["squares_ready"], 1)
            act.wait_ge(S["squares_summed"], KT + 2)
            for h, (c0, n) in enumerate(HALVES):
                act.activation(rs[:, c0:c0 + n], m.aux[:, h, 0:n], ACT.Sqrt, bias=m.eps[:, 0:1], scale=1.0 / D).then_inc(S["root_ready"], 1)
            for k in range(KT):
                act.wait_ge(S["h_ready"], k + 1)
                act.activation(m.hh[:, k, :], stg[:, k % 2, :], ACT.Copy).then_inc(S["h_hi"], 1)
            with act.Fori(0, N_PQ // 2) as i:
                for s in range(2):
                    u = i * 2 + (U_PQ + s)
                    act.wait_ge(m.mm_done, u + 3)
                    act.wait_ge(S["scored"], i * 2 + (s + 1))
                    for hf, (c0, w) in enumerate(HALVES):
                        x = act.activation(stg[:, s, c0:c0 + w], m.acc[:, s, hf, 0:w], ACT.Copy)
                    x.then_inc(S["query_ready"], 1)
                    act.wait_ge(S["query_ready"], i * 2 + (s + 1))
                    act.sem_inc(m.acc_free, 1)
                    split_hi(m, act, u + 2, s, i + (U_PQ // 2 + 1))
                    if s == 1:
                        for v in range(2):
                            act.wait_ge(S["scored"], i * 2 + (v + 3))
                            act.activation(sc[:, 0:4, ds(i * 2 + v, 1), :].rearrange("p t a n -> p (t a) n"), m.aux[0:TW, 2 * v, :].rearrange("p (t n) -> p t n", t=4), ACT.Copy)
                            act.activation(sc[:, 4, ds(i * 2 + v, 1), :].rearrange("p a n -> p (a n)"), m.aux[0:TW, 2 * v + 1, 0:P], ACT.Copy).then_inc(S["scores_kept"], 1)

        @block.tensor
        def _(pe):
            for u in range(U_GLU, U_OUT):
                s = u % 2
                pe.wait_ge(m.lo_done, u + 3)
                pe.wait_ge(m.acc_free, u + 2)
                tiles = [(t, hf) for t in range(2) for hf in range(2)]
                order = [(t, hf, k) for k in range(8) for t, hf in tiles] if u == U_GLU else [(t, hf, k) for t, hf in tiles for k in range(8)]
                for t, hf, k in order:
                    (c0, n), o = HALVES[hf], m.acc[:, t, hf, 0:HALVES[hf][1]]
                    if u == U_GLU and t == hf == 0:
                        pe.wait_ge(S["gelu_lo"], k + 1)
                    pe.matmul(o, m.wh[s][:, 2 * k + t, :], gh[:, k, c0:c0 + n], start=(k == 0), stop=False)
                    pe.matmul(o, m.wh[s][:, 2 * k + t, :], gl[:, k, c0:c0 + n], start=False, stop=False)
                    mm = pe.matmul(o, m.wl[s][:, 2 * k + t, :], gh[:, k, c0:c0 + n], start=False, stop=(k == 7))
                mm.then_inc(m.mm_done, 1)
            pe.wait_ge(S["heads_lo"], H)
            pe.wait_ge(S["mixed_lo"], 8)
            def add_squares(s, count, first=False, last=False):
                pe.wait_ge(S["squares_ready"], count)
                for h, (c0, n) in enumerate(HALVES):
                    mm = pe.matmul(m.aux[:, h, 0:n], m.ones[:, :], sq[:, s, c0:c0 + n], start=first, stop=last, skip_group_check=True)
                mm.then_inc(S["squares_summed"], 1)

            for s in range(2):
                unit_matmuls(m, pe, U_OUT + s, s, m.hh, m.hl, s)
            add_squares(0, 1, first=True)
            with pe.Fori(0, N_OUT // 2 - 1) as i:
                for s in range(2):
                    unit_matmuls(m, pe, i * 2 + (U_OUT + s + 2), s, m.hh, m.hl, s)
                    add_squares(1 - s, i * 2 + (s + 2))
            add_squares(1, KT, last=True)
            pe.wait_ge(S["keys_in"], 16)
            def queries(i, first):
                for s in range(2):
                    unit_matmuls(m, pe, i * 2 + (U_PQ + s), s, m.hh, m.hl, s, wait_k=S["h_lo"] if first and s == 0 else None)
                for s in range(2):
                    pe.wait_ge(S["query_ready"], i * 2 + (s + 1))
                    pe.wait_ge(S["scores_kept"], i * 2 + (s + 1))
                    for t in range(TT):
                        mm = pe.matmul(m.aux[0:TW, 2 * s + t // 4, P * (t % 4):P * (t % 4) + P], stg[:, s, TW * t:TW * t + TW],
                                       keysT[:, ds(i * 2 + s, 1), :].rearrange("p a n -> p (a n)"), start=True, stop=True)
                    mm.then_inc(S["scored"], 1)

            queries(0, True)
            with pe.Fori(0, N_PQ // 2 - 1) as i:
                queries(i + 1, False)

        @block.vector
        def _(dve):
            ch = Chain(dve, S["chain"])
            dve.sem_inc(S["scored"], 2)
            dve.sem_inc(S["scores_kept"], 2)
            dve.sem_inc(S["squares_summed"], 2)
            for k in range(8):
                dve.wait_ge(S["gelu_hi"], k + 1)
                dve.tensor_tensor(gl[:, k, :], yg[:, k, :], gh[:, k, :].bitcast(F32), ALU.subtract).then_inc(S["gelu_lo"], 1)
            for t in range(8):
                dve.wait_ge(S["sigmoid_ready"], t + 1)
                dve.wait_ge(S["gelu_lo"], 8)
                dve.tensor_tensor(yg[:, t, :], yg[:, t, :], stg[:, t % 2, :], ALU.mult).then_inc(S["mixed"], 1)
                dve.wait_ge(S["mixed_hi"], t + 1)
                dve.tensor_tensor(m.hl[:, 8 + t, :], yg[:, t, :], m.hh[:, 8 + t, :].bitcast(F32), ALU.subtract).then_inc(S["mixed_lo"], 1)
            dve.wait_ge(S["x_in"], 16)
            with dve.Fori(0, N_OUT // 2) as i:
                for s in range(2):
                    dve.wait_ge(m.mm_done, i * 2 + (U_OUT + s + 3))
                    for hf, (c0, n) in enumerate(HALVES):
                        x = m.xt[:, ds(i * 2 + s, 1), c0:c0 + n].rearrange("p a n -> p (a n)")
                        x = dve.tensor_tensor(x, x, m.acc[:, s, hf, 0:n], ALU.add)
                    x.then_inc(S["residual_added"], 1)
                    dve.wait_ge(S["residual_added"], i * 2 + (s + 1))
                    dve.sem_inc(m.acc_free, 1)
            dve.wait_ge(S["root_ready"], 2)
            ch(dve.reciprocal(rs[:, :], rs[:, :]))
            for k in range(KT):
                if k >= 2:
                    dve.wait_ge(S["h_lo"], k - 1)
                dve.scalar_tensor_tensor(stg[:, k % 2, :], m.xt[:, k, :], m.gains[:, 1, k:k + 1], rs[:, :], ALU.mult, ALU.mult).then_inc(S["h_ready"], 1)


TK = 16
HK = H * TK
NB, BW = 13, T // 13
NEG = -3.0e38
GRP, NG = 4, 32

def stage_e(nc, m, ins, outs):
    at, sem = m.at, m.sem
    f0 = m.free
    m.top = m.x0
    sct = at("sct", [TW, 16, P]); cand = at("cand", [TW, H, TK, TK]); eq = at("eq", [TW, HK, TK])
    assert m.end <= m.x0 + KT * T * 4
    m.top = f0 - NPG * P * 4
    wk = at("wk", [TW, 2, 256]); vals = at("vals", [TW, 16, TK]); idx = at("idx", [TW, 16, TK], U32); idf = at("idf", [TW, 16, TK])
    tv = at("tv", [TW, H, TK])
    assert m.end <= f0, (m.end, f0)
    sc = m.sc
    gs = at("gs", [P, P, BW], F32, off=f0)
    m.top = f0 + 2 * P * BW * 4
    tp = at("tp", [TW, H, TK], U32); tpa = at("tpa", [TW, H, TK], U32); pf = at("pf", [TW, HK])
    gx = at("gx", [TW, 3, HK]); sm = at("esm", [TW, 2, H]); iota = at("iota", [P, P]); gt = at("gt", [P, 3, T])
    m.top = m.x0
    o2 = at("o2", [P, 8, P]); og = at("og", [P, 8, P]); gts = at("gts", [P, 3, BW])
    assert m.top <= m.x0 + 3 * 8192
    m.top = m.x0 + 3 * 8192
    ast = at("ast", [P, 2, T])
    assert m.end <= m.x0 + KT * T * 4
    S = {n: sem("e_" + n) for n in "const_in tile_copied gelu_done st0 st1 exps_ready best_shifted choice_ready choice_turned choice_kept chain block_copied key2_ready key1_ready spread_done spread_kept gates_stored block_spread".split()}
    st = [S["st0"], S["st1"]]
    PA, UA = TT, 8
    PB, UB = NB, 4
    UC = N_EXP - PA * UA - PB * UB
    B0 = U_EXP_U + PA * UA
    C0 = B0 + PB * UB
    PC = UC // 2
    TPU = BW // UB
    gD, aD = m.gD, m.aD
    with nc.Block() as block:
        @block.sync
        def _(sp):
            sp.dma_start(iota[:, :], ins["iota"][:, :]).then_inc(S["const_in"], 16)
            for x in ("choice_ready", "block_spread", "choice_kept", "choice_turned", "spread_kept"):
                sp.sem_inc(S[x], 1)
            sp.sem_inc(S["spread_done"], 5)
            sp.sem_inc(st[0], 16); sp.sem_inc(st[1], 16); sp.sem_inc(S["gates_stored"], 16)
            with sp.Fori(0, N_EXP // 2) as i:
                for s in range(2):
                    load_unit(m, sp, i * 2 + (U_EXP_U + s + 2), s)

        @block.gpsimd
        def _(pool):
            def los(n, first, turns):
                with pool.Fori(0, turns) as i:
                    for k in range(n):
                        split_lo(m, pool, i * n + (first + k + 2), k % 2)
            los(UA, U_EXP_U, PA)
            los(UB, B0, PB)
            los(2, C0, PC)

        @block.scalar
        def _(act):
            def take(u, s, e, row, done):
                act.wait_ge(m.mm_done, u + 3)
                act.wait_ge(st[s], row * 16 + 16)
                for hf, (c0, w) in enumerate(HALVES):
                    x = act.activation(ast[:, s, c0:c0 + w], m.acc[:, s, hf, 0:w], ACT.Gelu_apprx_tanh)
                x.then_inc(S["gelu_done"], 1)
                act.wait_ge(S["gelu_done"], done)
                act.sem_inc(m.acc_free, 1)
                act.dma_start(aD[ds(e, 1), :, :].rearrange("a p n -> (a p) n"), ast[:, s, :]).then_inc(st[s], 16)

            with act.Fori(0, PA) as i:
                act.wait_ge(S["choice_ready"], i + 1)
                act.activation(sct[:, :, :], sc[:, ds(i, 1), :, :].rearrange("p a b c -> p (a b) c"), ACT.Copy).then_inc(S["tile_copied"], 1)
                for n in range(UA):
                    u = i * UA + (U_EXP_U + n)
                    if n == UA - 1:
                        act.wait_ge(S["best_shifted"], i + 1)
                        act.activation(tv[:, :, :], tv[:, :, :], ACT.Exp).then_inc(S["exps_ready"], 1)
                    take(u, n % 2, i * UA + n, i * (UA // 2) + n // 2, i * UA + (n + 1))
                    split_hi(m, act, u + 2, n % 2, i * (UA // 2) + (U_EXP_U // 2 + n // 2 + 1))
                act.wait_ge(S["choice_turned"], i + 2)
                act.activation(gt[:, :, :].rearrange("p x (t n) -> p t x n", t=TT)[:, ds(i, 1), :, :].rearrange("p a x n -> p (a x) n"),
                               m.aux[:, 0, 0:3 * TW].rearrange("p (x n) -> p x n", x=3), ACT.Copy).then_inc(S["choice_kept"], 1)
            with act.Fori(0, PB) as i:
                act.wait_ge(S["choice_kept"], TT + 1)
                act.wait_ge(S["block_spread"], i + 1)
                act.activation(gts[:, :, :], gt[:, :, :].rearrange("p x (t n) -> p t x n", t=NB)[:, ds(i, 1), :, :].rearrange("p a x n -> p (a x) n"), ACT.Copy).then_inc(S["block_copied"], 1)
                for n in range(UB):
                    u = i * UB + (B0 + n)
                    take(u, n % 2, i * UB + (PA * UA + n), i * (UB // 2) + (PA * UA // 2 + n // 2), i * UB + (PA * UA + n + 1))
                    split_hi(m, act, u + 2, n % 2, i * (UB // 2) + (B0 // 2 + n // 2 + 1))
                act.wait_ge(S["spread_kept"], i * (BW // 4) + (BW // 4 + 1))
                act.dma_start(gD[ds(i, 1), :, :, :].rearrange("a p e n -> (a p) (e n)"), gs[:, :, :].rearrange("p e n -> p (e n)")).then_inc(S["gates_stored"], 16)
            with act.Fori(0, PC) as i:
                for n in range(2):
                    u = i * 2 + (C0 + n)
                    take(u, n, i * 2 + (C0 - U_EXP_U + n), i + ((C0 - U_EXP_U) // 2), i * 2 + (C0 - U_EXP_U + n + 1))
                    split_hi(m, act, u + 2, n, i + (C0 // 2 + 1))
            for s in range(2):
                act.wait_ge(st[s], 16 + 16 * N_EXP // 2)
            act.wait_ge(S["gates_stored"], 16 + 16 * NB)

        @block.tensor
        def _(pe):
            with pe.Fori(0, PA) as i:
                for n in range(UA):
                    unit_matmuls(m, pe, i * UA + (U_EXP_U + n), n % 2, m.hh, m.hl, n % 2)
                pe.wait_ge(S["choice_ready"], i + 2)
                pe.wait_ge(S["choice_kept"], i + 1)
                for x in range(3):
                    mm = pe.transpose(m.aux[:, 0, TW * x:TW * x + TW], gx[:, x, :], m.ident[0:TW, 0:TW])
                mm.then_inc(S["choice_turned"], 1)
            with pe.Fori(0, PB) as i:
                for n in range(UB):
                    unit_matmuls(m, pe, i * UB + (B0 + n), n % 2, m.hh, m.hl, n % 2)
                    for k in range(TPU):
                        t = n * TPU + k
                        pe.wait_ge(S["key2_ready"], i * BW + (t + 1))
                        pe.wait_ge(S["key1_ready"], i * BW + (t + 1))
                        if t % 4 == 0:
                            pe.wait_ge(S["spread_kept"], i * (BW // 4) + max(t // 4, 1))
                        mm = pe.matmul(m.aux[:, 1 + (t // 4) % 2, P * (t % 4):P * (t % 4) + P], o2[:, t % 8, :], og[:, t % 8, :], start=True, stop=True)
                        mm.then_inc(S["spread_done"], 1)
            with pe.Fori(0, PC) as i:
                for n in range(2):
                    unit_matmuls(m, pe, i * 2 + (C0 + n), n, m.hh, m.hl, n)

        @block.vector
        def _(dve):
            ch = Chain(dve, S["chain"])
            dve.wait_ge(S["const_in"], 16)
            with dve.Fori(0, PA) as i:
                ch = Chain(dve, S["chain"])
                dve.wait_ge(S["tile_copied"], i + 1)
                ch(dve.memset(sm[:, :, :], 0.0))
                for c in range(16):
                    w = wk[:, c % 2, 0:P]
                    ch(dve.max(vals[:, c, 0:8], sct[:, c, :]))
                    ch(dve.max_index(idx[:, c, 0:8], vals[:, c, 0:8], sct[:, c, :]))
                    ch(dve.match_replace(w, vals[:, c, 0:8], sct[:, c, :], NEG))
                    ch(dve.max(vals[:, c, 8:16], w))
                    ch(dve.max_index(idx[:, c, 8:16], vals[:, c, 8:16], w))
                ch(dve.tensor_copy(idf[:, :, :], idx[:, :, :]))
                v = vals[:, :, :].rearrange("p (h c) k -> p h c k", c=2)
                ch(dve.tensor_tensor(cand[:, :, :, :], v[:, :, 0, :].unsqueeze(3).broadcast_to([TW, H, TK, TK]), v[:, :, 1, :].unsqueeze(2).broadcast_to([TW, H, TK, TK]), ALU.add))
                for h in range(H):
                    cd = cand[:, h, :, :].rearrange("p a b -> p (a b)")
                    w = wk[:, h % 2, :]
                    ch(dve.max(tv[:, h, 0:8], cd))
                    ch(dve.max_index(tp[:, h, 0:8], tv[:, h, 0:8], cd))
                    ch(dve.match_replace(w, tv[:, h, 0:8], cd, NEG))
                    ch(dve.max(tv[:, h, 8:16], w))
                    ch(dve.max_index(tp[:, h, 8:16], tv[:, h, 8:16], w))
                ch(dve.tensor_copy(sm[:, 0, :], tv[:, :, 0]))
                dve.tensor_tensor(tv[:, :, :], tv[:, :, :], sm[:, 0, :].unsqueeze(2).broadcast_to([TW, H, TK]), ALU.subtract).then_inc(S["best_shifted"], 1)
                il = idf[:, :, :].rearrange("p (h c) k -> p h c k", c=2)
                dve.wait_ge(S["choice_turned"], i + 1)
                for c in range(2):
                    if c == 0:
                        ch(dve.tensor_scalar(tpa[:, :, :], tp[:, :, :], 4, None, ALU.logical_shift_right))
                    else:
                        ch(dve.tensor_scalar(tpa[:, :, :], tp[:, :, :], 15, None, ALU.bitwise_and))
                    ch(dve.tensor_copy(pf[:, :], tpa[:, :, :].rearrange("p h k -> p (h k)")))
                    ch(dve.tensor_tensor(eq[:, :, :], pf[:, :].unsqueeze(2).broadcast_to([TW, HK, TK]), iota[0:TW, 0:TK].unsqueeze(1).broadcast_to([TW, HK, TK]), ALU.is_equal))
                    e4 = eq[:, :, :].rearrange("p (h k) j -> p h k j", h=H)
                    ch(dve.tensor_tensor(e4, e4, il[:, :, c, :].unsqueeze(2).broadcast_to([TW, H, TK, TK]), ALU.mult))
                    ch(dve.tensor_reduce(gx[:, 1 + c, :], eq[:, :, :], AX.X, ALU.add))
                dve.wait_ge(S["exps_ready"], i + 1)
                ch(dve.tensor_reduce(sm[:, 0, :], tv[:, :, :], AX.X, ALU.add))
                ch(dve.reciprocal(sm[:, 1, :], sm[:, 0, :]))
                ch(dve.tensor_tensor(gx[:, 0, :].rearrange("p (h k) -> p h k", h=H), tv[:, :, :], sm[:, 1, :].unsqueeze(2).broadcast_to([TW, H, TK]), ALU.mult))
                dve.sem_inc(S["choice_ready"], 1)
                dve.sem_clear(S["chain"])
            with dve.Fori(0, PB) as i:
                dve.wait_ge(S["block_copied"], i + 1)
                def spread(g):
                    dve.wait_ge(S["spread_done"], i * BW + (4 * g + 9))
                    if g == 0:
                        dve.wait_ge(S["gates_stored"], i * 16 + 16)
                    dve.tensor_copy(gs[:, :, 4 * g:4 * g + 4].rearrange("p e t -> p t e"), m.aux[:, 1 + g % 2, :].rearrange("p (t e) -> p t e", t=4)).then_inc(S["spread_kept"], 1)
                for t in range(BW):
                    if t % 4 == 0:
                        dve.wait_ge(S["spread_done"], i * BW + (t + 1))
                    dve.tensor_scalar(o2[:, t % 8, :], iota[:, :], gts[:, 2, t:t + 1], None, ALU.is_equal).then_inc(S["key2_ready"], 1)
                    dve.tensor_scalar(og[:, t % 8, :], iota[:, :], gts[:, 1, t:t + 1], gts[:, 0, t:t + 1], ALU.is_equal, ALU.mult).then_inc(S["key1_ready"], 1)
                    if t % 4 == 3 and t >= 7:
                        spread(t // 4 - 1)
                spread(BW // 4 - 1)
                dve.wait_ge(S["key1_ready"], i * BW + BW)
                dve.sem_inc(S["block_spread"], 1)

def stage_f(nc, m, ins, outs):
    at, sem = m.at, m.sem
    b = m.x0 + KT * T * 4
    SZ = GRP * T * 4
    a4 = [at(f"a4{s}", [P, GRP, T], F32, off=b + s * SZ) for s in range(2)]
    g4 = [at(f"g4{s}", [P, NB, GRP, BW], F32, off=b + (2 + s) * SZ) for s in range(2)]
    vh = [at(f"vh{s}", [P, GRP, T], F32R, off=b + (4 + s) * SZ) for s in range(2)]
    vl = [at(f"vl{s}", [P, GRP, T], F32R, off=b + (6 + s) * SZ) for s in range(2)]
    m.top = m.free
    sq = at("sq3", [P, 4, T]); rs = at("rs3", [P, T])
    S = {n: sem("g_" + n) for n in "x_in ain0 ain1 gin0 gin1 weighed first_weighed weighed_hi first_hi weighed_lo first_lo sum_added tile_done squares_ready squares_summed root_ready out_ready out_stored".split()}
    ain, gin = [S["ain0"], S["ain1"]], [S["gin0"], S["gin1"]]
    with nc.Block() as block:
        def turn_loads(sp, i, last):
            for gg in range(2):
                g = i * 2 + gg
                for n in range(4):
                    if last and gg == 1 and n >= 2:
                        continue
                    load_unit(m, sp, i * 8 + (U_EXP_V + 4 * gg + n + 2), n % 2)
                    if n == 1 and not (last and gg == 1):
                        loads_ag(sp, g + 1, 1 - gg, i + (1 if gg == 1 else 0))

        def loads_ag(sp, g, s, pair):
            sp.wait_ge(S["tile_done"], g * 16 - 15)
            sp.dma_start(a4[s][:, :, :], m.aD[ds(g * GRP, GRP), :, :].rearrange("e p n -> p e n")).then_inc(ain[s], 16)
            sp.dma_start(g4[s][:, :, :, :].rearrange("p b e n -> p b (e n)"), m.gD[:, :, ds(g * GRP, GRP), :].rearrange("b p e n -> p b (e n)")).then_inc(gin[s], 16)

        @block.sync
        def _(sp):
            sp.dma_start(a4[0][:, :, :], m.aD[0:GRP, :, :].rearrange("e p n -> p e n")).then_inc(ain[0], 16)
            sp.dma_start(g4[0][:, :, :, :].rearrange("p b e n -> p b (e n)"), m.gD[:, :, 0:GRP, :].rearrange("b p e n -> p b (e n)")).then_inc(gin[0], 16)
            sp.dma_start(m.xt[:, :, :], m.x2[:, :, :]).then_inc(S["x_in"], 16)
            with sp.Fori(0, NG // 2 - 1) as i:
                turn_loads(sp, i, False)
            turn_loads(sp, NG // 2 - 1, True)
            for k in range(KT):
                sp.wait_ge(S["out_ready"], k + 1)
                sp.dma_start(outs["y_t"][:, k, :], m.xt[:, k, :]).then_inc(S["out_stored"], 16)
            sp.wait_ge(S["out_stored"], 16 * KT)

        @block.gpsimd
        def _(pool):
            def turn(i, last):
                for n in range(6 if last else 8):
                    split_lo(m, pool, i * 8 + (U_EXP_V + n + 2), n % 2)
            with pool.Fori(0, NG // 2 - 1) as i:
                turn(i, False)
            turn(NG // 2 - 1, True)

        @block.scalar
        def _(act):
            def w_hi(g, s):
                act.wait_ge(S["weighed"], g + 1)
                act.wait_ge(S["tile_done"], g * 16 - 15)
                act.activation(vh[s][:, :, :], a4[s][:, :, :], ACT.Copy).then_inc(S["weighed_hi"], 1)
            for e in range(GRP):
                act.wait_ge(S["first_weighed"], e + 1)
                act.activation(vh[0][:, e, :], a4[0][:, e, :], ACT.Copy).then_inc(S["first_hi"], 1)
            act.wait_ge(S["first_hi"], GRP)
            act.sem_inc(S["weighed_hi"], 1)

            def square(k):
                if k >= 4:
                    act.wait_ge(S["squares_summed"], k - 3)
                act.wait_ge(S["sum_added"], 2 + 16 * (NG - 1) + k + 1)
                act.activation(sq[:, k % 4, :], m.xt[:, k, :], ACT.Square).then_inc(S["squares_ready"], 1)

            def turn(i, last):
                for gg in range(2):
                    for n in range(4):
                        if not (last and gg == 1 and n >= 2):
                            split_hi(m, act, i * 8 + (U_EXP_V + 4 * gg + n + 2), n % 2, i * 4 + (U_EXP_V // 2 + 2 * gg + n // 2 + 1),
                                     (S["tile_done"], i * 32 + (16 * gg + 4 * n + 4)))
                        if n == 1 and not (last and gg == 1):
                            w_hi(i * 2 + (gg + 1), 1 - gg)
                        if last and gg == 1 and n >= 1:
                            for k in range(4 * n - 4, 4 * n):
                                square(k)
            with act.Fori(0, NG // 2 - 1) as i:
                turn(i, False)
            turn(NG // 2 - 1, True)
            for k in range(KT - 4, KT):
                square(k)
            act.wait_ge(S["squares_summed"], KT)
            for h, (c0, n) in enumerate(HALVES):
                act.activation(rs[:, c0:c0 + n], m.aux[:, h, 0:n], ACT.Sqrt, bias=m.eps[:, 0:1], scale=1.0 / D).then_inc(S["root_ready"], 1)

        @block.tensor
        def _(pe):
            def add_squares(k):
                pe.wait_ge(S["squares_ready"], k + 1)
                for h, (c0, n) in enumerate(HALVES):
                    mm = pe.matmul(m.aux[:, h, 0:n], m.ones[:, :], sq[:, k % 4, c0:c0 + n], start=(k == 0), stop=(k == KT - 1), skip_group_check=True)
                mm.then_inc(S["squares_summed"], 1)

            def turn(i, last):
                for gg in range(2):
                    g = i * 2 + gg
                    pe.wait_ge(S["weighed_lo"], g + 1)
                    for n in range(4):
                        u = i * 8 + (U_EXP_V + 4 * gg + n)
                        s = n % 2
                        pe.wait_ge(m.lo_done, u + 3)
                        for d in range(4):
                            r = i * 32 + (16 * gg + 4 * n + d)
                            pe.wait_ge(S["sum_added"], r + 1)
                            for hf, (c0, w) in enumerate(HALVES):
                                o = m.acc[:, d % 2, hf, 0:w]
                                for e in range(GRP):
                                    pe.matmul(o, m.wh[s][:, 4 * e + d, :], vh[gg][:, e, c0:c0 + w], start=(e == 0), stop=False)
                                    pe.matmul(o, m.wh[s][:, 4 * e + d, :], vl[gg][:, e, c0:c0 + w], start=False, stop=False)
                                    mm = pe.matmul(o, m.wl[s][:, 4 * e + d, :], vh[gg][:, e, c0:c0 + w], start=False, stop=(e == GRP - 1))
                            mm.then_inc(S["tile_done"], 1)
                        if last and gg == 1 and n >= 1:
                            for k in range(4 * n - 4, 4 * n):
                                add_squares(k)

            with pe.Fori(0, NG // 2 - 1) as i:
                turn(i, False)
            turn(NG // 2 - 1, True)
            for k in range(KT - 4, KT):
                add_squares(k)

        @block.vector
        def _(dve):
            dve.sem_inc(S["sum_added"], 2)
            def weigh(g, s, pair):
                dve.wait_ge(ain[s], pair * 16 + 16)
                dve.wait_ge(gin[s], pair * 16 + 16)
                a = a4[s][:, :, :].rearrange("p e (b n) -> p e b n", b=NB)
                dve.tensor_tensor(a, a, g4[s][:, :, :, :].rearrange("p b e n -> p e b n"), ALU.mult).then_inc(S["weighed"], 1)
            def low(g, s):
                dve.wait_ge(S["weighed_hi"], g + 1)
                dve.tensor_tensor(vl[s][:, :, :], a4[s][:, :, :], vh[s][:, :, :].bitcast(F32), ALU.subtract).then_inc(S["weighed_lo"], 1)
            dve.wait_ge(ain[0], 16)
            dve.wait_ge(gin[0], 16)
            for e in range(GRP):
                a = a4[0][:, e, :].rearrange("p (b n) -> p b n", b=NB)
                x = dve.tensor_tensor(a, a, g4[0][:, :, e, :], ALU.mult).then_inc(S["first_weighed"], 1)
            dve.wait_ge(S["first_weighed"], GRP)
            dve.sem_inc(S["weighed"], 1)
            for e in range(GRP):
                dve.wait_ge(S["first_hi"], e + 1)
                dve.tensor_tensor(vl[0][:, e, :], a4[0][:, e, :], vh[0][:, e, :].bitcast(F32), ALU.subtract).then_inc(S["first_lo"], 1)
            dve.wait_ge(S["first_lo"], GRP)
            dve.sem_inc(S["weighed_lo"], 1)
            dve.wait_ge(S["x_in"], 16)
            def turn(i, last):
                for gg in range(2):
                    more = not (last and gg == 1)
                    for n in range(4):
                        for d in range(4):
                            r = i * 32 + (16 * gg + 4 * n + d)
                            dve.wait_ge(S["tile_done"], r + 1)
                            for hf, (c0, w) in enumerate(HALVES):
                                x = m.xt[:, 4 * n + d, c0:c0 + w]
                                x = dve.tensor_tensor(x, x, m.acc[:, d % 2, hf, 0:w], ALU.add)
                            x.then_inc(S["sum_added"], 1)
                        if n == 1 and more:
                            weigh(i * 2 + (gg + 1), 1 - gg, i + (1 if gg == 1 else 0))
                        if n == 2 and more:
                            low(i * 2 + (gg + 1), 1 - gg)
            with dve.Fori(0, NG // 2 - 1) as i:
                turn(i, False)
            turn(NG // 2 - 1, True)
            dve.wait_ge(S["root_ready"], 2)
            dve.reciprocal(rs[:, :], rs[:, :]).then_inc(S["tile_done"], 1)
            dve.wait_ge(S["tile_done"], 16 * NG + 1)
            for k in range(KT):
                dve.wait_ge(S["squares_summed"], KT)
                dve.scalar_tensor_tensor(m.xt[:, k, :], m.xt[:, k, :], m.gains[:, 2, k:k + 1], rs[:, :], ALU.mult, ALU.mult).then_inc(S["out_ready"], 1)


def program(nc, ins, outs):
    with ExitStack() as ctx:
        m = common(nc, ctx, ins, outs)
        dram = lambda n, s: nc.dram_tensor(n, s, F32).ap()
        m.qT, m.uT, m.yT = (dram(n, [8, P, T]) for n in ("q_rows", "u_rows", "y_rows"))
        m.kT, m.vT = outs["k_t"], outs["v_t"]
        m.x2 = dram("x_mid", [P, KT, T])
        m.aD = dram("expert_acts", [P, P, T])
        m.gD = dram("expert_gates", [NB, P, P, BW])
        for stage in (stage_a, stage_p1, stage_l1, stage_p3, stage_d, stage_e, stage_f):
            own = []

            def new(name):
                own.append(nc.alloc_semaphore(name))
                return own[-1]

            m.sem = new
            stage(nc, m, ins, outs)
            nc.clear_and_free_semaphores(own)
            nc.all_engine_barrier()


def _units(w, width):
    k, n = w.shape
    return w.reshape(k // P, P, n // width, width).transpose(2, 1, 0, 3).reshape(n // width, P, -1)


def _states(a):
    rest = a.shape[2:]
    return a.reshape(GP, 2, NST, *rest).transpose(1, 2, 0, *range(3, 3 + len(rest))).reshape(P, GP, *rest)


def _cols(a):
    return a.reshape(-1, P).T


def _constants():
    c = {"ident": np.eye(P), "ones": np.ones((P, P)), "eps": np.full((P, 1), EPS), "iota": np.tile(np.arange(P), (P, 1))}
    rot = np.zeros((P, P))
    for b in (0, 64):
        for j in range(32):
            rot[b + 32 + j, b + j], rot[b + j, b + 32 + j] = -1, 1
    c["rot"] = rot
    f = np.float32
    inv = f(1.0) / (f(10000.0) ** (np.arange(32, dtype=f) * f(2) / f(64)))
    pos = np.concatenate([np.full(NS, PAST), np.arange(NT)]).astype(f)
    ang = (pos[None, :] * np.tile(inv, 4)[:, None]).astype(f)
    c["cos_t"], c["sin_t"] = np.cos(ang), np.sin(ang)
    c["dmask"] = np.concatenate([np.eye(64), np.eye(64)])
    c["cmask"] = np.kron(np.eye(2), np.ones((64, 1)))
    c["cmask4"] = np.concatenate([c["cmask"], -c["cmask"]], 1)
    c["causal"] = np.where(np.arange(P)[:, None] >= np.arange(P)[None, :], 0, -1e30)
    return {n: np.ascontiguousarray(a, dtype=f) for n, a in c.items()}


_OUTS = {"k_t": (8, P, T), "v_t": (8, P, T), "ssm_prompt": (P, 2, GP), "ssm_sample": (P, NS, 2, GP), "y_t": (P, KT, T)}


def kernel(x_prompt, x_sample, cache_k, cache_v, state_ssm_re, state_ssm_im, page_table,
           g_mix, w_in, lambda_q1, lambda_k1, lambda_q2, lambda_k2, g_sub,
           ssm_a_re, ssm_a_im, ssm_log_dt, ssm_b_re, ssm_b_im, ssm_c_re, ssm_c_im, ssm_d,
           w_glu, b_glu, w_out, g_ffn, peer_w_q, peer_sub_keys, peer_u, peer_v, g_final):
    import concourse.bacc as _bacc
    from concourse.bass_utils import run_bass_kernel_spmd as _run

    order = list(range(8)) + [8 + 8 * j + n for n in range(8) for j in range(3)]
    experts = peer_u[0].reshape(P, P, KT, P).transpose(0, 3, 2, 1).reshape(P, P, D)
    values = peer_v[0].reshape(NG, GRP, P, 4, 512).transpose(0, 3, 2, 1, 4).reshape(P, P, D)
    arrays = {
        "x_t": np.concatenate([x_sample[:, 0], x_prompt[0]]).T.reshape(KT, P, T).transpose(1, 0, 2),
        "gains": np.stack([_cols(g_mix[0]), _cols(g_ffn[0]), _cols(g_final)], 1),
        "units": np.concatenate([_units(w_in[0], P)[order], _units(w_glu[0], 2 * P), _units(w_out[0], P), _units(peer_w_q[0], P), experts, values]),
        "page_table": page_table.reshape(1, P),
        "cache_k": cache_k[0].reshape(-1, PAGE, H * P), "cache_v": cache_v[0].reshape(-1, PAGE, H * P),
        "lambdas": np.stack([lambda_q1[0], lambda_k1[0], lambda_q2[0], lambda_k2[0]]),
        "a_re": _states(ssm_a_re[0]), "a_im": _states(ssm_a_im[0]),
        "log_dt": _states(np.repeat(ssm_log_dt[0][:, None], NST, 1)),
        "b_re": _states(ssm_b_re[0]), "b_im": _states(ssm_b_im[0]),
        "c_re": _states(ssm_c_re[0].transpose(0, 2, 1)), "c_im": _states(ssm_c_im[0].transpose(0, 2, 1)),
        "h0_re": _states(state_ssm_re[0].transpose(1, 2, 0)).transpose(0, 2, 1),
        "h0_im": _states(state_ssm_im[0].transpose(1, 2, 0)).transpose(0, 2, 1),
        "d_t": ssm_d[0].T, "b_glu": _cols(b_glu[0]), "g_sub": g_sub[0].reshape(P, 1),
        "keys_t": peer_sub_keys[0].reshape(16, P, P).transpose(2, 0, 1),
        **_constants(),
    }
    arrays = {n: np.ascontiguousarray(a) for n, a in arrays.items()}
    nc = _bacc.Bacc("TRN2", target_bir_lowering=False, num_devices=1)
    ins = {n: nc.dram_tensor(n, a.shape, mybir.dt.from_np(a.dtype), kind="ExternalInput").ap() for n, a in arrays.items()}
    outs = {n: nc.dram_tensor(n, s, F32, kind="ExternalOutput").ap() for n, s in _OUTS.items()}
    program(nc, ins, outs)
    r = _run(nc, [arrays], core_ids=[0]).results[0]

    y = r["y_t"].transpose(2, 1, 0).reshape(T, D)
    k, v = (r[n].transpose(2, 0, 1) for n in ("k_t", "v_t"))
    hp = r["ssm_prompt"].reshape(2, NST, 2, GP).transpose(2, 3, 0, 1).reshape(2, 1, 1, G, NST)
    hs = r["ssm_sample"].reshape(2, NST, NS, 2, GP).transpose(3, 2, 4, 0, 1).reshape(2, 1, NS, G, NST)
    c = np.ascontiguousarray
    return (c(y[None, NS:]), c(y[:NS, None]), c(k[None, None, NS:]), c(v[None, None, NS:]), c(hp[0]), c(hp[1]),
            c(k[None, :NS, None]), c(v[None, :NS, None]), c(hs[0]), c(hs[1]))
```
